# Optimizing a Trainium2 kernel written in Bass

```python
import math
import jax, jax.numpy as jnp
from jax import lax
import numpy as np

D_MODEL = 1024
BATCH = 1
SEQ = 256
DEPTH = 2

HEAD_DIM = 64
N_DIFF_HEADS = 4
DIFF_V_DIM = 2 * HEAD_DIM
N_FOX_HEADS = 8
D_DIFF_QK = N_DIFF_HEADS * HEAD_DIM
D_DIFF_OUT = N_DIFF_HEADS * DIFF_V_DIM
D_FOX = N_FOX_HEADS * HEAD_DIM
D_MIX = D_DIFF_OUT + D_FOX
D_IN = 4 * D_DIFF_QK + D_DIFF_OUT + 3 * D_FOX + N_FOX_HEADS
SPLIT_POINTS = (D_DIFF_QK, 2 * D_DIFF_QK, 3 * D_DIFF_QK, 4 * D_DIFF_QK,
                4 * D_DIFF_QK + D_DIFF_OUT,
                4 * D_DIFF_QK + D_DIFF_OUT + D_FOX,
                4 * D_DIFF_QK + D_DIFF_OUT + 2 * D_FOX,
                4 * D_DIFF_QK + D_DIFF_OUT + 3 * D_FOX)
ATTN_SCALE = 1.0 / math.sqrt(HEAD_DIM)
ROPE_DIM = HEAD_DIM // 4
ROPE_THETA = 500000.0
Q_BLOCK = 128
N_MEM = 256
MEM_HEADS = 4
MEM_HEAD_DIM = D_MODEL // MEM_HEADS
MEM_SCALE = 1.0 / math.sqrt(MEM_HEAD_DIM)
D_FF = 2816
N_EXPERTS = 8
TOP_K = 2
D_EXPERT = 3584
N_DENSE = (DEPTH + 1) // 2
N_MOE = DEPTH // 2
EPS = 1e-6
SUBLN_EPS = 1e-5

kernel_name = "hybrid_diff_fox_moe_trunk"

def rmsnorm(x, g, eps=EPS):
    xf = x.astype(jnp.float32)
    y = xf * lax.rsqrt(jnp.mean(xf * xf, axis=-1, keepdims=True) + eps)
    return (y * g.astype(jnp.float32)).astype(x.dtype)

def rope_tables(positions, dtype):
    inv_freq = ROPE_THETA ** (-jnp.arange(0, ROPE_DIM, 2, dtype=jnp.float32) / ROPE_DIM)
    ang = positions.astype(jnp.float32)[..., None] * inv_freq
    return (jnp.cos(ang)[:, :, None, :].astype(dtype),
            jnp.sin(ang)[:, :, None, :].astype(dtype))

def apply_partial_rope(t, cos, sin):
    half = ROPE_DIM // 2
    t1, t2, rest = t[..., :half], t[..., half:ROPE_DIM], t[..., ROPE_DIM:]
    return jnp.concatenate([t1 * cos - t2 * sin, t2 * cos + t1 * sin, rest], axis=-1)

def hybrid_mixer(h, cos, sin, w_in, lam_q1, lam_k1, lam_q2, lam_k2, diff_subln_g, fox_bias, w_out, lam_init):
    B, S, _ = h.shape
    proj = h @ w_in
    q1, q2, k1, k2, v_d, q_f, k_f, v_f, f_logit = jnp.split(proj, SPLIT_POINTS, axis=-1)
    hd = lambda t, n: t.reshape(B, S, n, -1)
    q1 = apply_partial_rope(hd(q1, N_DIFF_HEADS), cos, sin)
    q2 = apply_partial_rope(hd(q2, N_DIFF_HEADS), cos, sin)
    k1 = apply_partial_rope(hd(k1, N_DIFF_HEADS), cos, sin)
    k2 = apply_partial_rope(hd(k2, N_DIFF_HEADS), cos, sin)
    v_d = hd(v_d, N_DIFF_HEADS)
    q_f, k_f, v_f = hd(q_f, N_FOX_HEADS), hd(k_f, N_FOX_HEADS), hd(v_f, N_FOX_HEADS)

    lam = (jnp.exp(jnp.sum(lam_q1.astype(jnp.float32) * lam_k1.astype(jnp.float32)))
           - jnp.exp(jnp.sum(lam_q2.astype(jnp.float32) * lam_k2.astype(jnp.float32)))
           + lam_init)

    log_f = jax.nn.log_sigmoid((f_logit + fox_bias).astype(jnp.float32))
    c = lax.cumsum(log_f, axis=1)
    c_k = jnp.transpose(c, (0, 2, 1))[:, :, None, :]

    nb = S // Q_BLOCK
    key_idx = jnp.arange(S)

    def to_blocks(t):
        return jnp.moveaxis(t.reshape(B, nb, Q_BLOCK, *t.shape[2:]), 1, 0)

    def from_blocks(t):
        return jnp.moveaxis(t, 0, 1).reshape(B, S, *t.shape[3:])

    def block(args):
        qb1, qb2, qbf, cb, start = args
        causal = key_idx[None, :] <= (start + jnp.arange(Q_BLOCK))[:, None]
        s1 = jnp.einsum('bqhd,bkhd->bhqk', qb1, k1).astype(jnp.float32) * ATTN_SCALE
        s2 = jnp.einsum('bqhd,bkhd->bhqk', qb2, k2).astype(jnp.float32) * ATTN_SCALE
        p1 = jax.nn.softmax(jnp.where(causal, s1, -jnp.inf), axis=-1)
        p2 = jax.nn.softmax(jnp.where(causal, s2, -jnp.inf), axis=-1)
        o_d = jnp.einsum('bhqk,bkhe->bqhe', (p1 - lam * p2).astype(v_d.dtype), v_d)
        sf = (jnp.einsum('bqhd,bkhd->bhqk', qbf, k_f).astype(jnp.float32) * ATTN_SCALE
              + jnp.transpose(cb, (0, 2, 1))[..., None] - c_k)
        pf = jax.nn.softmax(jnp.where(causal, sf, -jnp.inf), axis=-1)
        o_f = jnp.einsum('bhqk,bkhd->bqhd', pf.astype(v_f.dtype), v_f)
        return o_d, o_f

    o_d, o_f = lax.map(block, (to_blocks(q1), to_blocks(q2), to_blocks(q_f), to_blocks(c),
                               jnp.arange(nb) * Q_BLOCK))
    o_d = rmsnorm(from_blocks(o_d), diff_subln_g, SUBLN_EPS) * (1.0 - lam_init)
    o_f = from_blocks(o_f)
    mixed = jnp.concatenate([o_d.reshape(B, S, D_DIFF_OUT), o_f.reshape(B, S, D_FOX)], axis=-1)
    return mixed @ w_out

def memory_cross_attention(h, mem_n, w_q, w_kv, w_o):
    B, S, _ = h.shape
    q = (h @ w_q).reshape(B, S, MEM_HEADS, MEM_HEAD_DIM)
    k, v = jnp.split(mem_n @ w_kv, 2, axis=-1)
    k = k.reshape(B, N_MEM, MEM_HEADS, MEM_HEAD_DIM)
    v = v.reshape(B, N_MEM, MEM_HEADS, MEM_HEAD_DIM)
    s = jnp.einsum('bqhd,bmhd->bhqm', q, k).astype(jnp.float32) * MEM_SCALE
    p = jax.nn.softmax(s, axis=-1).astype(v.dtype)
    o = jnp.einsum('bhqm,bmhd->bqhd', p, v).reshape(B, S, D_MODEL)
    return o @ w_o

def dense_swiglu(h, w1, w3, w2):
    return (jax.nn.silu(h @ w1) * (h @ w3)) @ w2

def moe_swiglu(h, w_router, w1, w3, w2):
    B, S, D = h.shape
    xt = h.reshape(B * S, D)
    logits = (xt @ w_router).astype(jnp.float32)
    top_vals, top_idx = lax.top_k(logits, TOP_K)
    gates = jax.nn.softmax(top_vals, axis=-1)
    combine = jnp.sum(jax.nn.one_hot(top_idx, N_EXPERTS, dtype=jnp.float32) * gates[..., None], axis=1)
    combine = combine.astype(h.dtype)
    y = jnp.zeros_like(xt)
    for e in range(N_EXPERTS):
        y = y + combine[:, e:e + 1] * ((jax.nn.silu(xt @ w1[e]) * (xt @ w3[e])) @ w2[e])
    return y.reshape(B, S, D)

def setup_inputs(seed: int = 0) -> dict:
    key = jax.random.key(seed)
    ks = jax.random.split(key, 32)
    f32 = jnp.float32
    nrm = lambda k, shape, fan_in: jax.random.normal(k, shape, f32) * (fan_in ** -0.5)
    gain = lambda k, shape: 1.0 + 0.02 * jax.random.normal(k, shape, f32)
    x = jax.random.normal(ks[0], (BATCH, SEQ, D_MODEL), f32)
    mem = jax.random.normal(ks[1], (BATCH, N_MEM, D_MODEL), f32)
    offsets = jax.random.randint(ks[2], (BATCH, 1), 0, 4096, dtype=jnp.int32)
    positions = offsets + jnp.arange(SEQ, dtype=jnp.int32)[None, :]
    return {
        "x": x,
        "mem": mem,
        "positions": positions,
        "norm_mix_g": gain(ks[3], (DEPTH, D_MODEL)),
        "w_in": nrm(ks[4], (DEPTH, D_MODEL, D_IN), D_MODEL),
        "lam_q1": 0.1 * jax.random.normal(ks[5], (DEPTH, HEAD_DIM), f32),
        "lam_k1": 0.1 * jax.random.normal(ks[6], (DEPTH, HEAD_DIM), f32),
        "lam_q2": 0.1 * jax.random.normal(ks[7], (DEPTH, HEAD_DIM), f32),
        "lam_k2": 0.1 * jax.random.normal(ks[8], (DEPTH, HEAD_DIM), f32),
        "diff_subln_g": gain(ks[9], (DEPTH, DIFF_V_DIM)),
        "fox_bias": 3.0 + 0.1 * jax.random.normal(ks[10], (DEPTH, N_FOX_HEADS), f32),
        "w_out": nrm(ks[11], (DEPTH, D_MIX, D_MODEL), D_MIX),
        "norm_mem_g": gain(ks[12], (DEPTH, D_MODEL)),
        "mem_norm_g": gain(ks[13], (DEPTH, D_MODEL)),
        "w_mq": nrm(ks[14], (DEPTH, D_MODEL, D_MODEL), D_MODEL),
        "w_mkv": nrm(ks[15], (DEPTH, D_MODEL, 2 * D_MODEL), D_MODEL),
        "w_mo": nrm(ks[16], (DEPTH, D_MODEL, D_MODEL), D_MODEL),
        "norm_ffn_g": gain(ks[17], (DEPTH, D_MODEL)),
        "w_ff1": nrm(ks[18], (N_DENSE, D_MODEL, D_FF), D_MODEL),
        "w_ff3": nrm(ks[19], (N_DENSE, D_MODEL, D_FF), D_MODEL),
        "w_ff2": nrm(ks[20], (N_DENSE, D_FF, D_MODEL), D_FF),
        "w_router": nrm(ks[21], (N_MOE, D_MODEL, N_EXPERTS), D_MODEL),
        "w_e1": nrm(ks[22], (N_MOE, N_EXPERTS, D_MODEL, D_EXPERT), D_MODEL),
        "w_e3": nrm(ks[23], (N_MOE, N_EXPERTS, D_MODEL, D_EXPERT), D_MODEL),
        "w_e2": nrm(ks[24], (N_MOE, N_EXPERTS, D_EXPERT, D_MODEL), D_EXPERT),
        "final_norm_g": gain(ks[25], (D_MODEL,)),
    }

def reference(x, mem, positions, norm_mix_g, w_in, lam_q1, lam_k1, lam_q2, lam_k2, diff_subln_g,
              fox_bias, w_out, norm_mem_g, mem_norm_g, w_mq, w_mkv, w_mo, norm_ffn_g,
              w_ff1, w_ff3, w_ff2, w_router, w_e1, w_e3, w_e2, final_norm_g):
    cos, sin = rope_tables(positions, x.dtype)
    h = x
    for l in range(DEPTH):
        lam_init = 0.8 - 0.6 * math.exp(-0.3 * l)
        h = h + hybrid_mixer(rmsnorm(h, norm_mix_g[l]), cos, sin, w_in[l], lam_q1[l], lam_k1[l],
                             lam_q2[l], lam_k2[l], diff_subln_g[l], fox_bias[l], w_out[l], lam_init)
        h = h + memory_cross_attention(rmsnorm(h, norm_mem_g[l]), rmsnorm(mem, mem_norm_g[l]),
                                       w_mq[l], w_mkv[l], w_mo[l])
        hn = rmsnorm(h, norm_ffn_g[l])
        if l % 2 == 0:
            i = l // 2
            h = h + dense_swiglu(hn, w_ff1[i], w_ff3[i], w_ff2[i])
        else:
            i = l // 2
            h = h + moe_swiglu(hn, w_router[i], w_e1[i], w_e3[i], w_e2[i])
    return rmsnorm(h, final_norm_g)


_drawn_inputs = setup_inputs


def setup_inputs(seed=0):
    import zlib

    import numpy as np

    out = dict(_drawn_inputs(seed))
    spreads = {}
    factors = {'norm_mem_g': 4.63, 'mem_norm_g': 8.0, 'final_norm_g': 7.861, 'norm_ffn_g': 5.185}
    for name, (base, spread) in spreads.items():
        noise = np.random.default_rng([zlib.crc32(name.encode()), seed]).standard_normal(out[name].shape)
        drawn = base * np.exp(spread * noise) if base else spread * noise
        out[name] = __import__('jax').numpy.asarray(drawn.astype(out[name].dtype))
    for name, factor in factors.items():
        out[name] = (out[name] * factor).astype(out[name].dtype)
    return out
```

```python
from contextlib import ExitStack
import math

import numpy as np

import concourse.bass as bass
from concourse import mybir
from concourse.alu_op_type import AluOpType as ALU

F32 = mybir.dt.float32
F32R = mybir.dt.float32r
BF16 = mybir.dt.bfloat16
I32 = mybir.dt.int32
U32 = mybir.dt.uint32
ACT = mybir.ActivationFunctionType
AX = mybir.AxisListType

P = 128
SEQ, D = 256, 1024
TT = SEQ // P
KT = D // P
LAYERS = 2
HD = 64
N_DIFF, N_FOX = 4, 8
D_MAPS = 4 * N_DIFF * HD
C_VD = D_MAPS
C_QF = C_VD + 2 * N_DIFF * HD
C_KF = C_QF + N_FOX * HD
C_VF = C_KF + N_FOX * HD
C_FL = C_VF + N_FOX * HD
D_IN = C_FL + N_FOX
ROPE_HALF = HD // 8
MEM_HEADS, MEM_HD = 4, 256
D_FF, D_EXP, N_EXP = 2816, 3584, 8
EPS, SUB_EPS = 1e-6, 1e-5
NEG = -1e30

COLS = 512
UNIT = 2048
RAW, SPLIT = 6, 3
U_IN, U_MKV, U_OUT, U_MQ, U_MO, U_FFN = 0, 12, 20, 24, 28, 32
FF_FULL = D_FF // COLS
U_DENSE = 6 * FF_FULL + 3
L_UNITS = U_FFN + U_DENSE
EXP_CH = D_EXP // COLS
E_UNITS = 6 * EXP_CH
M0 = L_UNITS + U_FFN
ITEMS = N_DIFF + N_FOX
MAPS = 2 * N_DIFF + N_FOX
SPAN = P + SEQ

TWO_PI = 2.0 * math.pi
PI_HI = 6.28125
PI_MID = float(np.float32(round((TWO_PI - PI_HI) * 2**20) / 2**20))
PI_LO = TWO_PI - PI_HI - PI_MID
ROUND = 1.5 * 2.0**23
SIN_MAX = 3.1415925


def item_maps(i):
    return [2 * i, 2 * i + 1] if i < N_DIFF else [N_DIFF + i]


def map_item(m):
    return m // 2 if m < 2 * N_DIFF else m - N_DIFF


def map_blocks(m):
    if m < 2 * N_DIFF:
        h, which = m // 2, m % 2
        return 2 * which + h // 2, 4 + 2 * which + h // 2, HD * (h % 2)
    h = m - 2 * N_DIFF
    return 8 + h // 2, 12 + h // 2, HD * (h % 2)


def trunk(nc, t, out):
    ctx = ExitStack()
    with ctx:
        def sb(name, shape, dt=F32, stack=ctx):
            return stack.enter_context(nc.sbuf_tensor(name, shape, dt))

        def sem(name):
            return ctx.enter_context(nc.semaphore(name))

        raw = sb("raw", [P, RAW, UNIT])
        w_hi = sb("w_hi", [P, SPLIT, UNIT], F32R)
        w_lo = sb("w_lo", [P, SPLIT, UNIT], F32R)
        h = sb("h", [P, TT, D])
        hn = sb("hn", [P, TT, D])
        x_hi = sb("x_hi", [P, KT, SEQ], F32R)
        x_lo = sb("x_lo", [P, KT, SEQ], F32R)
        junk = sb("junk", [P, D], BF16)
        gain = sb("gain", [P, 65])
        ident = sb("ident", [P, P])
        tri = sb("tri", [P, SEQ])
        mask = sb("mask", [P, SPAN])
        slots = sb("slots", [P, P])
        eight = sb("eight", [P, N_EXP])
        sub_g = sb("sub_g", [P, LAYERS, P])
        fox_b = sb("fox_b", [P, LAYERS * N_FOX])
        eps_c = sb("eps_c", [P, 2])
        pos_i = sb("pos_i", [P, TT], I32)
        cs = sb("cs", [P, 2, TT, ROPE_HALF])
        small = sb("small", [P, 3, KT * 8])
        s_hi = sb("s_hi", [P, 3, KT * 8], F32R)
        s_lo = sb("s_lo", [P, 3, KT * 8], F32R)
        stat = sb("stat", [P, 8, 8])
        mem_r = sb("mem_r", [P, TT])
        lam = sb("lam", [P, 8])
        negmax = sb("negmax", [P, MAPS, TT])
        esum = sb("esum", [P, MAPS, TT])
        einv = sb("einv", [P, MAPS, TT])
        fl = sb("fl", [P, 4, TT, N_FOX])
        cq = sb("cq", [P, TT, N_FOX])
        route = sb("route", [P, TT, 12, N_EXP + 2])
        t_idx = sb("t_idx", [P, TT, 8], U32)
        n_over = sb("n_over", [P, 1], I32)
        attn = ExitStack()
        proj = sb("proj", [P, TT, D_IN - N_FOX], stack=attn)
        kv = sb("kv", [P, TT, 2 * D], stack=attn)
        qkt = sb("qkt", [P, 16, SEQ], stack=attn)
        decay = sb("decay", [P, N_FOX, SPAN], stack=attn)
        attn.close()
        ffn = ExitStack()
        gate = sb("gate", [P, TT, COLS], stack=ffn)
        g_hi = sb("g_hi", [P, 2, 4, SEQ], F32R, stack=ffn)
        g_lo = sb("g_lo", [P, 2, 4, SEQ], F32R, stack=ffn)
        xe_hi = sb("xe_hi", [P, KT, P], F32R, stack=ffn)
        xe_lo = sb("xe_lo", [P, KT, P], F32R, stack=ffn)
        ye = sb("ye", [P, D], stack=ffn)
        pick = sb("pick", [P, TT, P], stack=ffn)
        pick_t = sb("pick_t", [P, TT, P], stack=ffn)
        ffn_g = sb("ffn_g", [P, D], stack=ffn)
        fin_g = sb("fin_g", [P, D], stack=ffn)
        result = sb("result", [P, TT, D], stack=ffn)
        ffn.close()

        mixed = proj[:, :, 0:D]
        mem_q = proj[:, :, D:2 * D]
        gain_rows = hn[0:64, 0, 0:P]
        ang = hn[:, 1, 0:256].rearrange("p (s k t i) -> p s k t i", s=8, k=2, t=TT)
        inv_f = hn[:, 1, 512:512 + ROPE_HALF]
        lam_v = kv[:, 0, D:D + 4 * LAYERS * HD].rearrange("p (v n) -> p v n", v=4)
        pos_f = hn[:, 1, 544:544 + TT]

        def probs(m):
            return proj[:, (m % 4) // 2, C_QF + (m % 2) * SPAN:C_QF + (m % 2 + 1) * SPAN]

        def probs_t(i):
            return hn[:, i % 2, 0:SPAN]

        def mem_p(i):
            return decay[:, 2 * (i % 2):2 * (i % 2) + 2, 0:SEQ]

        def mem_pt(i):
            return hn[:, i % 2, 0:2 * SEQ]

        ps = ctx.enter_context(nc.psum_tensor("ps", [P, 8, COLS], F32))

        def acc(pair):
            return ps[:, 2 * pair:2 * pair + 2, :]

        raw_landed = [sem(f"raw_landed{i}") for i in range(RAW)]
        hi_split, lo_split, unit_used = sem("hi_split"), sem("lo_split"), sem("unit_used")
        x_landed, mem_landed, out_landed = sem("x_landed"), sem("mem_landed"), sem("out_landed")
        const_landed, late_landed = sem("const_landed"), sem("late_landed")
        pool_made, ready0 = sem("pool_made"), sem("ready0")
        gains_turned, gains_kept = sem("gains_turned"), sem("gains_kept")
        ang_ready, sin_ready = sem("ang_ready"), sem("sin_ready")
        dots_ready, lam_exp, small_split = sem("dots_ready"), sem("lam_exp"), sem("small_split")
        rs_est, source_ready, ffn_added = sem("rs_est"), sem("source_ready"), sem("ffn_added")
        mem_est, mem_free = sem("mem_est"), sem("mem_free")
        turned, hi_turned, lo_turned = sem("turned"), sem("hi_turned"), sem("lo_turned")
        acc_free = sem("acc_free")
        dve_step, act_step, pool_step = sem("dve_step"), sem("act_step"), sem("pool_step")
        fl_done, fl_neg, fl_ln, logf_ready = sem("fl_done"), sem("fl_neg"), sem("fl_ln"), sem("logf_ready")
        roped, qk_turned, qk_kept = sem("roped"), sem("qk_turned"), sem("qk_kept")
        cq_done, ck_done, ck_used = sem("cq_done"), sem("ck_done"), sem("ck_used")
        scored, masked, expd, weighed = sem("scored"), sem("masked"), sem("expd"), sem("weighed")
        p_turned, p_kept, pv_done, pv_taken = sem("p_turned"), sem("p_kept"), sem("pv_done"), sem("pv_taken")
        sub_est = sem("sub_est")
        mqk_turned, mqk_kept = sem("mqk_turned"), sem("mqk_kept")
        mscored, mmax, mexpd = sem("mscored"), sem("mmax"), sem("mexpd")
        mp_turned, mp_kept, mpv_done, mpv_taken = sem("mp_turned"), sem("mp_kept"), sem("mpv_done"), sem("mpv_taken")
        silu_done, gated, g_turned = sem("silu_done"), sem("gated"), sem("g_turned")
        ghi_kept, glo_kept, out_zeroed = sem("ghi_kept"), sem("glo_kept"), sem("out_zeroed")
        routed, route_exp, picked_sum, counted = sem("routed"), sem("route_exp"), sem("picked_sum"), sem("counted")
        logits_done, comb_ready, over_ready = sem("logits_done"), sem("comb_ready"), sem("over_ready")
        e_silu, e_gated, e_turned = sem("e_silu"), sem("e_gated"), sem("e_turned")
        e_hi, e_lo, e_zeroed = sem("e_hi"), sem("e_lo"), sem("e_zeroed")
        pick_made, gathered, xe_hi_kept, xe_lo_kept = sem("pick_made"), sem("gathered"), sem("xe_hi_kept"), sem("xe_lo_kept")
        ye_done, ye_kept, scattered, pick_turned, pick_kept = (
            sem("ye_done"), sem("ye_kept"), sem("scattered"), sem("pick_turned"), sem("pick_kept"))
        summed, hn_gained = sem("summed"), sem("hn_gained")

        def halves(w):
            return w.rearrange("(u k p) n -> u p k n", k=4, p=P)

        w_in = [halves(t["w_in"][l]) for l in range(LAYERS)]
        w_out = [halves(t["w_out"][l]) for l in range(LAYERS)]
        w_mq = [halves(t["w_mq"][l]) for l in range(LAYERS)]
        w_mkv = [halves(t["w_mkv"][l]) for l in range(LAYERS)]
        w_mo = [halves(t["w_mo"][l]) for l in range(LAYERS)]
        ff1, ff3 = halves(t["w_ff1"][0]), halves(t["w_ff3"][0])
        ff2 = t["w_ff2"][0].rearrange("(u k p) n -> u p k n", k=2, p=P)
        e1 = t["w_e1"].rearrange("a e (u k p) f -> (a e u) p k f", k=4, p=P)
        e3 = t["w_e3"].rearrange("a e (u k p) f -> (a e u) p k f", k=4, p=P)
        e2 = t["w_e2"].rearrange("a e (u k p) n -> (a e u) p k n", k=2, p=P)

        def slot4(buf, n, size):
            return buf[:, n % size, :].rearrange("p (k n) -> p k n", k=4)

        def slot2(buf, n, size):
            return buf[:, n % size, :].rearrange("p (k n) -> p k n", k=2)

        def slot8(buf, n, size):
            return buf[:, n % size, :].rearrange("p (k n) -> p k n", k=8)

        block = ctx.enter_context(nc.Block())

        @block.sync
        def _(sp):
            def load(n, src, view=slot4, more=0, turns=0):
                if n >= RAW:
                    sp.wait_ge(lo_split, more + (n - RAW + 1))
                sp.dma_start(view(raw, n, RAW), src).then_inc(raw_landed[n % RAW], 16)

            sp.dma_start(h[:, :, :], t["x"][0].rearrange("(t p) n -> p t n", p=P)).then_inc(x_landed, 16)
            for l in range(LAYERS):
                n0 = l * L_UNITS
                if l == 0:
                    for c in range(6):
                        for u in range(2):
                            load(n0 + 2 * c + u, w_in[l][u, :, :, c * COLS:(c + 1) * COLS])
                else:
                    with sp.Fori(0, 2) as i:
                        for c in range(3):
                            for u in range(2):
                                load(n0 + 2 * c + u, w_in[l][u, :, :, bass.ds((3 * i + c) * COLS, COLS)], more=6 * i)
                for at, w, chunks in ((U_MKV, w_mkv, 4), (U_OUT, w_out, 2), (U_MQ, w_mq, 2), (U_MO, w_mo, 2)):
                    for c in range(chunks):
                        for u in range(2):
                            load(n0 + at + 2 * c + u, w[l][u, :, :, c * COLS:(c + 1) * COLS])
                if l == 0:
                    f0 = n0 + U_FFN
                    for k in range(4):
                        load(f0 + k, (ff1, ff3)[k // 2][k % 2, :, :, 0:COLS])
                    with sp.Fori(0, FF_FULL - 1) as i:
                        for k in range(4):
                            load(f0 + 4 + k, (ff1, ff3)[k // 2][k % 2, :, :, bass.ds((i + 1) * COLS, COLS)], more=6 * i)
                        for u in range(2):
                            load(f0 + 8 + u, ff2[2 * i + u], slot2, more=6 * i)
                    f1 = f0 + 4 + 6 * (FF_FULL - 1)
                    for k, w in enumerate((t["w_ff1"][0], t["w_ff3"][0])):
                        load(f1 + k, w.rearrange("(k p) n -> p k n", p=P)[:, :, FF_FULL * COLS:D_FF], slot8)
                    for u in range(3):
                        load(f1 + 2 + u, ff2[2 * (FF_FULL - 1) + u], slot2)

            def experts(q0):
                with sp.Fori(0, N_EXP) as e:
                    q = E_UNITS * (e + q0)
                    for k in range(4):
                        load(M0 + k, (e1, e3)[k // 2][2 * e + k % 2, :, :, 0:COLS], more=q)
                    with sp.Fori(1, EXP_CH) as j:
                        for k in range(4):
                            load(M0 + 4 + k, (e1, e3)[k // 2][2 * e + k % 2, :, :, bass.ds(j * COLS, COLS)],
                                 more=q + 6 * (j - 1))
                        for u in range(2):
                            load(M0 + 8 + u, e2[2 * EXP_CH * e + 2 * (j - 1) + u], slot2, more=q + 6 * (j - 1))
                    for u in range(2):
                        load(M0 + 6 * EXP_CH - 2 + u, e2[2 * EXP_CH * e + 2 * (EXP_CH - 1) + u], slot2, more=q)

            experts(0)
            sp.wait_ge(over_ready, 1)
            over = sp.value_load(n_over[0:1, 0:1], min_val=0, max_val=SEQ)
            with sp.If(over > 0):
                experts(N_EXP)
            sp.wait_ge(out_landed, 32)

        @block.gpsimd
        def _(pool):
            gains = (t["norm_mix_g"], t["norm_mem_g"], t["mem_norm_g"], t["norm_ffn_g"])
            for i, g in enumerate(gains):
                pool.dma_start(gain_rows[16 * i:16 * i + 16, :],
                               g.rearrange("l (k p) -> (l k) p", p=P)).then_inc(const_landed, 16)
            pool.dma_start(pos_i[:, :], t["positions"].rearrange("b (t p) -> p (b t)", p=P),
                           allow_slow_non_contiguous=True).then_inc(const_landed, 16)
            for i, v in enumerate(("lam_q1", "lam_k1", "lam_q2", "lam_k2")):
                pool.dma_start(lam_v[:, i, :], t[v].rearrange("l d -> (l d)").partition_broadcast(P)).then_inc(const_landed, 16)
            pool.dma_start(sub_g[:, :, :], t["diff_subln_g"].partition_broadcast(P)).then_inc(const_landed, 16)
            pool.dma_start(fox_b[:, :], t["fox_bias"].rearrange("l n -> (l n)").partition_broadcast(P)).then_inc(const_landed, 16)
            for l in range(LAYERS):
                pool.dma_start(small[:, l, :].rearrange("p (k n) -> p k n", n=N_FOX),
                               t["w_in"][l].rearrange("(k p) n -> p k n", p=P)[:, :, C_FL:D_IN]).then_inc(const_landed, 16)
            pool.dma_start(small[:, 2, :].rearrange("p (k n) -> p k n", n=N_EXP),
                           t["w_router"][0].rearrange("(k p) n -> p k n", p=P)).then_inc(const_landed, 16)
            pool.dma_start(kv[:, :, 0:D], t["mem"][0].rearrange("(t p) n -> p t n", p=P)).then_inc(mem_landed, 16)

            pool.memset(ident[:, :], 0.0).then_inc(pool_step, 1)
            pool.memset(tri[:, :], 1.0).then_inc(pool_step, 1)
            pool.memset(mask[:, :], 0.0).then_inc(pool_step, 1)
            pool.wait_ge(pool_step, 3)
            pool.affine_select(out=ident[:, :], in_=ident[:, :], compare_op=ALU.not_equal, fill=1.0, base=0,
                               pattern=[[-1, P]], channel_multiplier=1).then_inc(pool_made, 1)
            pool.affine_select(out=tri[:, 0:P], in_=tri[:, 0:P], compare_op=ALU.is_ge, fill=0.0, base=0,
                               pattern=[[1, P]], channel_multiplier=-1).then_inc(pool_made, 1)
            for c in (0, SEQ):
                pool.affine_select(out=mask[:, c:c + P], in_=mask[:, c:c + P], compare_op=ALU.is_ge, fill=NEG, base=0,
                                   pattern=[[-1, P]], channel_multiplier=1).then_inc(pool_made, 1)
            pool.iota(slots[:, :], pattern=[[1, P]], base=1, channel_multiplier=0,
                      allow_small_or_imprecise_dtypes=True).then_inc(pool_made, 1)
            pool.iota(eight[:, :], pattern=[[1, N_EXP]], base=0, channel_multiplier=0,
                      allow_small_or_imprecise_dtypes=True).then_inc(pool_made, 1)
            pool.wait_ge(ffn_added, 1)
            pool.dma_start(kv[:, :, 0:D], t["mem"][0].rearrange("(t p) n -> p t n", p=P)).then_inc(mem_landed, 16)
            pool.wait_ge(acc_free, 32)
            pool.dma_start(ffn_g[:, :], t["norm_ffn_g"][1].partition_broadcast(P)).then_inc(late_landed, 16)
            pool.dma_start(fin_g[:, :], t["final_norm_g"].partition_broadcast(P)).then_inc(late_landed, 16)

        @block.scalar
        def _(act):
            steps = [0]

            def link(ins):
                steps[0] += 1
                ins.then_inc(act_step, 1)
                act.wait_ge(act_step, steps[0])

            def split(n, more=0, turns=0):
                act.wait_ge(raw_landed[n % RAW], 16 * turns + 16 * (n // RAW + 1))
                if n >= SPLIT:
                    act.wait_ge(unit_used, more + (n - SPLIT + 1))
                act.activation(w_hi[:, n % SPLIT, :], raw[:, n % RAW, :], ACT.Copy).then_inc(hi_split, 1)

            def splits(a, b):
                for n in range(a, b):
                    split(n)

            def turn_hi(tn, columns):
                for g in range(4):
                    act.wait_ge(turned, 4 * tn + g + 1)
                    for k in (2 * g, 2 * g + 1):
                        c = columns(k)
                        act.activation(x_hi[:, k, :], ps[:, 6 + g % 2, (k % 2) * SEQ:(k % 2 + 1) * SEQ], ACT.Copy,
                                       scale=gain[:, c:c + 1]).then_inc(hi_turned, 1)

            def norm_stats(src, at, inc):
                for tt in range(TT):
                    link(act.activation(junk[:, :], src[:, tt, 0:D], ACT.Square, accum_out=stat[:, at, tt:tt + 1]))
                link(act.activation(stat[:, at, 2:4], stat[:, at, 0:2], ACT.Ln, scale=1.0 / D, bias=eps_c[:, 0:1]))
                act.activation(stat[:, at, 4:6], stat[:, at, 2:4], ACT.Exp, scale=-0.5).then_inc(inc, 1)

            act.wait_ge(ang_ready, 1)
            act.activation(cs[:, :, :, :], ang[:, 4, :, :, :], ACT.Sin).then_inc(sin_ready, 1)
            act.wait_ge(dots_ready, 1)
            act.activation(lam[:, 4:8], lam[:, 0:4], ACT.Exp).then_inc(lam_exp, 1)
            act.wait_ge(ready0, 1)
            act.wait_ge(x_landed, 16)
            norm_stats(h, 0, rs_est)

            for l in range(LAYERS):
                n0 = l * L_UNITS
                if l:
                    act.wait_ge(ffn_added, 1)
                    norm_stats(h, 0, rs_est)
                if l == 0:
                    act.wait_ge(gains_kept, 1)
                turn_hi(6 * l, lambda k: 8 * l + k)
                if l == 0:
                    act.wait_ge(mem_landed, 16)
                    norm_stats(kv, 1, mem_est)
                if l == 0:
                    splits(n0, n0 + 3)
                with act.Fori(0, 2) as i:
                    for k in range(6):
                        split(n0 + 3 + k, 6 * i, i)
                turn_hi(6 * l + 1, lambda k: 32 + 8 * l + k)

                act.wait_ge(fl_neg, l + 1)
                link(act.activation(fl[:, 2, :, :], fl[:, 1, :, :], ACT.Exp))
                act.activation(fl[:, 3, :, :], fl[:, 2, :, :], ACT.Ln, bias=1.0).then_inc(fl_ln, 1)
                splits(n0 + 15, n0 + 16)

                def keep_qk(g):
                    act.wait_ge(qk_turned, 8 * l + g + 1)
                    queries = g in (0, 1, 4, 5)
                    act.activation(qkt[:, 2 * g:2 * g + 2, :],
                                   ps[:, 6 + g % 2, :].rearrange("p (b n) -> p b n", b=2), ACT.Copy,
                                   scale=1.0 / math.sqrt(HD) if queries else 1.0).then_inc(qk_kept, 1)

                def exps(i):
                    for m in item_maps(i):
                        act.wait_ge(masked, MAPS * l + m + 1)
                        for tt, a, b in ((0, 0, P), (1, P, SPAN)):
                            ins = act.activation(probs(m)[:, a:b], probs(m)[:, a:b], ACT.Exp,
                                                 bias=negmax[:, m, tt:tt + 1], accum_out=esum[:, m, tt:tt + 1])
                        ins.then_inc(expd, 1)

                def keep_pt(i):
                    act.wait_ge(p_turned, ITEMS * l + i + 1)
                    if i >= 2:
                        act.wait_ge(pv_done, ITEMS * l + i - 1)
                    act.activation(probs_t(i), ps[:, 6 + i % 2, 0:SPAN], ACT.Copy).then_inc(p_kept, 1)

                for g in range(4):
                    keep_qk(g)
                splits(n0 + 16, n0 + 17)
                for g in range(4, 8):
                    keep_qk(g)
                splits(n0 + 17, n0 + 18)
                nxt = n0 + 18
                for s in range(ITEMS + 1):
                    if s < ITEMS:
                        exps(s)
                    if s < 5:
                        split(nxt)
                        nxt += 1
                    if s >= 1:
                        keep_pt(s - 1)
                    if s == N_DIFF + 1:
                        act.wait_ge(pv_taken, ITEMS * l + N_DIFF)
                        for i in range(N_DIFF):
                            for tt in range(TT):
                                ins = act.activation(junk[:, (2 * i + tt) * P:(2 * i + tt + 1) * P], mixed[:, tt, i * P:(i + 1) * P], ACT.Square,
                                                     accum_out=stat[:, 2, 2 * i + tt:2 * i + tt + 1])
                        link(ins)
                        link(act.activation(stat[:, 3, :], stat[:, 2, :], ACT.Ln, scale=1.0 / P, bias=eps_c[:, 1:2]))
                        act.activation(stat[:, 4, :], stat[:, 3, :], ACT.Exp, scale=-0.5).then_inc(sub_est, 1)
                turn_hi(6 * l + 2, lambda k: 64)
                splits(n0 + 23, n0 + 27)
                act.wait_ge(acc_free, 16 * l + 12)
                norm_stats(h, 0, rs_est)
                turn_hi(6 * l + 3, lambda k: 16 + 8 * l + k)
                splits(n0 + 27, n0 + 31)

                def keep_mqk(g):
                    act.wait_ge(mqk_turned, 8 * l + g + 1)
                    act.activation(qkt[:, 2 * g:2 * g + 2, :],
                                   ps[:, 6 + g % 2, :].rearrange("p (b n) -> p b n", b=2), ACT.Copy,
                                   scale=1.0 / math.sqrt(MEM_HD) if g >= 4 else 1.0).then_inc(mqk_kept, 1)

                for g in range(8):
                    keep_mqk(g)
                for s in range(MEM_HEADS + 1):
                    if s < MEM_HEADS:
                        act.wait_ge(mmax, MEM_HEADS * l + s + 1)
                        for tt in range(TT):
                            ins = act.activation(mem_p(s)[:, tt, :], ps[:, 4 + s % 2, tt * SEQ:(tt + 1) * SEQ], ACT.Exp,
                                                 bias=negmax[:, s, tt:tt + 1], accum_out=esum[:, s, tt:tt + 1])
                        ins.then_inc(mexpd, 1)
                    if s >= 1:
                        act.wait_ge(mp_turned, MEM_HEADS * l + s)
                        if s >= 3:
                            act.wait_ge(mpv_done, MEM_HEADS * l + s - 2)
                        act.activation(mem_pt(s - 1), ps[:, 6 + (s - 1) % 2, :], ACT.Copy).then_inc(mp_kept, 1)
                turn_hi(6 * l + 4, lambda k: 64)
                splits(n0 + 31, n0 + (35 if l == 0 else 32))
                act.wait_ge(acc_free, 16 * l + 16)
                norm_stats(h, 0, rs_est)
                turn_hi(6 * l + 5, (lambda k: 48 + k) if l == 0 else (lambda k: 64))

                if l == 0:
                    f0 = n0 + U_FFN

                    def silu(pair, used, want, wide=COLS):
                        act.wait_ge(unit_used, used)
                        act.activation(gate[:, :, 0:wide], acc(pair)[:, :, 0:wide], ACT.Silu).then_inc(silu_done, 1)

                    def keep_hi(pair, buf, want, blocks=4):
                        act.wait_ge(g_turned, want)
                        act.activation(g_hi[:, buf, 0:blocks, :], acc(pair).rearrange("p c (b n) -> p (c b) n", n=SEQ)[:, 0:blocks, :],
                                       ACT.Copy).then_inc(ghi_kept, 1)

                    splits(f0 + 3, f0 + 4)
                    silu(0, f0 + 2, 1)
                    splits(f0 + 4, f0 + 6)
                    keep_hi(0, 0, 1)
                    with act.Fori(0, (FF_FULL - 1) // 2) as i:
                        for r in range(2):
                            b = f0 + 4 + 6 * r
                            for k in (2, 3):
                                split(b + k, 12 * i, 2 * i)
                            silu((r + 1) % 2, 12 * i + (b + 2), 0)
                            for k in range(4, 8):
                                split(b + k, 12 * i, 2 * i)
                            keep_hi((r + 1) % 2, (r + 1) % 2, 2 * i + (r + 2))
                    f1 = f0 + 4 + 6 * (FF_FULL - 1)
                    splits(f1 + 2, f1 + 3)
                    silu(1, f1 + 1, 0, SEQ)
                    splits(f1 + 3, f1 + 5)
                    keep_hi(1, 1, FF_FULL + 1, 2)
                    splits(L_UNITS, L_UNITS + 3)

            act.wait_ge(routed, 1)
            act.activation(route[:, :, 4, 0:1], route[:, :, 3, 0:1], ACT.Exp).then_inc(route_exp, 1)

            def keep_xe(q):
                for g in range(2):
                    act.wait_ge(gathered, q * 2 + (g + 1))
                    act.activation(xe_hi[:, 4 * g:4 * g + 4, :], ps[:, 5 + g, :].rearrange("p (k n) -> p k n", k=4),
                                   ACT.Copy).then_inc(xe_hi_kept, 1)

            def keep_ye(q):
                act.wait_ge(ye_done, q + 1)
                act.activation(ye[:, :].rearrange("p (c n) -> p c n", c=2), ps[:, 2:4, :], ACT.Copy).then_inc(ye_kept, 1)

            def experts(q0):
                keep_xe(q0 + q0 // N_EXP)
                with act.Fori(0, N_EXP) as e:
                    q = e + q0
                    more = E_UNITS * q

                    def s(k, j=0):
                        split(M0 + k, more + 6 * j, EXP_CH * q + j)

                    s(0), s(1)
                    keep_ye(q + q0 // N_EXP)
                    s(2), s(3)
                    act.wait_ge(unit_used, more + (M0 + 2))
                    act.activation(gate[:, 0, :], ps[:, 0, :], ACT.Silu).then_inc(e_silu, 1)
                    s(4), s(5)
                    act.wait_ge(pick_turned, q + 1)
                    act.activation(pick_t[:, :, :], ps[:, 3, 0:SEQ].rearrange("p (t n) -> p t n", t=TT), ACT.Copy).then_inc(pick_kept, 1)
                    act.wait_ge(e_turned, EXP_CH * q + 1)
                    act.activation(g_hi[:, 0, :, 0:P], ps[:, 4, :].rearrange("p (b n) -> p b n", b=4), ACT.Copy).then_inc(e_hi, 1)
                    with act.Fori(0, EXP_CH - 1) as j:
                        s(6, j), s(7, j)
                        act.wait_ge(unit_used, more + 6 * j + (M0 + 6))
                        act.activation(gate[:, 0, :], ps[:, 0, :], ACT.Silu).then_inc(e_silu, 1)
                        for k in range(8, 12):
                            s(k, j)
                        act.wait_ge(e_turned, EXP_CH * q + j + 2)
                        act.activation(g_hi[:, 0, :, 0:P], ps[:, 4, :].rearrange("p (b n) -> p b n", b=4), ACT.Copy).then_inc(e_hi, 1)
                    keep_xe(q + q0 // N_EXP + 1)
                keep_ye(q0 + N_EXP + q0 // N_EXP)

            experts(0)
            act.wait_ge(over_ready, 1)
            over = act.value_load(n_over[0:1, 0:1], min_val=0, max_val=SEQ)
            with act.If(over > 0):
                experts(N_EXP)
            act.wait_ge(summed, 1)
            norm_stats(h, 0, rs_est)
            for tt in range(TT):
                act.wait_ge(source_ready, 6 * LAYERS + tt + 1)
                act.dma_start(out[0, tt * P:(tt + 1) * P, :], result[:, tt, :]).then_inc(out_landed, 16)

        @block.vector
        def _(dve):
            steps = [0]

            def link(ins):
                steps[0] += 1
                ins.then_inc(dve_step, 1)
                dve.wait_ge(dve_step, steps[0])

            def split(n, more=0):
                dve.wait_ge(hi_split, more + (n + 1))
                dve.tensor_tensor(w_lo[:, n % SPLIT, :], raw[:, n % RAW, :], w_hi[:, n % SPLIT, :].bitcast(F32),
                                  ALU.subtract).then_inc(lo_split, 1)

            def splits(a, b):
                for n in range(a, b):
                    split(n)

            def turn_lo(tn, columns):
                for k in range(KT):
                    dve.wait_ge(hi_turned, KT * tn + k // 2 * 2 + 2)
                    c = columns(k)
                    dve.scalar_tensor_tensor(out=x_lo[:, k, :], in0=ps[:, 6 + k // 2 % 2, (k % 2) * SEQ:(k % 2 + 1) * SEQ],
                                             scalar=gain[:, c:c + 1], in1=x_hi[:, k, :].bitcast(F32),
                                             op0=ALU.mult, op1=ALU.subtract).then_inc(lo_turned, 1)

            def refine(y, v, y0, tmp):
                link(dve.tensor_tensor(tmp, y0, y0, ALU.mult))
                link(dve.tensor_tensor(tmp, tmp, v, ALU.mult))
                link(dve.tensor_scalar(tmp, tmp, -0.5, 1.5, ALU.mult, ALU.add))
                link(dve.tensor_tensor(y, y0, tmp, ALU.mult))

            def rstd(at):
                link(dve.tensor_scalar(stat[:, at, 2:4], stat[:, at, 0:2], 1.0 / D, EPS, ALU.mult, ALU.add))
                refine(stat[:, at, 6:8], stat[:, at, 2:4], stat[:, at, 4:6], stat[:, 5, 0:2])

            def norm(number):
                dve.wait_ge(rs_est, number + 1)
                rstd(0)
                for tt in range(TT):
                    ins = dve.tensor_scalar(hn[:, tt, :], h[:, tt, :], stat[:, 0, 6 + tt:7 + tt], None, ALU.mult)
                return ins

            for i in range(ROPE_HALF):
                f = float(np.float32(500000.0) ** np.float32(-2.0 * i / (2 * ROPE_HALF)))
                ins = dve.memset(inv_f[:, i:i + 1], f)
            dve.memset(eps_c[:, 0:1], EPS)
            dve.memset(eps_c[:, 1:2], SUB_EPS)
            dve.memset(route[:, :, :, :], 0.0)
            link(dve.memset(gain[:, 64:65], 1.0))
            dve.memset(junk[:, 0:2], 0.0).then_inc(ready0, 1)
            dve.wait_ge(const_landed, 16 * 14)
            link(dve.tensor_copy(pos_f, pos_i[:, :]))
            for tt in range(TT):
                ins = dve.tensor_scalar(ang[:, 0, 1, tt, :], inv_f, pos_f[:, tt:tt + 1], None, ALU.mult)
            link(ins)
            link(dve.tensor_copy(ang[:, 0, 0, :, :], ang[:, 0, 1, :, :]))
            dve.tensor_scalar(ang[:, 1, 0, :, :], ang[:, 0, 0, :, :], 1.0 / TWO_PI, 0.25, ALU.mult, ALU.add)
            link(dve.tensor_scalar(ang[:, 1, 1, :, :], ang[:, 0, 1, :, :], 1.0 / TWO_PI, None, ALU.mult))
            link(dve.tensor_scalar(ang[:, 2, :, :, :], ang[:, 1, :, :, :], ROUND, None, ALU.add))
            link(dve.tensor_scalar(ang[:, 3, :, :, :], ang[:, 2, :, :, :], -ROUND, None, ALU.add))
            for part in (PI_HI, PI_MID, PI_LO):
                link(dve.scalar_tensor_tensor(out=ang[:, 0, :, :, :], in0=ang[:, 3, :, :, :], scalar=-part,
                                              in1=ang[:, 0, :, :, :], op0=ALU.mult, op1=ALU.add))
            link(dve.tensor_scalar(ang[:, 0, 0, :, :], ang[:, 0, 0, :, :], math.pi / 2, None, ALU.add))
            dve.tensor_scalar(ang[:, 4, :, :, :], ang[:, 0, :, :, :], SIN_MAX, -SIN_MAX, ALU.min, ALU.max).then_inc(ang_ready, 1)
            for i in range(2):
                for l in range(LAYERS):
                    a, b = lam_v[:, 2 * i, l * HD:(l + 1) * HD], lam_v[:, 2 * i + 1, l * HD:(l + 1) * HD]
                    ins = dve.tensor_tensor_reduce(junk[:, (2 * i + l) * HD:(2 * i + l + 1) * HD],
                                                   a, b, 1.0, 0.0, ALU.mult, ALU.add, lam[:, 2 * i + l:2 * i + l + 1])
            ins.then_inc(dots_ready, 1)
            for l in range(LAYERS):
                ins = dve.tensor_scalar(sub_g[:, l, :], sub_g[:, l, :], 1.0 - lam_init(l), None, ALU.mult)
            dve.wait_ge(lam_exp, 1)
            for l in range(LAYERS):
                ins = dve.scalar_tensor_tensor(out=lam[:, l:l + 1], in0=lam[:, 4 + l:5 + l], scalar=lam_init(l),
                                               in1=lam[:, 6 + l:7 + l], op0=ALU.add, op1=ALU.subtract)
            link(ins)
            link(dve.tensor_copy(s_hi[:, :, :], small[:, :, :]))
            dve.tensor_tensor(s_lo[:, :, :], small[:, :, :], s_hi[:, :, :].bitcast(F32), ALU.subtract).then_inc(small_split, 1)
            dve.wait_ge(gains_turned, 1)
            dve.tensor_copy(gain[:, 0:64], ps[:, 0, 0:64]).then_inc(gains_kept, 1)
            dve.wait_ge(sin_ready, 1)

            for l in range(LAYERS):
                n0 = l * L_UNITS
                a0 = 16 * l
                norm(3 * l).then_inc(source_ready, 1)
                if l == 0:
                    dve.wait_ge(gains_kept, 1)
                turn_lo(6 * l, lambda k: 8 * l + k)
                if l == 0:
                    dve.wait_ge(mem_est, 1)
                    rstd(1)
                dve.wait_ge(mem_landed, 16 * (l + 1))
                dve.wait_ge(turned, 4 * (6 * l + 1))
                for tt in range(TT):
                    ins = dve.tensor_scalar(hn[:, tt, :], kv[:, tt, 0:D], stat[:, 1, 6 + tt:7 + tt], None, ALU.mult)
                ins.then_inc(source_ready, 1)
                if l == 0:
                    splits(n0, n0 + 3)
                with dve.Fori(0, 2) as i:
                    for c in range(3):
                        split(n0 + 3 + 2 * c, 6 * i)
                        split(n0 + 4 + 2 * c, 6 * i)
                        dve.wait_ge(unit_used, 6 * i + (n0 + 2 * c + 2))
                        dve.tensor_copy(proj[:, :, bass.ds((3 * i + c) * COLS, COLS)], acc(c)).then_inc(acc_free, 1)
                dve.wait_ge(fl_done, l + 1)
                for tt in range(TT):
                    ins = dve.tensor_tensor(fl[:, 0, tt, :], ps[:, 7, tt * N_FOX:(tt + 1) * N_FOX],
                                            fox_b[:, l * N_FOX:(l + 1) * N_FOX], ALU.add)
                link(ins)
                dve.scalar_tensor_tensor(out=fl[:, 1, :, :], in0=fl[:, 0, :, :], scalar=-1.0, in1=fl[:, 0, :, :],
                                         op0=ALU.mult, op1=ALU.min).then_inc(fl_neg, 1)
                turn_lo(6 * l + 1, lambda k: 32 + 8 * l + k)
                heads = proj[:, :, 0:D_MAPS].rearrange("p t (h d) -> p t h d", d=HD)
                dve.wait_ge(ck_used, 8 * l) if l else None
                rot = decay[:, :, :].rearrange("p a b -> p (a b)")[:, 0:1024].rearrange(
                    "p (s t h i) -> p s t h i", s=4, t=TT, h=16)
                for tt in range(TT):
                    t1, t2 = heads[:, tt, :, 0:ROPE_HALF], heads[:, tt, :, ROPE_HALF:2 * ROPE_HALF]
                    cos = cs[:, 0, tt, :].unsqueeze(1).to_broadcast([P, 16, ROPE_HALF])
                    sin = cs[:, 1, tt, :].unsqueeze(1).to_broadcast([P, 16, ROPE_HALF])
                    for s, (x, f) in enumerate(((t1, cos), (t2, sin), (t2, cos), (t1, sin))):
                        ins = dve.tensor_tensor(rot[:, s, tt], x, f, ALU.mult)
                link(ins)
                for tt in range(TT):
                    dve.tensor_tensor(heads[:, tt, :, 0:ROPE_HALF], rot[:, 0, tt], rot[:, 1, tt], ALU.subtract)
                    ins = dve.tensor_tensor(heads[:, tt, :, ROPE_HALF:2 * ROPE_HALF], rot[:, 2, tt], rot[:, 3, tt], ALU.add)
                ins.then_inc(roped, 1)
                dve.wait_ge(fl_ln, l + 1)
                dve.scalar_tensor_tensor(out=fl[:, 1, :, :], in0=fl[:, 0, :, :], scalar=0.0, in1=fl[:, 3, :, :],
                                         op0=ALU.min, op1=ALU.subtract).then_inc(logf_ready, 1)

                def evict(c, dst):
                    dve.wait_ge(unit_used, n0 + 2 * c + 2)
                    dve.tensor_copy(dst, acc(0)).then_inc(acc_free, 1)

                splits(n0 + 15, n0 + 16)
                evict(6, kv[:, :, 0:COLS])
                splits(n0 + 16, n0 + 17)

                def mask_map(m):
                    dve.wait_ge(scored, MAPS * l + m + 1)
                    if m >= 4:
                        dve.wait_ge(p_turned, ITEMS * l + map_item(m - 4) + 1)
                    elif l:
                        dve.wait_ge(p_turned, ITEMS * l)
                    for tt, a, b in ((0, 0, P), (1, P, SPAN)):
                        add = mask[:, a:b] if m < 2 * N_DIFF else decay[:, m - 2 * N_DIFF, a:b]
                        ins = dve.tensor_tensor_reduce(probs(m)[:, a:b], ps[:, 4 + m % 2, a:b], add, 1.0, 3 * NEG,
                                                       ALU.add, ALU.max, negmax[:, m, tt:tt + 1])
                    link(ins)
                    dve.tensor_scalar(negmax[:, m, :], negmax[:, m, :], -1.0, None, ALU.mult).then_inc(masked, 1)

                def weigh(i):
                    for m in item_maps(i):
                        dve.wait_ge(expd, MAPS * l + m + 1)
                        ins = dve.reciprocal(einv[:, m, :], esum[:, m, :])
                    link(ins)
                    if i < N_DIFF:
                        a, b = item_maps(i)
                        link(dve.tensor_scalar(einv[:, b, :], einv[:, b, :], lam[:, l:l + 1], None, ALU.mult))
                        for tt, x, y in ((0, 0, P), (1, P, SPAN)):
                            ins = dve.tensor_scalar(probs(b)[:, x:y], probs(b)[:, x:y], einv[:, b, tt:tt + 1], None, ALU.mult)
                        link(ins)
                        for tt, x, y in ((0, 0, P), (1, P, SPAN)):
                            ins = dve.scalar_tensor_tensor(out=probs(a)[:, x:y], in0=probs(a)[:, x:y],
                                                           scalar=einv[:, a, tt:tt + 1], in1=probs(b)[:, x:y],
                                                           op0=ALU.mult, op1=ALU.subtract)
                        ins.then_inc(weighed, 1)

                def take_pv(i):
                    dve.wait_ge(pv_done, ITEMS * l + i + 1)
                    if i < N_DIFF:
                        dve.tensor_copy(mixed[:, :, i * P:(i + 1) * P],
                                        ps[:, 2 + i % 2, 0:2 * P].rearrange("p (t n) -> p t n", t=TT)).then_inc(pv_taken, 1)
                        return
                    f, m = i - N_DIFF, item_maps(i)[0]
                    for tt in range(TT):
                        ins = dve.tensor_scalar(mixed[:, tt, 2 * N_DIFF * HD + f * HD:2 * N_DIFF * HD + (f + 1) * HD],
                                                ps[:, 2 + i % 2, tt * HD:(tt + 1) * HD], einv[:, m, tt:tt + 1], None, ALU.mult)
                    ins.then_inc(pv_taken, 1)

                dve.wait_ge(cq_done, l + 1)
                link(dve.tensor_copy(cq[:, :, :], ps[:, 4, 0:TT * N_FOX].rearrange("p (t n) -> p t n", t=TT)))
                for f in range(N_FOX):
                    dve.wait_ge(ck_done, N_FOX * l + f + 1)
                    c = ps[:, 2 + f % 2, 0:SEQ]
                    dve.scalar_tensor_tensor(out=decay[:, f, 0:P], in0=mask[:, 0:P], scalar=cq[:, 0, f:f + 1],
                                             in1=c[:, 0:P], op0=ALU.add, op1=ALU.subtract)
                    dve.scalar_tensor_tensor(out=decay[:, f, P:SPAN], in0=mask[:, P:SPAN], scalar=cq[:, 1, f:f + 1],
                                             in1=c, op0=ALU.add, op1=ALU.subtract).then_inc(ck_used, 1)
                splits(n0 + 17, n0 + 18)
                evict(7, kv[:, :, COLS:2 * COLS])
                nxt = n0 + 18
                for s in range(ITEMS + 2):
                    if s < ITEMS:
                        for m in item_maps(s):
                            mask_map(m)
                    if s < 5:
                        split(nxt)
                        nxt += 1
                    if s >= 1 and s - 1 < ITEMS:
                        weigh(s - 1)
                    if s == 2:
                        evict(8, kv[:, :, 2 * COLS:3 * COLS])
                    if s == 4:
                        evict(9, kv[:, :, 3 * COLS:4 * COLS])
                    if s >= 2:
                        take_pv(s - 2)
                dve.wait_ge(sub_est, l + 1)
                link(dve.tensor_scalar(stat[:, 3, :], stat[:, 2, :], 1.0 / P, SUB_EPS, ALU.mult, ALU.add))
                refine(stat[:, 6, :], stat[:, 3, :], stat[:, 4, :], stat[:, 5, :])
                for i in range(N_DIFF):
                    for tt in range(TT):
                        o = mixed[:, tt, i * P:(i + 1) * P]
                        ins = dve.scalar_tensor_tensor(out=o, in0=o, scalar=stat[:, 6, 2 * i + tt:2 * i + tt + 1],
                                                       in1=sub_g[:, l, :], op0=ALU.mult, op1=ALU.mult)
                ins.then_inc(source_ready, 1)
                turn_lo(6 * l + 2, lambda k: 64)

                def add_chunk(c, unit):
                    dve.wait_ge(unit_used, unit + 1)
                    r = h[:, :, c * COLS:(c + 1) * COLS]
                    dve.tensor_tensor(r, r, acc(c % 2), ALU.add).then_inc(acc_free, 1)

                splits(n0 + 23, n0 + 24)
                add_chunk(0, n0 + U_OUT + 1)
                splits(n0 + 24, n0 + 26)
                add_chunk(1, n0 + U_OUT + 3)
                splits(n0 + 26, n0 + 27)
                norm(3 * l + 1).then_inc(source_ready, 1)
                turn_lo(6 * l + 3, lambda k: 16 + 8 * l + k)
                splits(n0 + 27, n0 + 28)
                for c in range(2):
                    dve.wait_ge(unit_used, n0 + U_MQ + 2 * c + 2)
                    dve.tensor_copy(mem_q[:, :, c * COLS:(c + 1) * COLS], acc(c)).then_inc(acc_free, 1)
                    splits(n0 + 28 + 2 * c, n0 + 30 + 2 * c) if c == 0 else splits(n0 + 30, n0 + 31)
                for s in range(MEM_HEADS + 2):
                    if s < MEM_HEADS:
                        dve.wait_ge(mscored, MEM_HEADS * l + s + 1)
                        link(dve.tensor_reduce(negmax[:, s, :], ps[:, 4 + s % 2, :].rearrange("p (t n) -> p t n", t=TT),
                                               AX.X, ALU.max))
                        dve.tensor_scalar(negmax[:, s, :], negmax[:, s, :], -1.0, None, ALU.mult).then_inc(mmax, 1)
                    if s >= 2:
                        i = s - 2
                        link(dve.reciprocal(einv[:, i, :], esum[:, i, :]))
                        dve.wait_ge(mpv_done, MEM_HEADS * l + i + 1)
                        for tt in range(TT):
                            ins = dve.tensor_scalar(mixed[:, tt, i * MEM_HD:(i + 1) * MEM_HD],
                                                    ps[:, 2 + i % 2, tt * SEQ:(tt + 1) * SEQ], einv[:, i, tt:tt + 1],
                                                    None, ALU.mult)
                        ins.then_inc(source_ready if i == MEM_HEADS - 1 else mpv_taken, 1)
                turn_lo(6 * l + 4, lambda k: 64)
                splits(n0 + 31, n0 + 32)
                add_chunk(0, n0 + U_MO + 1)
                if l == 0:
                    splits(n0 + 32, n0 + 34)
                add_chunk(1, n0 + U_MO + 3)
                if l == 0:
                    splits(n0 + 34, n0 + 35)
                    norm(3 * l + 2).then_inc(source_ready, 1)
                    turn_lo(6 * l + 5, lambda k: 48 + k)
                    f0 = n0 + U_FFN

                    def gated_chunk(pair, used, want, wide=COLS):
                        dve.wait_ge(silu_done, want)
                        dve.wait_ge(unit_used, used)
                        dve.tensor_tensor(gate[:, :, 0:wide], acc(pair)[:, :, 0:wide], gate[:, :, 0:wide],
                                          ALU.mult).then_inc(gated, 1)

                    def keep_lo(pair, buf, want, blocks=4):
                        dve.wait_ge(ghi_kept, want)
                        dve.tensor_tensor(g_lo[:, buf, 0:blocks, :],
                                          acc(pair).rearrange("p c (b n) -> p (c b) n", n=SEQ)[:, 0:blocks, :],
                                          g_hi[:, buf, 0:blocks, :].bitcast(F32), ALU.subtract).then_inc(glo_kept, 1)

                    dve.wait_ge(lo_turned, KT * (6 * l + 6))
                    dve.memset(ps[:, 4:8, :], 0.0).then_inc(out_zeroed, 1)
                    splits(f0 + 3, f0 + 6)
                    gated_chunk(1, f0 + 4, 1)
                    keep_lo(0, 0, 1)
                    with dve.Fori(0, (FF_FULL - 1) // 2) as i:
                        for r in range(2):
                            b = f0 + 4 + 6 * r
                            for k in range(2, 6):
                                split(b + k, 12 * i)
                            gated_chunk(r % 2, 12 * i + (b + 4), 2 * i + (r + 2))
                            for k in range(6, 8):
                                split(b + k, 12 * i)
                            keep_lo((r + 1) % 2, (r + 1) % 2, 2 * i + (r + 2))
                    f1 = f0 + 4 + 6 * (FF_FULL - 1)
                    splits(f1 + 2, f1 + 4)
                    gated_chunk(0, f1 + 2, FF_FULL + 1, SEQ)
                    splits(f1 + 4, f1 + 5)
                    keep_lo(1, 1, FF_FULL + 1, 2)
                    dve.wait_ge(unit_used, L_UNITS)
                    for tt in range(TT):
                        r = h[:, tt, :].rearrange("p (c n) -> p c n", c=2)
                        ins = dve.tensor_tensor(r, r, ps[:, 4 + 2 * tt:6 + 2 * tt, :], ALU.add)
                    ins.then_inc(ffn_added, 1)
                    splits(L_UNITS, L_UNITS + 3)

            dve.wait_ge(rs_est, 6)
            rstd(0)
            dve.wait_ge(late_landed, 32)
            for tt in range(TT):
                ins = dve.scalar_tensor_tensor(out=hn[:, tt, :], in0=h[:, tt, :], scalar=stat[:, 0, 6 + tt:7 + tt],
                                               in1=ffn_g[:, :], op0=ALU.mult, op1=ALU.mult)
            ins.then_inc(source_ready, 1)
            turn_lo(11, lambda k: 64)
            dve.wait_ge(logits_done, 1)
            lg, top, place, gap, ex = (route[:, :, i, :] for i in range(5))
            sel1, sel2, comb, posm, picks = (route[:, :, i, :] for i in range(5, 10))
            link(dve.tensor_copy(lg[:, :, 0:8], ps[:, 3, 0:TT * N_EXP].rearrange("p (t n) -> p t n", t=TT)))
            for tt in range(TT):
                ins = dve.max(top[:, tt, 0:8], lg[:, tt, 0:8])
            link(ins)
            for tt in range(TT):
                ins = dve.max_index(t_idx[:, tt, :], top[:, tt, 0:8], lg[:, tt, 0:8])
            link(ins)
            dve.tensor_tensor(gap[:, :, 0:1], top[:, :, 1:2], top[:, :, 0:1], ALU.subtract).then_inc(routed, 1)
            link(dve.tensor_copy(place[:, :, 0:8], t_idx[:, :, :]))
            for tt in range(TT):
                dve.tensor_scalar(sel1[:, tt, 0:8], eight[:, :], place[:, tt, 0:1], None, ALU.is_equal)
                ins = dve.tensor_scalar(sel2[:, tt, 0:8], eight[:, :], place[:, tt, 1:2], None, ALU.is_equal)
            link(ins)
            dve.tensor_tensor(picks[:, :, 0:8], sel1[:, :, 0:8], sel2[:, :, 0:8], ALU.add).then_inc(picked_sum, 1)
            dve.wait_ge(route_exp, 1)
            link(dve.tensor_scalar(gap[:, :, 1:2], ex[:, :, 0:1], 1.0, None, ALU.add))
            link(dve.reciprocal(gap[:, :, 2:3], gap[:, :, 1:2]))
            link(dve.tensor_tensor(gap[:, :, 3:4], gap[:, :, 2:3], ex[:, :, 0:1], ALU.mult))
            for tt in range(TT):
                ins = dve.tensor_scalar(sel2[:, tt, 0:8], sel2[:, tt, 0:8], gap[:, tt, 3:4], None, ALU.mult)
            link(ins)
            for tt in range(TT):
                ins = dve.scalar_tensor_tensor(out=comb[:, tt, 1:9], in0=sel1[:, tt, 0:8], scalar=gap[:, tt, 2:3],
                                               in1=sel2[:, tt, 0:8], op0=ALU.mult, op1=ALU.add)
            link(ins)
            dve.wait_ge(counted, 1)
            link(dve.tensor_tensor(posm[:, :, 0:8], ps[:, 2, 0:TT * N_EXP].rearrange("p (t n) -> p t n", t=TT),
                                   picks[:, :, 0:8], ALU.mult))
            link(dve.tensor_reduce(gap[:, 0, 4:5], ps[:, 2, TT * N_EXP:(TT + 1) * N_EXP], AX.X, ALU.max))
            link(dve.tensor_scalar(gap[:, 0, 5:6], gap[:, 0, 4:5], -float(P), 0.0, ALU.add, ALU.max))
            dve.tensor_copy(n_over[:, :], gap[:, 0, 5:6]).then_inc(over_ready, 1)
            dve.memset(pick_t[:, :, :], 0.0).then_inc(comb_ready, 1)
            dve.memset(ps[:, 2:4, :], 0.0).then_inc(comb_ready, 1)

            def make_pick(e, q):
                for tt in range(TT):
                    ins = dve.tensor_scalar(pick[:, tt, :], slots[:, :], posm[:, tt, bass.ds(e, 1)], None, ALU.is_equal)
                ins.then_inc(pick_made, 1)

            def keep_xe(q):
                for g in range(2):
                    dve.wait_ge(xe_hi_kept, q * 2 + (g + 1))
                    dve.tensor_tensor(xe_lo[:, 4 * g:4 * g + 4, :], ps[:, 5 + g, :].rearrange("p (k n) -> p k n", k=4),
                                      xe_hi[:, 4 * g:4 * g + 4, :].bitcast(F32), ALU.subtract).then_inc(xe_lo_kept, 1)

            def accumulate(q, column):
                dve.wait_ge(scattered, q + 1)
                for n, bank in enumerate((5, 6, 7, 2)):
                    tt, c = n // 2, n % 2
                    r = h[:, tt, c * COLS:(c + 1) * COLS]
                    ins = dve.scalar_tensor_tensor(out=r, in0=ps[:, bank, :], scalar=comb[:, tt, bass.ds(column, 1)],
                                                   in1=r, op0=ALU.mult, op1=ALU.add)
                return ins

            def experts(q0):
                b0 = q0 // N_EXP
                make_pick(0, 0)
                keep_xe(q0 + b0)
                with dve.Fori(0, N_EXP) as e:
                    q = e + q0
                    more = E_UNITS * q
                    for k in range(6):
                        split(M0 + k, more)
                    dve.wait_ge(e_silu, EXP_CH * q + 1)
                    dve.wait_ge(unit_used, more + (M0 + 4))
                    dve.tensor_tensor(gate[:, 0, :], ps[:, 1, :], gate[:, 0, :], ALU.mult).then_inc(e_gated, 1)
                    accumulate(q + b0, e).then_inc(hn_gained, 1)
                    dve.wait_ge(pick_turned, q + 1)
                    make_pick(e + 1, q + 1)
                    dve.wait_ge(pick_kept, q + 1)
                    dve.wait_ge(hn_gained, q + b0 + 1)
                    dve.memset(ps[:, 2:4, :], 0.0).then_inc(e_zeroed, 1)
                    dve.wait_ge(e_hi, EXP_CH * q + 1)
                    dve.tensor_tensor(g_lo[:, 0, :, 0:P], ps[:, 4, :].rearrange("p (b n) -> p b n", b=4),
                                      g_hi[:, 0, :, 0:P].bitcast(F32), ALU.subtract).then_inc(e_lo, 1)
                    with dve.Fori(0, EXP_CH - 1) as j:
                        for k in range(6, 10):
                            split(M0 + k, more + 6 * j)
                        dve.wait_ge(e_silu, EXP_CH * q + j + 2)
                        dve.wait_ge(unit_used, more + 6 * j + (M0 + 8))
                        dve.tensor_tensor(gate[:, 0, :], ps[:, 1, :], gate[:, 0, :], ALU.mult).then_inc(e_gated, 1)
                        for k in range(10, 12):
                            split(M0 + k, more + 6 * j)
                        dve.wait_ge(e_hi, EXP_CH * q + j + 2)
                        dve.tensor_tensor(g_lo[:, 0, :, 0:P], ps[:, 4, :].rearrange("p (b n) -> p b n", b=4),
                                          g_hi[:, 0, :, 0:P].bitcast(F32), ALU.subtract).then_inc(e_lo, 1)
                    keep_xe(q + b0 + 1)
                return b0

            experts(0)
            link(accumulate(N_EXP, N_EXP))
            over = dve.value_load(n_over[0:1, 0:1], min_val=0, max_val=SEQ)
            with dve.If(over > 0):
                base = steps[0]
                link(dve.tensor_scalar(posm[:, :, 0:8], posm[:, :, 0:8], -float(P), None, ALU.add))
                dve.memset(pick_t[:, :, :], 0.0).then_inc(comb_ready, 1)
                dve.memset(ps[:, 2:4, :], 0.0).then_inc(comb_ready, 1)
                experts(N_EXP)
                link(accumulate(2 * N_EXP + 1, N_EXP))
                steps[0] = base
            dve.sem_inc(summed, 1)

            dve.wait_ge(rs_est, 7)
            final = [0]

            def flink(ins):
                final[0] += 1
                ins.then_inc(ready0, 1)
                dve.wait_ge(ready0, 1 + final[0])

            flink(dve.tensor_scalar(stat[:, 0, 2:4], stat[:, 0, 0:2], 1.0 / D, EPS, ALU.mult, ALU.add))
            flink(dve.tensor_tensor(stat[:, 5, 0:2], stat[:, 0, 4:6], stat[:, 0, 4:6], ALU.mult))
            flink(dve.tensor_tensor(stat[:, 5, 0:2], stat[:, 5, 0:2], stat[:, 0, 2:4], ALU.mult))
            flink(dve.tensor_scalar(stat[:, 5, 0:2], stat[:, 5, 0:2], -0.5, 1.5, ALU.mult, ALU.add))
            flink(dve.tensor_tensor(stat[:, 0, 6:8], stat[:, 0, 4:6], stat[:, 5, 0:2], ALU.mult))
            for tt in range(TT):
                dve.scalar_tensor_tensor(out=result[:, tt, :], in0=h[:, tt, :], scalar=stat[:, 0, 6 + tt:7 + tt],
                                         in1=fin_g[:, :], op0=ALU.mult, op1=ALU.mult).then_inc(source_ready, 1)

        @block.tensor
        def _(pe):
            def mm3(o, xh, xl, wh, wl, first, last, **kw):
                pe.matmul(o, xh, wh, start=first, stop=False, **kw)
                pe.matmul(o, xh, wl, start=False, stop=False, **kw)
                return pe.matmul(o, xl, wh, start=False, stop=last, **kw)

            def turn(tn):
                src = mixed if tn % 6 in (2, 4) else hn
                pe.wait_ge(source_ready, tn + 1)
                for g in range(4):
                    if g >= 2:
                        pe.wait_ge(lo_turned, KT * tn + 2 * (g - 2) + 2)
                    for k in (2 * g, 2 * g + 1):
                        for tt in range(TT):
                            c = (k % 2) * SEQ + tt * P
                            ins = pe.transpose(ps[:, 6 + g % 2, c:c + P], src[:, tt, k * P:(k + 1) * P], ident[:, :])
                    ins.then_inc(turned, 1)

            def unit(n, half, pair, tn=None, more=0):
                pe.wait_ge(lo_split, more + (n + 1))
                wh, wl = slot4(w_hi, n, SPLIT), slot4(w_lo, n, SPLIT)
                for k in range(4):
                    kt = 4 * half + k
                    if tn is not None:
                        pe.wait_ge(lo_turned, KT * tn + kt + 1)
                    for tt in range(TT):
                        ins = mm3(acc(pair)[:, tt, :], x_hi[:, kt, tt * P:(tt + 1) * P], x_lo[:, kt, tt * P:(tt + 1) * P],
                                  wh[:, k, :], wl[:, k, :], kt == 0, kt == KT - 1)
                ins.then_inc(unit_used, 1)

            def narrow(which, bank):
                wh = s_hi[:, which, :].rearrange("p (k n) -> p k n", n=8)
                wl = s_lo[:, which, :].rearrange("p (k n) -> p k n", n=8)
                for tt in range(TT):
                    for kt in range(KT):
                        ins = mm3(ps[:, bank, tt * 8:(tt + 1) * 8], x_hi[:, kt, tt * P:(tt + 1) * P],
                                  x_lo[:, kt, tt * P:(tt + 1) * P], wh[:, kt, :], wl[:, kt, :], kt == 0, kt == KT - 1)
                return ins

            def sums(bank, x):
                pe.matmul(ps[:, bank, 0:8], tri[:, 0:P], x[:, 0], start=True, stop=True)
                pe.matmul(ps[:, bank, 8:16], tri[:, P:SEQ], x[:, 0], start=True, stop=False)
                return pe.matmul(ps[:, bank, 8:16], tri[:, 0:P], x[:, 1], start=False, stop=True)

            pe.wait_ge(pool_made, 6)
            pe.wait_ge(const_landed, 16 * 14)
            pe.transpose(ps[:, 0, 0:64], gain_rows, ident[0:64, 0:64]).then_inc(gains_turned, 1)

            for l in range(LAYERS):
                n0 = l * L_UNITS
                a0 = 16 * l
                turn(6 * l)
                if l == 0:
                    pe.wait_ge(gains_kept, 1)
                pe.wait_ge(lo_turned, KT * (6 * l + 1))
                with pe.Fori(0, 2) as i:
                    for c in range(3):
                        if l or c is not None:
                            pe.wait_ge(acc_free, 3 * i + (a0 + c - 2)) if a0 + c - 2 > 0 else None
                        for u in range(2):
                            unit(n0 + 2 * c + u, u, c, more=6 * i)
                if l == 0:
                    pe.wait_ge(small_split, 1)
                narrow(l, 7).then_inc(fl_done, 1)
                pe.wait_ge(fl_neg, l + 1)
                turn(6 * l + 1)
                pe.wait_ge(acc_free, a0 + 4)
                unit(n0 + 12, 0, 0, tn=6 * l + 1)
                unit(n0 + 13, 1, 0, tn=6 * l + 1)

                def turn_qk(g):
                    if g >= 2:
                        pe.wait_ge(qk_kept, 8 * l + g - 1)
                    for b in range(2):
                        blk = 2 * g + b if g < 4 else C_QF // P + 2 * (g - 4) + b
                        for tt in range(TT):
                            ins = pe.transpose(ps[:, 6 + g % 2, b * SEQ + tt * P:b * SEQ + (tt + 1) * P],
                                               proj[:, tt, blk * P:(blk + 1) * P], ident[:, :])
                    ins.then_inc(qk_turned, 1)

                pe.wait_ge(roped, l + 1)
                for g in range(4):
                    turn_qk(g)
                pe.wait_ge(acc_free, a0 + 7)
                unit(n0 + 14, 0, 0)
                for g in range(4, 8):
                    turn_qk(g)
                pe.wait_ge(logf_ready, l + 1)
                pe.wait_ge(acc_free, a0 + 6)
                sums(4, fl[:, 1]).then_inc(cq_done, 1)
                for f in range(N_FOX):
                    if f >= 2:
                        pe.wait_ge(ck_used, N_FOX * l + f - 1)
                    o = ps[:, 2 + f % 2, 0:SEQ]
                    f0, f1 = (fl[:, 1, tt, f:f + 1].to_broadcast([P, P]) for tt in range(TT))
                    pe.matmul(o, f0, tri[:, :], start=True, stop=False)
                    pe.matmul(o[:, P:SEQ], f1, tri[:, 0:P], start=False, stop=True).then_inc(ck_done, 1)
                unit(n0 + 15, 1, 0)

                def scores(i):
                    for m in item_maps(i):
                        if m >= 2:
                            pe.wait_ge(masked, MAPS * l + m - 1)
                        elif m == 0:
                            pe.wait_ge(ck_used, N_FOX * (l + 1))
                        bq, bk, p0 = map_blocks(m)
                        q, k = qkt[p0:p0 + HD, bq, :], qkt[p0:p0 + HD, bk, :]
                        pe.matmul(ps[:, 4 + m % 2, 0:P], q[:, 0:P], k[:, 0:P], start=True, stop=True)
                        pe.matmul(ps[:, 4 + m % 2, P:SPAN], q[:, P:SEQ], k, start=True, stop=True).then_inc(scored, 1)

                def turn_p(i):
                    if i < N_DIFF:
                        pe.wait_ge(weighed, N_DIFF * l + i + 1)
                    else:
                        pe.wait_ge(expd, MAPS * l + item_maps(i)[0] + 1)
                    if i >= 2:
                        pe.wait_ge(p_kept, ITEMS * l + i - 1)
                    for b in range(3):
                        ins = pe.transpose(ps[:, 6 + i % 2, b * P:(b + 1) * P],
                                           probs(item_maps(i)[0])[:, b * P:(b + 1) * P], ident[:, :])
                    ins.then_inc(p_turned, 1)

                def pv(i):
                    pe.wait_ge(p_kept, ITEMS * l + i + 1)
                    if i >= 2:
                        pe.wait_ge(pv_taken, ITEMS * l + i - 1)
                    wide = P if i < N_DIFF else HD
                    c = C_VD + i * P if i < N_DIFF else C_VF + (i - N_DIFF) * HD
                    o, p = ps[:, 2 + i % 2, :], probs_t(i)
                    pe.matmul(o[:, 0:wide], p[:, 0:P], proj[:, 0, c:c + wide], start=True, stop=True)
                    pe.matmul(o[:, wide:2 * wide], p[:, P:2 * P], proj[:, 0, c:c + wide], start=True, stop=False)
                    pe.matmul(o[:, wide:2 * wide], p[:, 2 * P:SPAN], proj[:, 1, c:c + wide], start=False,
                              stop=True).then_inc(pv_done, 1)

                pe.wait_ge(qk_kept, 8 * (l + 1))
                nxt = n0 + 16
                for s in range(ITEMS + 2):
                    if s < ITEMS:
                        scores(s)
                    if s < 4:
                        if nxt % 2 == n0 % 2:
                            pe.wait_ge(acc_free, a0 + (nxt - n0) // 2)
                        unit(nxt, (nxt - n0) % 2, 0)
                        nxt += 1
                    if 1 <= s <= ITEMS:
                        turn_p(s - 1)
                    if s >= 2:
                        pv(s - 2)

                turn(6 * l + 2)
                pe.wait_ge(acc_free, a0 + 10)
                for c in range(2):
                    for u in range(2):
                        unit(n0 + U_OUT + 2 * c + u, u, c, tn=6 * l + 2 if c == 0 else None)
                turn(6 * l + 3)
                pe.wait_ge(acc_free, a0 + 12)
                for c in range(2):
                    for u in range(2):
                        unit(n0 + U_MQ + 2 * c + u, u, c, tn=6 * l + 3 if c == 0 else None)

                for g in range(8):
                    if g >= 2:
                        pe.wait_ge(mqk_kept, 8 * l + g - 1)
                    if g == 4:
                        pe.wait_ge(acc_free, a0 + 14)
                    src = kv if g < 4 else mem_q
                    for b in range(2):
                        blk = 2 * (g % 4) + b
                        for tt in range(TT):
                            ins = pe.transpose(ps[:, 6 + g % 2, b * SEQ + tt * P:b * SEQ + (tt + 1) * P],
                                               src[:, tt, blk * P:(blk + 1) * P], ident[:, :])
                    ins.then_inc(mqk_turned, 1)
                pe.wait_ge(mqk_kept, 8 * (l + 1))
                for s in range(MEM_HEADS + 2):
                    if s < MEM_HEADS:
                        if s >= 2:
                            pe.wait_ge(mexpd, MEM_HEADS * l + s - 1)
                        for tt in range(TT):
                            for b in range(2):
                                ins = pe.matmul(ps[:, 4 + s % 2, tt * SEQ:(tt + 1) * SEQ],
                                                qkt[:, 8 + 2 * s + b, tt * P:(tt + 1) * P], qkt[:, 2 * s + b, :],
                                                start=b == 0, stop=b == 1)
                        ins.then_inc(mscored, 1)
                    if 1 <= s <= MEM_HEADS:
                        i = s - 1
                        pe.wait_ge(mexpd, MEM_HEADS * l + i + 1)
                        if i >= 2:
                            pe.wait_ge(mp_kept, MEM_HEADS * l + i - 1)
                        for tt in range(TT):
                            for b in range(2):
                                c = (2 * tt + b) * P
                                ins = pe.transpose(ps[:, 6 + i % 2, c:c + P], mem_p(i)[:, tt, b * P:(b + 1) * P], ident[:, :])
                        ins.then_inc(mp_turned, 1)
                    if s >= 2:
                        i = s - 2
                        pe.wait_ge(mp_kept, MEM_HEADS * l + i + 1)
                        if i >= 2:
                            pe.wait_ge(mpv_taken, (MEM_HEADS - 1) * l + i - 1)
                        for tt in range(TT):
                            for b in range(2):
                                c = (2 * tt + b) * P
                                ins = pe.matmul(ps[:, 2 + i % 2, tt * SEQ:(tt + 1) * SEQ], mem_pt(i)[:, c:c + P],
                                                kv[:, b, D + i * MEM_HD:D + (i + 1) * MEM_HD], start=b == 0, stop=b == 1)
                        ins.then_inc(mpv_done, 1)
                turn(6 * l + 4)
                for c in range(2):
                    for u in range(2):
                        unit(n0 + U_MO + 2 * c + u, u, c, tn=6 * l + 4 if c == 0 else None)
                turn(6 * l + 5)
                if l == 0:
                    f0 = n0 + U_FFN
                    pe.wait_ge(acc_free, a0 + 16)
                    pe.wait_ge(lo_turned, KT * (6 * l + 6))

                    def turn_g(pair, want, blocks=4):
                        pe.wait_ge(gated, want)
                        for b in range(blocks):
                            for tt in range(TT):
                                o = acc(pair)[:, b // 2, (b % 2) * SEQ + tt * P:(b % 2) * SEQ + (tt + 1) * P]
                                ins = pe.transpose(o, gate[:, tt, b * P:(b + 1) * P], ident[:, :])
                        ins.then_inc(g_turned, 1)

                    def down(n, half, buf, more=0):
                        pe.wait_ge(lo_split, more + (n + 1))
                        wh, wl = slot2(w_hi, n, SPLIT), slot2(w_lo, n, SPLIT)
                        for k in range(2):
                            for tt in range(TT):
                                for c in range(2):
                                    b = 2 * half + k
                                    ins = mm3(ps[:, 4 + 2 * tt + c, :], g_hi[:, buf, b, tt * P:(tt + 1) * P],
                                              g_lo[:, buf, b, tt * P:(tt + 1) * P], wh[:, k, c * COLS:(c + 1) * COLS],
                                              wl[:, k, c * COLS:(c + 1) * COLS], False, False, skip_group_check=True)
                        ins.then_inc(unit_used, 1)

                    for k in range(4):
                        unit(f0 + k, k % 2, k // 2)
                    turn_g(0, 1)
                    pe.wait_ge(out_zeroed, 1)
                    with pe.Fori(0, (FF_FULL - 1) // 2) as i:
                        for r in range(2):
                            b = f0 + 4 + 6 * r
                            for k in range(2):
                                unit(b + k, k % 2, (r + 1) % 2, more=12 * i)
                            pe.wait_ge(glo_kept, 2 * i + (r + 1))
                            for k in range(2, 4):
                                unit(b + k, k % 2, r % 2, more=12 * i)
                            for k in range(2):
                                down(b + 4 + k, k, r % 2, more=12 * i)
                            turn_g((r + 1) % 2, 2 * i + (r + 2))
                    f1 = f0 + 4 + 6 * (FF_FULL - 1)
                    for k in range(2):
                        if k == 1:
                            pe.wait_ge(glo_kept, FF_FULL)
                        pe.wait_ge(lo_split, f1 + k + 1)
                        wh, wl = slot8(w_hi, f1 + k, SPLIT), slot8(w_lo, f1 + k, SPLIT)
                        for kt in range(KT):
                            for tt in range(TT):
                                ins = mm3(acc(1 - k)[:, tt, 0:SEQ], x_hi[:, kt, tt * P:(tt + 1) * P],
                                          x_lo[:, kt, tt * P:(tt + 1) * P], wh[:, kt, :], wl[:, kt, :], kt == 0, kt == KT - 1)
                        ins.then_inc(unit_used, 1)
                    down(f1 + 2, 0, 0)
                    down(f1 + 3, 1, 0)
                    turn_g(1, FF_FULL + 1, 2)
                    pe.wait_ge(glo_kept, FF_FULL + 1)
                    down(f1 + 4, 0, 1)

            pe.wait_ge(lo_turned, KT * 12)
            pe.wait_ge(acc_free, 32)
            narrow(2, 3).then_inc(logits_done, 1)
            pe.wait_ge(picked_sum, 1)
            sums(2, route[:, :, 9, 0:8])
            for tt in range(TT):
                ins = pe.matmul(ps[:, 2, 16:24], tri[:, P:SEQ], route[:, tt, 9, 0:8], start=tt == 0, stop=tt == 1)
            ins.then_inc(counted, 1)

            def gather(q):
                pe.wait_ge(pick_made, q + 1)
                for g in range(2):
                    for k in range(4):
                        for tt in range(TT):
                            c = (4 * g + k) * P
                            ins = pe.matmul(ps[:, 5 + g, k * P:(k + 1) * P], hn[:, tt, c:c + P], pick[:, tt, :],
                                            start=tt == 0, stop=tt == 1)
                    ins.then_inc(gathered, 1)

            def scatter(q):
                pe.wait_ge(ye_kept, q + 1)
                for n, bank in enumerate((5, 6, 7, 2)):
                    tt, c = n // 2, n % 2
                    ins = pe.matmul(ps[:, bank, :], pick_t[:, tt, :], ye[:, c * COLS:(c + 1) * COLS], start=True, stop=True)
                ins.then_inc(scattered, 1)

            def up(n, half, bank, more):
                pe.wait_ge(lo_split, more + (n + 1))
                wh, wl = slot4(w_hi, n, SPLIT), slot4(w_lo, n, SPLIT)
                for k in range(4):
                    kt = 4 * half + k
                    ins = mm3(ps[:, bank, :], xe_hi[:, kt, :], xe_lo[:, kt, :], wh[:, k, :], wl[:, k, :], kt == 0, kt == KT - 1)
                ins.then_inc(unit_used, 1)

            def down1(n, half, more):
                pe.wait_ge(lo_split, more + (n + 1))
                wh, wl = slot2(w_hi, n, SPLIT), slot2(w_lo, n, SPLIT)
                for k in range(2):
                    for c in range(2):
                        b = 2 * half + k
                        ins = mm3(ps[:, 2 + c, :], g_hi[:, 0, b, 0:P], g_lo[:, 0, b, 0:P], wh[:, k, c * COLS:(c + 1) * COLS],
                                  wl[:, k, c * COLS:(c + 1) * COLS], False, False, skip_group_check=True)
                ins.then_inc(unit_used, 1)

            def turn_e(want):
                pe.wait_ge(e_gated, want)
                for b in range(4):
                    ins = pe.transpose(ps[:, 4, b * P:(b + 1) * P], gate[:, 0, b * P:(b + 1) * P], ident[:, :])
                ins.then_inc(e_turned, 1)

            def experts(q0):
                b0 = q0 // N_EXP
                pe.wait_ge(comb_ready, 2 + 2 * b0)
                gather(q0 + b0)
                pe.transpose(ps[:, 7, 0:P], ident[:, :], ident[:, :]).then_inc(ye_done, 1)
                with pe.Fori(0, N_EXP) as e:
                    q = e + q0
                    more = E_UNITS * q
                    pe.wait_ge(xe_lo_kept, 2 * (q + b0) + 2)
                    for k in range(4):
                        up(M0 + k, k % 2, k // 2, more)
                    scatter(q + b0)
                    for tt in range(TT):
                        ins = pe.transpose(ps[:, 3, tt * P:(tt + 1) * P], pick[:, tt, :], ident[:, :])
                    ins.then_inc(pick_turned, 1)
                    turn_e(EXP_CH * q + 1)
                    with pe.Fori(0, EXP_CH - 1) as j:
                        for k in range(4):
                            up(M0 + 4 + k, k % 2, k // 2, more + 6 * j)
                        pe.wait_ge(e_lo, EXP_CH * q + j + 1)
                        pe.wait_ge(e_zeroed, q + 1)
                        for k in range(2):
                            down1(M0 + 8 + k, k, more + 6 * j)
                        turn_e(EXP_CH * q + j + 2)
                    gather(q + b0 + 1)
                    pe.wait_ge(e_lo, EXP_CH * q + EXP_CH)
                    down1(M0 + 6 * EXP_CH - 2, 0, more)
                    down1(M0 + 6 * EXP_CH - 1, 1, more)
                    pe.transpose(ps[:, 7, 0:P], ident[:, :], ident[:, :]).then_inc(ye_done, 1)
                pe.wait_ge(xe_lo_kept, 2 * (q0 + N_EXP + b0) + 2)
                scatter(q0 + N_EXP + b0)

            experts(0)
            pe.wait_ge(over_ready, 1)
            over = pe.value_load(n_over[0:1, 0:1], min_val=0, max_val=SEQ)
            with pe.If(over > 0):
                experts(N_EXP)


def lam_init(l):
    return 0.8 - 0.6 * math.exp(-0.3 * l)


NAMES = ["x", "mem", "positions", "norm_mix_g", "w_in", "lam_q1", "lam_k1", "lam_q2", "lam_k2", "diff_subln_g",
         "fox_bias", "w_out", "norm_mem_g", "mem_norm_g", "w_mq", "w_mkv", "w_mo", "norm_ffn_g", "w_ff1", "w_ff3",
         "w_ff2", "w_router", "w_e1", "w_e3", "w_e2", "final_norm_g"]


def kernel(**inputs):
    import concourse.bacc as bacc
    from concourse.bass_utils import run_bass_kernel_spmd

    nc = bacc.Bacc("TRN2", target_bir_lowering=False, num_devices=1)
    arrays, aps = {}, {}
    for name in NAMES:
        a = np.ascontiguousarray(inputs[name])
        arrays[name] = a
        aps[name] = nc.dram_tensor(name, a.shape, mybir.dt.from_np(a.dtype), kind="ExternalInput").ap()
    out = nc.dram_tensor("out", (1, SEQ, D), F32, kind="ExternalOutput").ap()
    trunk(nc, aps, out)
    r = run_bass_kernel_spmd(nc, [arrays], core_ids=[0])
    return r.results[0]["out"]
```

```python
from contextlib import ExitStack
import math

import numpy as np

import concourse.bass as bass
from concourse import mybir
from concourse.alu_op_type import AluOpType as ALU

F32 = mybir.dt.float32
F32R = mybir.dt.float32r
BF16 = mybir.dt.bfloat16
I32 = mybir.dt.int32
U32 = mybir.dt.uint32
ACT = mybir.ActivationFunctionType
AX = mybir.AxisListType

P = 128
SEQ, D = 256, 1024
TT = SEQ // P
KT = D // P
LAYERS = 2
HD = 64
N_DIFF, N_FOX = 4, 8
D_MAPS = 4 * N_DIFF * HD
C_VD = D_MAPS
C_QF = C_VD + 2 * N_DIFF * HD
C_KF = C_QF + N_FOX * HD
C_VF = C_KF + N_FOX * HD
C_FL = C_VF + N_FOX * HD
D_IN = C_FL + N_FOX
ROPE_HALF = HD // 8
MEM_HEADS, MEM_HD = 4, 256
D_FF, D_EXP, N_EXP = 2816, 3584, 8
EPS, SUB_EPS = 1e-6, 1e-5
NEG = -1e30

COLS = 512
UNIT = 2048
RAW, SPLIT = 6, 3
U_IN, U_MKV, U_OUT, U_MQ, U_MO, U_FFN = 0, 12, 20, 24, 28, 32
FF_FULL = D_FF // COLS
U_DENSE = 6 * FF_FULL + 3
L_UNITS = U_FFN + U_DENSE
EXP_CH = D_EXP // COLS
E_UNITS = 6 * EXP_CH
M0 = L_UNITS + U_FFN
ITEMS = N_DIFF + N_FOX
MAPS = 2 * N_DIFF + N_FOX
N_FINAL, N_MEM = 3 * LAYERS, 3 * LAYERS + 1
SPAN = P + SEQ

TWO_PI = 2.0 * math.pi
PI_HI = 6.28125
PI_MID = float(np.float32(round((TWO_PI - PI_HI) * 2**20) / 2**20))
PI_LO = TWO_PI - PI_HI - PI_MID
ROUND = 1.5 * 2.0**23
SIN_MAX = 3.1415925


def item_maps(i):
    return [2 * i, 2 * i + 1] if i < N_DIFF else [N_DIFF + i]


def map_item(m):
    return m // 2 if m < 2 * N_DIFF else m - N_DIFF


def map_blocks(m):
    if m < 2 * N_DIFF:
        h, which = m // 2, m % 2
        return 2 * which + h // 2, 4 + 2 * which + h // 2, HD * (h % 2)
    h = m - 2 * N_DIFF
    return 8 + h // 2, 12 + h // 2, HD * (h % 2)


def trunk(nc, t, out):
    ctx = ExitStack()
    with ctx:
        def sb(name, shape, dt=F32, stack=ctx):
            return stack.enter_context(nc.sbuf_tensor(name, shape, dt))

        def sem(name):
            return ctx.enter_context(nc.semaphore(name))

        raw = sb("raw", [P, RAW, UNIT])
        w_hi = sb("w_hi", [P, SPLIT, UNIT], F32R)
        w_lo = sb("w_lo", [P, SPLIT, UNIT], F32R)
        h = sb("h", [P, TT, D])
        hn = sb("hn", [P, TT, D])
        x_hi = sb("x_hi", [P, KT, SEQ], F32R)
        x_lo = sb("x_lo", [P, KT, SEQ], F32R)
        junk = sb("junk", [P, D], BF16)
        gain = sb("gain", [P, 65])
        ident = sb("ident", [P, P])
        tri = sb("tri", [P, SEQ])
        mask = sb("mask", [P, SPAN])
        slots = sb("slots", [P, P])
        eight = sb("eight", [P, N_EXP])
        sub_g = sb("sub_g", [P, LAYERS, P])
        fox_b = sb("fox_b", [P, LAYERS * N_FOX])
        eps_c = sb("eps_c", [P, 2])
        pos_i = sb("pos_i", [P, TT], I32)
        cs = sb("cs", [P, 2, TT, ROPE_HALF])
        small = sb("small", [P, 3, KT * 8])
        s_hi = sb("s_hi", [P, 3, KT * 8], F32R)
        s_lo = sb("s_lo", [P, 3, KT * 8], F32R)
        stat = sb("stat", [P, 8, 8])
        sub = sb("sub", [P, 5, 8])
        newton = sb("newton", [P, 2])
        mem_r = sb("mem_r", [P, TT])
        lam = sb("lam", [P, 8])
        negmax = sb("negmax", [P, MAPS, TT])
        esum = sb("esum", [P, MAPS, TT])
        einv = sb("einv", [P, MAPS, TT])
        fl = sb("fl", [P, 4, TT, N_FOX])
        cq = sb("cq", [P, TT, N_FOX])
        route = sb("route", [P, TT, 12, N_EXP + 2])
        t_idx = sb("t_idx", [P, TT, 8], U32)
        n_over = sb("n_over", [P, 1], I32)
        attn = ExitStack()
        proj = sb("proj", [P, TT, D_IN - N_FOX], stack=attn)
        kv = sb("kv", [P, TT, 2 * D], stack=attn)
        qkt = sb("qkt", [P, 16, SEQ], stack=attn)
        decay = sb("decay", [P, N_FOX, SPAN], stack=attn)
        attn.close()
        ffn = ExitStack()
        gate = sb("gate", [P, TT, COLS], stack=ffn)
        g_hi = sb("g_hi", [P, 2, 4, SEQ], F32R, stack=ffn)
        g_lo = sb("g_lo", [P, 2, 4, SEQ], F32R, stack=ffn)
        xe_hi = sb("xe_hi", [P, KT, P], F32R, stack=ffn)
        xe_lo = sb("xe_lo", [P, KT, P], F32R, stack=ffn)
        ye = sb("ye", [P, D], stack=ffn)
        pick = sb("pick", [P, TT, P], stack=ffn)
        pick_t = sb("pick_t", [P, TT, P], stack=ffn)
        ffn_g = sb("ffn_g", [P, D], stack=ffn)
        fin_g = sb("fin_g", [P, D], stack=ffn)
        result = sb("result", [P, TT, D], stack=ffn)
        ffn.close()

        mixed = proj[:, :, 0:D]
        mem_q = proj[:, :, D:2 * D]
        gain_rows = hn[0:64, 0, 0:P]
        ang = hn[:, 1, 0:256].rearrange("p (s k t i) -> p s k t i", s=8, k=2, t=TT)
        inv_f = hn[:, 1, 512:512 + ROPE_HALF]
        lam_v = kv[:, 0, D:D + 4 * LAYERS * HD].rearrange("p (v n) -> p v n", v=4)
        pos_f = hn[:, 1, 544:544 + TT]

        def probs(m):
            return proj[:, (m % 4) // 2, C_QF + (m % 2) * SPAN:C_QF + (m % 2 + 1) * SPAN]

        def probs_t(i):
            return hn[:, i % 2, 0:SPAN]

        def mem_p(i):
            return decay[:, 2 * (i % 2):2 * (i % 2) + 2, 0:SEQ]

        def mem_pt(i):
            return hn[:, i % 2, 0:2 * SEQ]

        ps = ctx.enter_context(nc.psum_tensor("ps", [P, 8, COLS], F32))

        def acc(pair):
            return ps[:, 2 * pair:2 * pair + 2, :]

        raw_landed = [sem(f"raw_landed{i}") for i in range(RAW)]
        hi_split, lo_split, unit_used = sem("hi_split"), sem("lo_split"), sem("unit_used")
        x_landed, mem_landed, mem_again, out_landed = (
            sem("x_landed"), sem("mem_landed"), sem("mem_again"), sem("out_landed"))
        const_landed, late_landed = sem("const_landed"), sem("late_landed")
        pool_made, final_step = sem("pool_made"), sem("final_step")
        gains_turned, gains_kept = sem("gains_turned"), sem("gains_kept")
        ang_ready, sin_ready = sem("ang_ready"), sem("sin_ready")
        dots_ready, lam_exp, small_split = sem("dots_ready"), sem("lam_exp"), sem("small_split")
        rs_est, source_ready, ffn_added = sem("rs_est"), sem("source_ready"), sem("ffn_added")
        ident_made, gains_landed, pos_landed = sem("ident_made"), sem("gains_landed"), sem("pos_landed")
        ffn_rooted, hn_ready, result_ready = sem("ffn_rooted"), sem("hn_ready"), sem("result_ready")
        mem_est, mem_free = sem("mem_est"), sem("mem_free")
        turned, hi_turned, lo_turned = sem("turned"), sem("hi_turned"), sem("lo_turned")
        acc_free = sem("acc_free")
        dve_step, act_step, pool_step = sem("dve_step"), sem("act_step"), sem("pool_step")
        fl_done, fl_neg, fl_ln, logf_ready = sem("fl_done"), sem("fl_neg"), sem("fl_ln"), sem("logf_ready")
        roped, qk_turned, qk_kept = sem("roped"), sem("qk_turned"), sem("qk_kept")
        cq_done, ck_done, ck_used = sem("cq_done"), sem("ck_done"), sem("ck_used")
        scored, masked, expd, weighed = sem("scored"), sem("masked"), sem("expd"), sem("weighed")
        p_turned, p_kept, pv_done, pv_taken = sem("p_turned"), sem("p_kept"), sem("pv_done"), sem("pv_taken")
        sub_est = sem("sub_est")
        mqk_turned, mqk_kept = sem("mqk_turned"), sem("mqk_kept")
        mscored, mmax, mexpd = sem("mscored"), sem("mmax"), sem("mexpd")
        mp_turned, mp_kept, mpv_done, mpv_taken = sem("mp_turned"), sem("mp_kept"), sem("mpv_done"), sem("mpv_taken")
        silu_done, gated, g_turned = sem("silu_done"), sem("gated"), sem("g_turned")
        ghi_kept, glo_kept, out_zeroed = sem("ghi_kept"), sem("glo_kept"), sem("out_zeroed")
        routed, route_exp, picked_sum, counted = sem("routed"), sem("route_exp"), sem("picked_sum"), sem("counted")
        logits_done, comb_ready, over_ready = sem("logits_done"), sem("comb_ready"), sem("over_ready")
        e_silu, e_gated, e_turned = sem("e_silu"), sem("e_gated"), sem("e_turned")
        e_hi, e_lo, e_zeroed = sem("e_hi"), sem("e_lo"), sem("e_zeroed")
        pick_made, gathered, xe_hi_kept, xe_lo_kept = sem("pick_made"), sem("gathered"), sem("xe_hi_kept"), sem("xe_lo_kept")
        ye_done, ye_kept, scattered, pick_turned, pick_kept = (
            sem("ye_done"), sem("ye_kept"), sem("scattered"), sem("pick_turned"), sem("pick_kept"))
        summed, hn_gained = sem("summed"), sem("hn_gained")

        def halves(w):
            return w.rearrange("(u k p) n -> u p k n", k=4, p=P)

        w_in = [halves(t["w_in"][l]) for l in range(LAYERS)]
        w_out = [halves(t["w_out"][l]) for l in range(LAYERS)]
        w_mq = [halves(t["w_mq"][l]) for l in range(LAYERS)]
        w_mkv = [halves(t["w_mkv"][l]) for l in range(LAYERS)]
        w_mo = [halves(t["w_mo"][l]) for l in range(LAYERS)]
        ff1, ff3 = halves(t["w_ff1"][0]), halves(t["w_ff3"][0])
        ff2 = t["w_ff2"][0].rearrange("(u k p) n -> u p k n", k=2, p=P)
        e1 = t["w_e1"].rearrange("a e (u k p) f -> (a e u) p k f", k=4, p=P)
        e3 = t["w_e3"].rearrange("a e (u k p) f -> (a e u) p k f", k=4, p=P)
        e2 = t["w_e2"].rearrange("a e (u k p) n -> (a e u) p k n", k=2, p=P)

        def slot4(buf, n, size):
            return buf[:, n % size, :].rearrange("p (k n) -> p k n", k=4)

        def slot2(buf, n, size):
            return buf[:, n % size, :].rearrange("p (k n) -> p k n", k=2)

        def slot8(buf, n, size):
            return buf[:, n % size, :].rearrange("p (k n) -> p k n", k=8)

        block = ctx.enter_context(nc.Block())

        @block.sync
        def _(sp):
            def load(n, src, view=slot4, more=0):
                if n >= RAW:
                    sp.wait_ge(lo_split, more + (n - RAW + 1))
                sp.dma_start(view(raw, n, RAW), src).then_inc(raw_landed[n % RAW], 16)

            def small_loads():
                for i, v in enumerate(("lam_q1", "lam_k1", "lam_q2", "lam_k2")):
                    sp.dma_start(lam_v[:, i, :], t[v].rearrange("l d -> (l d)").partition_broadcast(P)).then_inc(const_landed, 16)
                sp.dma_start(sub_g[:, :, :], t["diff_subln_g"].partition_broadcast(P)).then_inc(const_landed, 16)
                sp.dma_start(fox_b[:, :], t["fox_bias"].rearrange("l n -> (l n)").partition_broadcast(P)).then_inc(const_landed, 16)
                for l in range(LAYERS):
                    sp.dma_start(small[:, l, :].rearrange("p (k n) -> p k n", n=N_FOX),
                                 t["w_in"][l].rearrange("(k p) n -> p k n", p=P)[:, :, C_FL:D_IN]).then_inc(const_landed, 16)
                sp.dma_start(small[:, 2, :].rearrange("p (k n) -> p k n", n=N_EXP),
                             t["w_router"][0].rearrange("(k p) n -> p k n", p=P)).then_inc(const_landed, 16)

            gains = (t["norm_mix_g"], t["norm_mem_g"], t["mem_norm_g"], t["norm_ffn_g"])
            for i, g in enumerate(gains):
                sp.dma_start(gain_rows[16 * i:16 * i + 16, :],
                             g.rearrange("l (k p) -> (l k) p", p=P)).then_inc(gains_landed, 16)
            sp.dma_start(h[:, :, :], t["x"][0].rearrange("(t p) n -> p t n", p=P)).then_inc(x_landed, 16)
            for l in range(LAYERS):
                n0 = l * L_UNITS
                if l == 0:
                    for c in range(6):
                        for u in range(2):
                            load(n0 + 2 * c + u, w_in[l][u, :, :, c * COLS:(c + 1) * COLS])
                            if (c, u) == (0, 1):
                                small_loads()
                            if (c, u) == (1, 0):
                                sp.dma_start(kv[:, :, 0:D], t["mem"][0].rearrange("(t p) n -> p t n", p=P)).then_inc(mem_landed, 16)
                else:
                    with sp.Fori(0, 2) as i:
                        for c in range(3):
                            for u in range(2):
                                load(n0 + 2 * c + u, w_in[l][u, :, :, bass.ds((3 * i + c) * COLS, COLS)], more=6 * i)
                for at, w, chunks in ((U_MKV, w_mkv, 4), (U_OUT, w_out, 2), (U_MQ, w_mq, 2), (U_MO, w_mo, 2)):
                    for c in range(chunks):
                        for u in range(2):
                            load(n0 + at + 2 * c + u, w[l][u, :, :, c * COLS:(c + 1) * COLS])
                if l == 0:
                    f0 = n0 + U_FFN
                    for k in range(4):
                        load(f0 + k, (ff1, ff3)[k // 2][k % 2, :, :, 0:COLS])
                    with sp.Fori(0, FF_FULL - 1) as i:
                        for k in range(4):
                            load(f0 + 4 + k, (ff1, ff3)[k // 2][k % 2, :, :, bass.ds((i + 1) * COLS, COLS)], more=6 * i)
                        for u in range(2):
                            load(f0 + 8 + u, ff2[2 * i + u], slot2, more=6 * i)
                    f1 = f0 + 4 + 6 * (FF_FULL - 1)
                    for k, w in enumerate((t["w_ff1"][0], t["w_ff3"][0])):
                        load(f1 + k, w.rearrange("(k p) n -> p k n", p=P)[:, :, FF_FULL * COLS:D_FF], slot8)
                    for u in range(3):
                        load(f1 + 2 + u, ff2[2 * (FF_FULL - 1) + u], slot2)

            def experts(q0):
                with sp.Fori(0, N_EXP) as e:
                    q = E_UNITS * (e + q0)
                    for k in range(4):
                        load(M0 + k, (e1, e3)[k // 2][2 * e + k % 2, :, :, 0:COLS], more=q)
                    with sp.Fori(1, EXP_CH) as j:
                        for k in range(4):
                            load(M0 + 4 + k, (e1, e3)[k // 2][2 * e + k % 2, :, :, bass.ds(j * COLS, COLS)],
                                 more=q + 6 * (j - 1))
                        for u in range(2):
                            load(M0 + 8 + u, e2[2 * EXP_CH * e + 2 * (j - 1) + u], slot2, more=q + 6 * (j - 1))
                    for u in range(2):
                        load(M0 + 6 * EXP_CH - 2 + u, e2[2 * EXP_CH * e + 2 * (EXP_CH - 1) + u], slot2, more=q)

            experts(0)
            sp.wait_ge(over_ready, 1)
            over = sp.value_load(n_over[0:1, 0:1], min_val=0, max_val=SEQ)
            with sp.If(over > 0):
                experts(N_EXP)
            sp.wait_ge(out_landed, 32)

        @block.gpsimd
        def _(pool):
            pool.memset(ident[:, :], 0.0).then_inc(pool_step, 1)
            pool.wait_ge(pool_step, 1)
            pool.affine_select(out=ident[:, :], in_=ident[:, :], compare_op=ALU.not_equal, fill=1.0, base=0,
                               pattern=[[-1, P]], channel_multiplier=1).then_inc(ident_made, 1)
            pool.dma_start(pos_i[:, :], t["positions"].rearrange("b (t p) -> p (b t)", p=P),
                           allow_slow_non_contiguous=True).then_inc(pos_landed, 16)

            pool.memset(tri[:, :], 1.0).then_inc(pool_step, 1)
            pool.memset(mask[:, :], 0.0).then_inc(pool_step, 1)
            pool.wait_ge(pool_step, 3)
            pool.affine_select(out=tri[:, 0:P], in_=tri[:, 0:P], compare_op=ALU.is_ge, fill=0.0, base=0,
                               pattern=[[1, P]], channel_multiplier=-1).then_inc(pool_made, 1)
            for c in (0, SEQ):
                pool.affine_select(out=mask[:, c:c + P], in_=mask[:, c:c + P], compare_op=ALU.is_ge, fill=NEG, base=0,
                                   pattern=[[-1, P]], channel_multiplier=1).then_inc(pool_made, 1)
            pool.iota(slots[:, :], pattern=[[1, P]], base=1, channel_multiplier=0,
                      allow_small_or_imprecise_dtypes=True).then_inc(pool_made, 1)
            pool.iota(eight[:, :], pattern=[[1, N_EXP]], base=0, channel_multiplier=0,
                      allow_small_or_imprecise_dtypes=True).then_inc(pool_made, 1)
            pool.wait_ge(ffn_added, 1)
            pool.dma_start(kv[:, :, 0:D], t["mem"][0].rearrange("(t p) n -> p t n", p=P)).then_inc(mem_again, 16)
            pool.wait_ge(acc_free, 32)
            pool.dma_start(ffn_g[:, :], t["norm_ffn_g"][1].partition_broadcast(P)).then_inc(late_landed, 16)
            pool.dma_start(fin_g[:, :], t["final_norm_g"].partition_broadcast(P)).then_inc(late_landed, 16)

        @block.scalar
        def _(act):
            steps = [0]

            def link(ins):
                steps[0] += 1
                ins.then_inc(act_step, 1)
                act.wait_ge(act_step, steps[0])

            def split(n, more=0, turns=0):
                act.wait_ge(raw_landed[n % RAW], 16 * turns + 16 * (n // RAW + 1))
                if n >= SPLIT:
                    act.wait_ge(unit_used, more + (n - SPLIT + 1))
                act.activation(w_hi[:, n % SPLIT, :], raw[:, n % RAW, :], ACT.Copy).then_inc(hi_split, 1)

            def splits(a, b):
                for n in range(a, b):
                    split(n)

            def turn_hi(tn, columns, groups=range(4)):
                for g in groups:
                    act.wait_ge(turned, 4 * tn + g + 1)
                    for k in (2 * g, 2 * g + 1):
                        c = columns(k)
                        act.activation(x_hi[:, k, :], ps[:, 6 + g % 2, (k % 2) * SEQ:(k % 2 + 1) * SEQ], ACT.Copy,
                                       scale=gain[:, c:c + 1]).then_inc(hi_turned, 1)

            def norm_stats(src, at, inc):
                for tt in range(TT):
                    link(act.activation(junk[:, :], src[:, tt, 0:D], ACT.Square, accum_out=stat[:, at, tt:tt + 1]))
                link(act.activation(stat[:, at, 2:4], stat[:, at, 0:2], ACT.Ln, scale=1.0 / D, bias=eps_c[:, 0:1]))
                act.activation(stat[:, at, 4:6], stat[:, at, 2:4], ACT.Exp, scale=-0.5).then_inc(inc, 1)

            def half_turns(tn, columns, b, more):
                splits(b + 3, b + 5)
                turn_hi(tn, columns, (0, 1))
                splits(b + 5, b + 7)
                turn_hi(tn, columns, (2, 3))
                splits(b + 7, b + 7 + more)

            for l in range(LAYERS):
                n0 = l * L_UNITS
                if l == 0:
                    act.wait_ge(ang_ready, 1)
                    act.activation(cs[:, :, :, :], ang[:, 4, :, :, :], ACT.Sin).then_inc(sin_ready, 1)
                    act.wait_ge(gains_kept, 1)
                turn_hi(6 * l, lambda k: 8 * l + k)
                if l == 0:
                    splits(n0, n0 + 1)
                norm_stats(h, 3 * l, rs_est)
                if l == 0:
                    splits(n0 + 1, n0 + 3)
                    act.wait_ge(mem_landed, 16)
                    norm_stats(kv, N_MEM, mem_est)
                    act.wait_ge(dots_ready, 1)
                    act.activation(lam[:, 4:8], lam[:, 0:4], ACT.Exp).then_inc(lam_exp, 1)
                with act.Fori(0, 2) as i:
                    for k in range(6):
                        split(n0 + 3 + k, 6 * i, i)
                turn_hi(6 * l + 1, lambda k: 32 + 8 * l + k)

                act.wait_ge(fl_neg, l + 1)
                link(act.activation(fl[:, 2, :, :], fl[:, 1, :, :], ACT.Exp))
                act.activation(fl[:, 3, :, :], fl[:, 2, :, :], ACT.Ln, bias=1.0).then_inc(fl_ln, 1)
                splits(n0 + 15, n0 + 16)

                def keep_qk(g):
                    act.wait_ge(qk_turned, 8 * l + g + 1)
                    queries = g in (0, 1, 4, 5)
                    act.activation(qkt[:, 2 * g:2 * g + 2, :],
                                   ps[:, 6 + g % 2, :].rearrange("p (b n) -> p b n", b=2), ACT.Copy,
                                   scale=1.0 / math.sqrt(HD) if queries else 1.0).then_inc(qk_kept, 1)

                def exps(i):
                    for m in item_maps(i):
                        act.wait_ge(masked, MAPS * l + m + 1)
                        for tt, a, b in ((0, 0, P), (1, P, SPAN)):
                            ins = act.activation(probs(m)[:, a:b], probs(m)[:, a:b], ACT.Exp,
                                                 bias=negmax[:, m, tt:tt + 1], accum_out=esum[:, m, tt:tt + 1])
                        ins.then_inc(expd, 1)

                def keep_pt(i):
                    act.wait_ge(p_turned, ITEMS * l + i + 1)
                    if i >= 2:
                        act.wait_ge(pv_done, ITEMS * l + i - 1)
                    act.activation(probs_t(i), ps[:, 6 + i % 2, 0:SPAN], ACT.Copy).then_inc(p_kept, 1)

                for g in range(4):
                    keep_qk(g)
                splits(n0 + 16, n0 + 17)
                for g in range(4, 8):
                    keep_qk(g)
                splits(n0 + 17, n0 + 18)
                nxt = n0 + 18
                for s in range(ITEMS + 1):
                    if s < ITEMS:
                        exps(s)
                    if s < 5:
                        split(nxt)
                        nxt += 1
                    if s >= 1:
                        keep_pt(s - 1)
                    if s == N_DIFF + 1:
                        act.wait_ge(pv_taken, ITEMS * l + N_DIFF)
                        for i in range(N_DIFF):
                            for tt in range(TT):
                                ins = act.activation(junk[:, (2 * i + tt) * P:(2 * i + tt + 1) * P], mixed[:, tt, i * P:(i + 1) * P], ACT.Square,
                                                     accum_out=sub[:, 0, 2 * i + tt:2 * i + tt + 1])
                        link(ins)
                        link(act.activation(sub[:, 1, :], sub[:, 0, :], ACT.Ln, scale=1.0 / P, bias=eps_c[:, 1:2]))
                        act.activation(sub[:, 2, :], sub[:, 1, :], ACT.Exp, scale=-0.5).then_inc(sub_est, 1)
                turn_hi(6 * l + 2, lambda k: 64)
                half_turns(6 * l + 3, lambda k: 16 + 8 * l + k, n0 + U_OUT, 1)
                norm_stats(h, 3 * l + 1, rs_est)
                splits(n0 + 28, n0 + 31)

                def keep_mqk(g):
                    act.wait_ge(mqk_turned, 8 * l + g + 1)
                    act.activation(qkt[:, 2 * g:2 * g + 2, :],
                                   ps[:, 6 + g % 2, :].rearrange("p (b n) -> p b n", b=2), ACT.Copy,
                                   scale=1.0 / math.sqrt(MEM_HD) if g >= 4 else 1.0).then_inc(mqk_kept, 1)

                for g in range(8):
                    keep_mqk(g)
                for s in range(MEM_HEADS + 1):
                    if s < MEM_HEADS:
                        act.wait_ge(mmax, MEM_HEADS * l + s + 1)
                        for tt in range(TT):
                            ins = act.activation(mem_p(s)[:, tt, :], ps[:, 4 + s % 2, tt * SEQ:(tt + 1) * SEQ], ACT.Exp,
                                                 bias=negmax[:, s, tt:tt + 1], accum_out=esum[:, s, tt:tt + 1])
                        ins.then_inc(mexpd, 1)
                    if s >= 1:
                        act.wait_ge(mp_turned, MEM_HEADS * l + s)
                        if s >= 3:
                            act.wait_ge(mpv_done, MEM_HEADS * l + s - 2)
                        act.activation(mem_pt(s - 1), ps[:, 6 + (s - 1) % 2, :], ACT.Copy).then_inc(mp_kept, 1)
                turn_hi(6 * l + 4, lambda k: 64)
                half_turns(6 * l + 5, lambda k: 48 + 8 * l + k, n0 + U_MO, 1 - l)
                norm_stats(h, 3 * l + 2, rs_est)

                if l == 0:
                    f0 = n0 + U_FFN

                    def silu(pair, used, wide=COLS):
                        act.wait_ge(unit_used, used)
                        for tt in range(TT):
                            ins = act.activation(gate[:, tt, 0:wide], acc(pair)[:, tt, 0:wide], ACT.Silu,
                                                 scale=stat[:, 2, 6 + tt:7 + tt])
                        ins.then_inc(silu_done, 1)

                    def keep_hi(pair, buf, want, blocks=4):
                        act.wait_ge(g_turned, want)
                        act.activation(g_hi[:, buf, 0:blocks, :], acc(pair).rearrange("p c (b n) -> p (c b) n", n=SEQ)[:, 0:blocks, :],
                                       ACT.Copy).then_inc(ghi_kept, 1)

                    act.wait_ge(ffn_rooted, 1)
                    silu(0, f0 + 2)
                    splits(f0 + 4, f0 + 6)
                    keep_hi(0, 0, 1)
                    with act.Fori(0, (FF_FULL - 1) // 2) as i:
                        for r in range(2):
                            b = f0 + 4 + 6 * r
                            for k in (2, 3):
                                split(b + k, 12 * i, 2 * i)
                            silu((r + 1) % 2, 12 * i + (b + 2))
                            for k in range(4, 8):
                                split(b + k, 12 * i, 2 * i)
                            keep_hi((r + 1) % 2, (r + 1) % 2, 2 * i + (r + 2))
                    f1 = f0 + 4 + 6 * (FF_FULL - 1)
                    splits(f1 + 2, f1 + 3)
                    silu(1, f1 + 1, SEQ)
                    splits(f1 + 3, f1 + 5)
                    keep_hi(1, 1, FF_FULL + 1, 2)
                    splits(L_UNITS, L_UNITS + 3)

            act.wait_ge(routed, 1)
            act.activation(route[:, :, 4, 0:1], route[:, :, 3, 0:1], ACT.Exp).then_inc(route_exp, 1)

            def keep_xe(q):
                for g in range(2):
                    act.wait_ge(gathered, q * 2 + (g + 1))
                    act.activation(xe_hi[:, 4 * g:4 * g + 4, :], ps[:, 5 + g, :].rearrange("p (k n) -> p k n", k=4),
                                   ACT.Copy).then_inc(xe_hi_kept, 1)

            def keep_ye(q):
                act.wait_ge(ye_done, q + 1)
                act.activation(ye[:, :].rearrange("p (c n) -> p c n", c=2), ps[:, 2:4, :], ACT.Copy).then_inc(ye_kept, 1)

            def expert(q, b0, ahead=0):
                more = E_UNITS * q

                def s(k, j=0):
                    split(M0 + k, more + 6 * j, EXP_CH * q + j)

                for k in range(ahead, 2):
                    s(k)
                keep_ye(q + b0)
                for k in range(max(ahead, 2), 4):
                    s(k)
                act.wait_ge(unit_used, more + (M0 + 2))
                act.activation(gate[:, 0, :], ps[:, 0, :], ACT.Silu).then_inc(e_silu, 1)
                s(4), s(5)
                act.wait_ge(pick_turned, q + 1)
                act.activation(pick_t[:, :, :], ps[:, 3, 0:SEQ].rearrange("p (t n) -> p t n", t=TT), ACT.Copy).then_inc(pick_kept, 1)
                act.wait_ge(e_turned, EXP_CH * q + 1)
                act.activation(g_hi[:, 0, :, 0:P], ps[:, 4, :].rearrange("p (b n) -> p b n", b=4), ACT.Copy).then_inc(e_hi, 1)
                with act.Fori(0, EXP_CH - 1) as j:
                    s(6, j), s(7, j)
                    act.wait_ge(unit_used, more + 6 * j + (M0 + 6))
                    act.activation(gate[:, 0, :], ps[:, 0, :], ACT.Silu).then_inc(e_silu, 1)
                    for k in range(8, 12):
                        s(k, j)
                    act.wait_ge(e_turned, EXP_CH * q + j + 2)
                    act.activation(g_hi[:, 0, :, 0:P], ps[:, 4, :].rearrange("p (b n) -> p b n", b=4), ACT.Copy).then_inc(e_hi, 1)
                keep_xe(q + b0 + 1)

            keep_xe(0)
            expert(0, 0, ahead=3)
            with act.Fori(1, N_EXP) as e:
                expert(e, 0)
            keep_ye(N_EXP)
            act.wait_ge(over_ready, 1)
            over = act.value_load(n_over[0:1, 0:1], min_val=0, max_val=SEQ)
            with act.If(over > 0):
                keep_xe(N_EXP + 1)
                with act.Fori(0, N_EXP) as e:
                    expert(e + N_EXP, 1)
                keep_ye(2 * N_EXP + 1)
            act.wait_ge(summed, 1)
            norm_stats(h, N_FINAL, rs_est)
            for tt in range(TT):
                act.wait_ge(result_ready, tt + 1)
                act.dma_start(out[0, tt * P:(tt + 1) * P, :], result[:, tt, :]).then_inc(out_landed, 16)

        @block.vector
        def _(dve):
            steps = [0]

            def link(ins):
                steps[0] += 1
                ins.then_inc(dve_step, 1)
                dve.wait_ge(dve_step, steps[0])

            def split(n, more=0):
                dve.wait_ge(hi_split, more + (n + 1))
                dve.tensor_tensor(w_lo[:, n % SPLIT, :], raw[:, n % RAW, :], w_hi[:, n % SPLIT, :].bitcast(F32),
                                  ALU.subtract).then_inc(lo_split, 1)

            def splits(a, b):
                for n in range(a, b):
                    split(n)

            def turn_lo(tn, columns, tiles=range(KT)):
                for k in tiles:
                    dve.wait_ge(hi_turned, KT * tn + k // 2 * 2 + 2)
                    c = columns(k)
                    dve.scalar_tensor_tensor(out=x_lo[:, k, :], in0=ps[:, 6 + k // 2 % 2, (k % 2) * SEQ:(k % 2 + 1) * SEQ],
                                             scalar=gain[:, c:c + 1], in1=x_hi[:, k, :].bitcast(F32),
                                             op0=ALU.mult, op1=ALU.subtract).then_inc(lo_turned, 1)

            def refine(y, v, y0, tmp):
                link(dve.tensor_tensor(tmp, y0, y0, ALU.mult))
                link(dve.tensor_tensor(tmp, tmp, v, ALU.mult))
                link(dve.tensor_scalar(tmp, tmp, -0.5, 1.5, ALU.mult, ALU.add))
                link(dve.tensor_tensor(y, y0, tmp, ALU.mult))

            def rstd(at):
                link(dve.tensor_scalar(stat[:, at, 2:4], stat[:, at, 0:2], 1.0 / D, EPS, ALU.mult, ALU.add))
                refine(stat[:, at, 6:8], stat[:, at, 2:4], stat[:, at, 4:6], newton[:, :])

            def norm(number):
                dve.wait_ge(rs_est, number + 1)
                rstd(number)

            def root(number, tt):
                return stat[:, number, 6 + tt:7 + tt]

            for i in range(ROPE_HALF):
                f = float(np.float32(500000.0) ** np.float32(-2.0 * i / (2 * ROPE_HALF)))
                ins = dve.memset(inv_f[:, i:i + 1], f)
            dve.memset(eps_c[:, 0:1], EPS)
            dve.memset(eps_c[:, 1:2], SUB_EPS)
            dve.memset(gain[:, 64:65], 1.0)
            link(ins)
            dve.wait_ge(pos_landed, 16)
            link(dve.tensor_copy(pos_f, pos_i[:, :]))
            for tt in range(TT):
                ins = dve.tensor_scalar(ang[:, 0, 1, tt, :], inv_f, pos_f[:, tt:tt + 1], None, ALU.mult)
            link(ins)
            link(dve.tensor_copy(ang[:, 0, 0, :, :], ang[:, 0, 1, :, :]))
            dve.tensor_scalar(ang[:, 1, 0, :, :], ang[:, 0, 0, :, :], 1.0 / TWO_PI, 0.25, ALU.mult, ALU.add)
            link(dve.tensor_scalar(ang[:, 1, 1, :, :], ang[:, 0, 1, :, :], 1.0 / TWO_PI, None, ALU.mult))
            link(dve.tensor_scalar(ang[:, 2, :, :, :], ang[:, 1, :, :, :], ROUND, None, ALU.add))
            link(dve.tensor_scalar(ang[:, 3, :, :, :], ang[:, 2, :, :, :], -ROUND, None, ALU.add))
            for part in (PI_HI, PI_MID, PI_LO):
                link(dve.scalar_tensor_tensor(out=ang[:, 0, :, :, :], in0=ang[:, 3, :, :, :], scalar=-part,
                                              in1=ang[:, 0, :, :, :], op0=ALU.mult, op1=ALU.add))
            link(dve.tensor_scalar(ang[:, 0, 0, :, :], ang[:, 0, 0, :, :], math.pi / 2, None, ALU.add))
            dve.tensor_scalar(ang[:, 4, :, :, :], ang[:, 0, :, :, :], SIN_MAX, -SIN_MAX, ALU.min, ALU.max).then_inc(ang_ready, 1)
            link(dve.memset(route[:, :, :, :], 0.0))
            dve.wait_ge(gains_turned, 1)
            dve.tensor_copy(gain[:, 0:64], ps[:, 0, 0:64]).then_inc(gains_kept, 1)
            dve.wait_ge(gains_kept, 1)
            turn_lo(0, lambda k: k)
            splits(0, 1)
            norm(0)
            splits(1, 3)
            dve.wait_ge(const_landed, 16 * 9)
            for i in range(2):
                for l in range(LAYERS):
                    a, b = lam_v[:, 2 * i, l * HD:(l + 1) * HD], lam_v[:, 2 * i + 1, l * HD:(l + 1) * HD]
                    ins = dve.tensor_tensor_reduce(decay[:, 2 * i + l, 0:HD],
                                                   a, b, 1.0, 0.0, ALU.mult, ALU.add, lam[:, 2 * i + l:2 * i + l + 1])
            ins.then_inc(dots_ready, 1)
            for l in range(LAYERS):
                ins = dve.tensor_scalar(sub_g[:, l, :], sub_g[:, l, :], 1.0 - lam_init(l), None, ALU.mult)
            dve.wait_ge(lam_exp, 1)
            for l in range(LAYERS):
                ins = dve.scalar_tensor_tensor(out=lam[:, l:l + 1], in0=lam[:, 4 + l:5 + l], scalar=lam_init(l),
                                               in1=lam[:, 6 + l:7 + l], op0=ALU.add, op1=ALU.subtract)
            link(ins)
            link(dve.tensor_copy(s_hi[:, :, :], small[:, :, :]))
            dve.tensor_tensor(s_lo[:, :, :], small[:, :, :], s_hi[:, :, :].bitcast(F32), ALU.subtract).then_inc(small_split, 1)
            dve.wait_ge(sin_ready, 1)

            for l in range(LAYERS):
                n0 = l * L_UNITS
                a0 = 16 * l
                if l:
                    turn_lo(6 * l, lambda k: 8 * l + k)
                if l == 0:
                    dve.wait_ge(mem_est, 1)
                    rstd(N_MEM)
                else:
                    norm(3 * l)
                dve.wait_ge((mem_landed, mem_again)[l], 16)
                for tt in range(TT):
                    ins = dve.tensor_scalar(hn[:, tt, :], kv[:, tt, 0:D], root(N_MEM, tt), None, ALU.mult)
                ins.then_inc(source_ready, 1)
                with dve.Fori(0, 2) as i:
                    for c in range(3):
                        split(n0 + 3 + 2 * c, 6 * i)
                        split(n0 + 4 + 2 * c, 6 * i)
                        dve.wait_ge(unit_used, 6 * i + (n0 + 2 * c + 2))
                        for tt in range(TT):
                            ins = dve.tensor_scalar(proj[:, tt, bass.ds((3 * i + c) * COLS, COLS)], acc(c)[:, tt, :],
                                                    root(3 * l, tt), None, ALU.mult)
                        ins.then_inc(acc_free, 1)
                dve.wait_ge(fl_done, l + 1)
                for tt in range(TT):
                    ins = dve.scalar_tensor_tensor(out=fl[:, 0, tt, :], in0=ps[:, 7, tt * N_FOX:(tt + 1) * N_FOX],
                                                   scalar=root(3 * l, tt), in1=fox_b[:, l * N_FOX:(l + 1) * N_FOX],
                                                   op0=ALU.mult, op1=ALU.add)
                link(ins)
                dve.scalar_tensor_tensor(out=fl[:, 1, :, :], in0=fl[:, 0, :, :], scalar=-1.0, in1=fl[:, 0, :, :],
                                         op0=ALU.mult, op1=ALU.min).then_inc(fl_neg, 1)
                turn_lo(6 * l + 1, lambda k: 32 + 8 * l + k)
                heads = proj[:, :, 0:D_MAPS].rearrange("p t (h d) -> p t h d", d=HD)
                rot = decay[:, :, :].rearrange("p a b -> p (a b)")[:, 0:1024].rearrange(
                    "p (s t h i) -> p s t h i", s=4, t=TT, h=16)
                for tt in range(TT):
                    t1, t2 = heads[:, tt, :, 0:ROPE_HALF], heads[:, tt, :, ROPE_HALF:2 * ROPE_HALF]
                    cos = cs[:, 0, tt, :].unsqueeze(1).to_broadcast([P, 16, ROPE_HALF])
                    sin = cs[:, 1, tt, :].unsqueeze(1).to_broadcast([P, 16, ROPE_HALF])
                    for s, (x, f) in enumerate(((t1, cos), (t2, sin), (t2, cos), (t1, sin))):
                        ins = dve.tensor_tensor(rot[:, s, tt], x, f, ALU.mult)
                link(ins)
                for tt in range(TT):
                    dve.tensor_tensor(heads[:, tt, :, 0:ROPE_HALF], rot[:, 0, tt], rot[:, 1, tt], ALU.subtract)
                    ins = dve.tensor_tensor(heads[:, tt, :, ROPE_HALF:2 * ROPE_HALF], rot[:, 2, tt], rot[:, 3, tt], ALU.add)
                ins.then_inc(roped, 1)
                dve.wait_ge(fl_ln, l + 1)
                dve.scalar_tensor_tensor(out=fl[:, 1, :, :], in0=fl[:, 0, :, :], scalar=0.0, in1=fl[:, 3, :, :],
                                         op0=ALU.min, op1=ALU.subtract).then_inc(logf_ready, 1)

                def evict(c, dst):
                    dve.wait_ge(unit_used, n0 + 2 * c + 2)
                    dve.tensor_copy(dst, acc(0)).then_inc(acc_free, 1)

                splits(n0 + 15, n0 + 16)
                evict(6, kv[:, :, 0:COLS])
                splits(n0 + 16, n0 + 17)

                def mask_map(m):
                    dve.wait_ge(scored, MAPS * l + m + 1)
                    if m >= 4:
                        dve.wait_ge(p_turned, ITEMS * l + map_item(m - 4) + 1)
                    elif l:
                        dve.wait_ge(p_turned, ITEMS * l)
                    for tt, a, b in ((0, 0, P), (1, P, SPAN)):
                        add = mask[:, a:b] if m < 2 * N_DIFF else decay[:, m - 2 * N_DIFF, a:b]
                        ins = dve.tensor_tensor_reduce(probs(m)[:, a:b], ps[:, 4 + m % 2, a:b], add, 1.0, 3 * NEG,
                                                       ALU.add, ALU.max, negmax[:, m, tt:tt + 1])
                    link(ins)
                    dve.tensor_scalar(negmax[:, m, :], negmax[:, m, :], -1.0, None, ALU.mult).then_inc(masked, 1)

                def weigh(i):
                    for m in item_maps(i):
                        dve.wait_ge(expd, MAPS * l + m + 1)
                        ins = dve.reciprocal(einv[:, m, :], esum[:, m, :])
                    link(ins)
                    if i < N_DIFF:
                        a, b = item_maps(i)
                        link(dve.tensor_scalar(einv[:, b, :], einv[:, b, :], lam[:, l:l + 1], None, ALU.mult))
                        for tt, x, y in ((0, 0, P), (1, P, SPAN)):
                            ins = dve.tensor_scalar(probs(b)[:, x:y], probs(b)[:, x:y], einv[:, b, tt:tt + 1], None, ALU.mult)
                        link(ins)
                        for tt, x, y in ((0, 0, P), (1, P, SPAN)):
                            ins = dve.scalar_tensor_tensor(out=probs(a)[:, x:y], in0=probs(a)[:, x:y],
                                                           scalar=einv[:, a, tt:tt + 1], in1=probs(b)[:, x:y],
                                                           op0=ALU.mult, op1=ALU.subtract)
                        ins.then_inc(weighed, 1)

                def take_pv(i):
                    dve.wait_ge(pv_done, ITEMS * l + i + 1)
                    if i < N_DIFF:
                        dve.tensor_copy(mixed[:, :, i * P:(i + 1) * P],
                                        ps[:, 2 + i % 2, 0:2 * P].rearrange("p (t n) -> p t n", t=TT)).then_inc(pv_taken, 1)
                        return
                    f, m = i - N_DIFF, item_maps(i)[0]
                    for tt in range(TT):
                        ins = dve.tensor_scalar(mixed[:, tt, 2 * N_DIFF * HD + f * HD:2 * N_DIFF * HD + (f + 1) * HD],
                                                ps[:, 2 + i % 2, tt * HD:(tt + 1) * HD], einv[:, m, tt:tt + 1], None, ALU.mult)
                    ins.then_inc(pv_taken, 1)

                def norm_heads():
                    dve.wait_ge(sub_est, l + 1)
                    link(dve.tensor_scalar(sub[:, 1, :], sub[:, 0, :], 1.0 / P, SUB_EPS, ALU.mult, ALU.add))
                    refine(sub[:, 4, :], sub[:, 1, :], sub[:, 2, :], sub[:, 3, :])
                    for i in range(N_DIFF):
                        for tt in range(TT):
                            o = mixed[:, tt, i * P:(i + 1) * P]
                            ins = dve.scalar_tensor_tensor(out=o, in0=o, scalar=sub[:, 4, 2 * i + tt:2 * i + tt + 1],
                                                           in1=sub_g[:, l, :], op0=ALU.mult, op1=ALU.mult)
                    ins.then_inc(source_ready, 1)

                dve.wait_ge(pool_made, 5)
                dve.wait_ge(cq_done, l + 1)
                link(dve.tensor_copy(cq[:, :, :], ps[:, 4, 0:TT * N_FOX].rearrange("p (t n) -> p t n", t=TT)))
                for f in range(N_FOX):
                    dve.wait_ge(ck_done, N_FOX * l + f + 1)
                    c = ps[:, 2 + f % 2, 0:SEQ]
                    dve.scalar_tensor_tensor(out=decay[:, f, 0:P], in0=mask[:, 0:P], scalar=cq[:, 0, f:f + 1],
                                             in1=c[:, 0:P], op0=ALU.add, op1=ALU.subtract)
                    dve.scalar_tensor_tensor(out=decay[:, f, P:SPAN], in0=mask[:, P:SPAN], scalar=cq[:, 1, f:f + 1],
                                             in1=c, op0=ALU.add, op1=ALU.subtract).then_inc(ck_used, 1)
                splits(n0 + 17, n0 + 18)
                evict(7, kv[:, :, COLS:2 * COLS])
                nxt = n0 + 18
                for s in range(ITEMS + 2):
                    if s == 2:
                        evict(8, kv[:, :, 2 * COLS:3 * COLS])
                    if 1 <= s <= N_DIFF:
                        weigh(s - 1)
                    if s < ITEMS:
                        for m in item_maps(s):
                            mask_map(m)
                    if s < 5:
                        split(nxt)
                        nxt += 1
                    if s == 5:
                        evict(9, kv[:, :, 3 * COLS:4 * COLS])
                    if N_DIFF < s <= ITEMS:
                        weigh(s - 1)
                    if s >= 2:
                        take_pv(s - 2)
                    if s == N_DIFF + 4:
                        norm_heads()
                turn_lo(6 * l + 2, lambda k: 64)

                def add_chunk(c, unit):
                    dve.wait_ge(unit_used, unit + 1)
                    r = h[:, :, c * COLS:(c + 1) * COLS]
                    dve.tensor_tensor(r, r, acc(c % 2), ALU.add).then_inc(acc_free, 1)

                def half_turns(tn, columns, b, more):
                    splits(b + 3, b + 4)
                    add_chunk(0, b + 1)
                    splits(b + 4, b + 5)
                    turn_lo(tn, columns, range(4))
                    splits(b + 5, b + 6)
                    add_chunk(1, b + 3)
                    splits(b + 6, b + 7)
                    turn_lo(tn, columns, range(4, 8))
                    splits(b + 7, b + 7 + more)

                half_turns(6 * l + 3, lambda k: 16 + 8 * l + k, n0 + U_OUT, 1)
                norm(3 * l + 1)

                def evict_q(c):
                    dve.wait_ge(unit_used, n0 + U_MQ + 2 * c + 2)
                    for tt in range(TT):
                        ins = dve.tensor_scalar(mem_q[:, tt, c * COLS:(c + 1) * COLS], acc(c)[:, tt, :],
                                                root(3 * l + 1, tt), None, ALU.mult)
                    ins.then_inc(acc_free, 1)

                evict_q(0)
                splits(n0 + 28, n0 + 30)
                evict_q(1)
                splits(n0 + 30, n0 + 31)
                for s in range(MEM_HEADS + 2):
                    if s < MEM_HEADS:
                        dve.wait_ge(mscored, MEM_HEADS * l + s + 1)
                        link(dve.tensor_reduce(negmax[:, s, :], ps[:, 4 + s % 2, :].rearrange("p (t n) -> p t n", t=TT),
                                               AX.X, ALU.max))
                        dve.tensor_scalar(negmax[:, s, :], negmax[:, s, :], -1.0, None, ALU.mult).then_inc(mmax, 1)
                    if s >= 2:
                        i = s - 2
                        link(dve.reciprocal(einv[:, i, :], esum[:, i, :]))
                        dve.wait_ge(mpv_done, MEM_HEADS * l + i + 1)
                        for tt in range(TT):
                            ins = dve.tensor_scalar(mixed[:, tt, i * MEM_HD:(i + 1) * MEM_HD],
                                                    ps[:, 2 + i % 2, tt * SEQ:(tt + 1) * SEQ], einv[:, i, tt:tt + 1],
                                                    None, ALU.mult)
                        ins.then_inc(source_ready if i == MEM_HEADS - 1 else mpv_taken, 1)
                turn_lo(6 * l + 4, lambda k: 64)
                half_turns(6 * l + 5, lambda k: 48 + 8 * l + k, n0 + U_MO, 1 - l)
                norm(3 * l + 2)
                if l == 0:
                    dve.sem_inc(ffn_rooted, 1)
                    f0 = n0 + U_FFN

                    def gated_chunk(pair, used, want, wide=COLS):
                        dve.wait_ge(silu_done, want)
                        dve.wait_ge(unit_used, used)
                        for tt in range(TT):
                            ins = dve.scalar_tensor_tensor(out=gate[:, tt, 0:wide], in0=acc(pair)[:, tt, 0:wide],
                                                           scalar=root(2, tt), in1=gate[:, tt, 0:wide],
                                                           op0=ALU.mult, op1=ALU.mult)
                        ins.then_inc(gated, 1)

                    def keep_lo(pair, buf, want, blocks=4):
                        dve.wait_ge(ghi_kept, want)
                        dve.tensor_tensor(g_lo[:, buf, 0:blocks, :],
                                          acc(pair).rearrange("p c (b n) -> p (c b) n", n=SEQ)[:, 0:blocks, :],
                                          g_hi[:, buf, 0:blocks, :].bitcast(F32), ALU.subtract).then_inc(glo_kept, 1)

                    dve.wait_ge(lo_turned, KT * (6 * l + 6))
                    dve.memset(ps[:, 4:8, :], 0.0).then_inc(out_zeroed, 1)
                    splits(f0 + 4, f0 + 6)
                    gated_chunk(1, f0 + 4, 1)
                    keep_lo(0, 0, 1)
                    with dve.Fori(0, (FF_FULL - 1) // 2) as i:
                        for r in range(2):
                            b = f0 + 4 + 6 * r
                            for k in range(2, 6):
                                split(b + k, 12 * i)
                            gated_chunk(r % 2, 12 * i + (b + 4), 2 * i + (r + 2))
                            for k in range(6, 8):
                                split(b + k, 12 * i)
                            keep_lo((r + 1) % 2, (r + 1) % 2, 2 * i + (r + 2))
                    f1 = f0 + 4 + 6 * (FF_FULL - 1)
                    splits(f1 + 2, f1 + 4)
                    gated_chunk(0, f1 + 2, FF_FULL + 1, SEQ)
                    splits(f1 + 4, f1 + 5)
                    keep_lo(1, 1, FF_FULL + 1, 2)
                    dve.wait_ge(unit_used, L_UNITS)
                    for tt in range(TT):
                        r = h[:, tt, :].rearrange("p (c n) -> p c n", c=2)
                        ins = dve.tensor_tensor(r, r, ps[:, 4 + 2 * tt:6 + 2 * tt, :], ALU.add)
                    ins.then_inc(ffn_added, 1)
                    splits(L_UNITS, L_UNITS + 3)

            dve.wait_ge(logits_done, 1)
            lg, top, place, gap, ex = (route[:, :, i, :] for i in range(5))
            sel1, sel2, comb, posm, picks = (route[:, :, i, :] for i in range(5, 10))
            for tt in range(TT):
                ins = dve.tensor_scalar(lg[:, tt, 0:8], ps[:, 3, tt * N_EXP:(tt + 1) * N_EXP], root(5, tt), None, ALU.mult)
            link(ins)
            for tt in range(TT):
                ins = dve.max(top[:, tt, 0:8], lg[:, tt, 0:8])
            link(ins)
            for tt in range(TT):
                ins = dve.max_index(t_idx[:, tt, :], top[:, tt, 0:8], lg[:, tt, 0:8])
            link(ins)
            dve.tensor_tensor(gap[:, :, 0:1], top[:, :, 1:2], top[:, :, 0:1], ALU.subtract).then_inc(routed, 1)
            link(dve.tensor_copy(place[:, :, 0:8], t_idx[:, :, :]))
            for tt in range(TT):
                dve.tensor_scalar(sel1[:, tt, 0:8], eight[:, :], place[:, tt, 0:1], None, ALU.is_equal)
                ins = dve.tensor_scalar(sel2[:, tt, 0:8], eight[:, :], place[:, tt, 1:2], None, ALU.is_equal)
            link(ins)
            dve.tensor_tensor(picks[:, :, 0:8], sel1[:, :, 0:8], sel2[:, :, 0:8], ALU.add).then_inc(picked_sum, 1)
            dve.wait_ge(route_exp, 1)
            link(dve.tensor_scalar(gap[:, :, 1:2], ex[:, :, 0:1], 1.0, None, ALU.add))
            link(dve.reciprocal(gap[:, :, 2:3], gap[:, :, 1:2]))
            link(dve.tensor_tensor(gap[:, :, 3:4], gap[:, :, 2:3], ex[:, :, 0:1], ALU.mult))
            for tt in range(TT):
                ins = dve.tensor_scalar(sel2[:, tt, 0:8], sel2[:, tt, 0:8], gap[:, tt, 3:4], None, ALU.mult)
            link(ins)
            for tt in range(TT):
                ins = dve.scalar_tensor_tensor(out=comb[:, tt, 1:9], in0=sel1[:, tt, 0:8], scalar=gap[:, tt, 2:3],
                                               in1=sel2[:, tt, 0:8], op0=ALU.mult, op1=ALU.add)
            link(ins)
            dve.wait_ge(counted, 1)
            link(dve.tensor_tensor(posm[:, :, 0:8], ps[:, 2, 0:TT * N_EXP].rearrange("p (t n) -> p t n", t=TT),
                                   picks[:, :, 0:8], ALU.mult))
            link(dve.tensor_reduce(gap[:, 0, 4:5], ps[:, 2, TT * N_EXP:(TT + 1) * N_EXP], AX.X, ALU.max))
            link(dve.tensor_scalar(gap[:, 0, 5:6], gap[:, 0, 4:5], -float(P), 0.0, ALU.add, ALU.max))
            dve.tensor_copy(n_over[:, :], gap[:, 0, 5:6]).then_inc(over_ready, 1)
            dve.wait_ge(late_landed, 32)
            for tt in range(TT):
                ins = dve.scalar_tensor_tensor(out=hn[:, tt, :], in0=h[:, tt, :], scalar=root(5, tt),
                                               in1=ffn_g[:, :], op0=ALU.mult, op1=ALU.mult)
            ins.then_inc(hn_ready, 1)
            dve.memset(pick_t[:, :, :], 0.0).then_inc(comb_ready, 1)
            dve.memset(ps[:, 2:4, :], 0.0).then_inc(comb_ready, 1)

            def make_pick(e, q):
                for tt in range(TT):
                    ins = dve.tensor_scalar(pick[:, tt, :], slots[:, :], posm[:, tt, bass.ds(e, 1)], None, ALU.is_equal)
                ins.then_inc(pick_made, 1)

            def keep_xe(q):
                for g in range(2):
                    dve.wait_ge(xe_hi_kept, q * 2 + (g + 1))
                    dve.tensor_tensor(xe_lo[:, 4 * g:4 * g + 4, :], ps[:, 5 + g, :].rearrange("p (k n) -> p k n", k=4),
                                      xe_hi[:, 4 * g:4 * g + 4, :].bitcast(F32), ALU.subtract).then_inc(xe_lo_kept, 1)

            def accumulate(q, column):
                dve.wait_ge(scattered, q + 1)
                for n, bank in enumerate((5, 6, 7, 2)):
                    tt, c = n // 2, n % 2
                    r = h[:, tt, c * COLS:(c + 1) * COLS]
                    ins = dve.scalar_tensor_tensor(out=r, in0=ps[:, bank, :], scalar=comb[:, tt, bass.ds(column, 1)],
                                                   in1=r, op0=ALU.mult, op1=ALU.add)
                return ins

            def expert(e, q0, b0, ahead=0):
                q = e + q0
                more = E_UNITS * q
                for k in range(ahead, 6):
                    split(M0 + k, more)
                dve.wait_ge(e_silu, EXP_CH * q + 1)
                dve.wait_ge(unit_used, more + (M0 + 4))
                dve.tensor_tensor(gate[:, 0, :], ps[:, 1, :], gate[:, 0, :], ALU.mult).then_inc(e_gated, 1)
                accumulate(q + b0, e).then_inc(hn_gained, 1)
                dve.wait_ge(pick_turned, q + 1)
                make_pick(e + 1, q + 1)
                dve.wait_ge(pick_kept, q + 1)
                dve.wait_ge(hn_gained, q + b0 + 1)
                dve.memset(ps[:, 2:4, :], 0.0).then_inc(e_zeroed, 1)
                dve.wait_ge(e_hi, EXP_CH * q + 1)
                dve.tensor_tensor(g_lo[:, 0, :, 0:P], ps[:, 4, :].rearrange("p (b n) -> p b n", b=4),
                                  g_hi[:, 0, :, 0:P].bitcast(F32), ALU.subtract).then_inc(e_lo, 1)
                with dve.Fori(0, EXP_CH - 1) as j:
                    for k in range(6, 10):
                        split(M0 + k, more + 6 * j)
                    dve.wait_ge(e_silu, EXP_CH * q + j + 2)
                    dve.wait_ge(unit_used, more + 6 * j + (M0 + 8))
                    dve.tensor_tensor(gate[:, 0, :], ps[:, 1, :], gate[:, 0, :], ALU.mult).then_inc(e_gated, 1)
                    for k in range(10, 12):
                        split(M0 + k, more + 6 * j)
                    dve.wait_ge(e_hi, EXP_CH * q + j + 2)
                    dve.tensor_tensor(g_lo[:, 0, :, 0:P], ps[:, 4, :].rearrange("p (b n) -> p b n", b=4),
                                      g_hi[:, 0, :, 0:P].bitcast(F32), ALU.subtract).then_inc(e_lo, 1)
                keep_xe(q + b0 + 1)

            make_pick(0, 0)
            keep_xe(0)
            expert(0, 0, 0, ahead=3)
            with dve.Fori(1, N_EXP) as e:
                expert(e, 0, 0)
            link(accumulate(N_EXP, N_EXP))
            over = dve.value_load(n_over[0:1, 0:1], min_val=0, max_val=SEQ)
            with dve.If(over > 0):
                base = steps[0]
                link(dve.tensor_scalar(posm[:, :, 0:8], posm[:, :, 0:8], -float(P), None, ALU.add))
                dve.memset(pick_t[:, :, :], 0.0).then_inc(comb_ready, 1)
                dve.memset(ps[:, 2:4, :], 0.0).then_inc(comb_ready, 1)
                make_pick(0, N_EXP)
                keep_xe(N_EXP + 1)
                with dve.Fori(0, N_EXP) as e:
                    expert(e, N_EXP, 1)
                link(accumulate(2 * N_EXP + 1, N_EXP))
                steps[0] = base
            dve.sem_inc(summed, 1)

            dve.wait_ge(rs_est, 7)
            final = [0]

            def flink(ins):
                final[0] += 1
                ins.then_inc(final_step, 1)
                dve.wait_ge(final_step, final[0])

            last = stat[:, N_FINAL, :]
            flink(dve.tensor_scalar(last[:, 2:4], last[:, 0:2], 1.0 / D, EPS, ALU.mult, ALU.add))
            flink(dve.tensor_tensor(newton[:, :], last[:, 4:6], last[:, 4:6], ALU.mult))
            flink(dve.tensor_tensor(newton[:, :], newton[:, :], last[:, 2:4], ALU.mult))
            flink(dve.tensor_scalar(newton[:, :], newton[:, :], -0.5, 1.5, ALU.mult, ALU.add))
            flink(dve.tensor_tensor(last[:, 6:8], last[:, 4:6], newton[:, :], ALU.mult))
            for tt in range(TT):
                dve.scalar_tensor_tensor(out=result[:, tt, :], in0=h[:, tt, :], scalar=root(N_FINAL, tt),
                                         in1=fin_g[:, :], op0=ALU.mult, op1=ALU.mult).then_inc(result_ready, 1)

        @block.tensor
        def _(pe):
            def mm3(o, xh, xl, wh, wl, first, last, **kw):
                pe.matmul(o, xh, wh, start=first, stop=False, **kw)
                pe.matmul(o, xh, wl, start=False, stop=False, **kw)
                return pe.matmul(o, xl, wh, start=False, stop=last, **kw)

            def turn(tn, groups=range(4)):
                l, which = tn // 6, tn % 6
                src = (h, hn, mixed, h, mixed, h)[which]
                if which in (1, 2):
                    pe.wait_ge(source_ready, 3 * l + which)
                elif tn == 0:
                    pe.wait_ge(x_landed, 16)
                elif which == 0:
                    pe.wait_ge(ffn_added, 1)
                for g in groups:
                    if which in (3, 5) and g % 2 == 0:
                        pe.wait_ge(acc_free, 16 * l + (11 if which == 3 else 15) + g // 2)
                    if which == 2 and g >= 2:
                        pe.wait_ge(pv_taken, ITEMS * l + N_DIFF + 4 * (g - 1))
                    if which == 4 and g < 3:
                        pe.wait_ge(mpv_taken, (MEM_HEADS - 1) * l + g + 1)
                    if which == 4 and g == 3:
                        pe.wait_ge(source_ready, 3 * l + 3)
                    if g >= 2:
                        pe.wait_ge(lo_turned, KT * tn + 2 * (g - 2) + 2)
                    for k in (2 * g, 2 * g + 1):
                        for tt in range(TT):
                            c = (k % 2) * SEQ + tt * P
                            ins = pe.transpose(ps[:, 6 + g % 2, c:c + P], src[:, tt, k * P:(k + 1) * P], ident[:, :])
                    ins.then_inc(turned, 1)

            def unit(n, half, pair, tn=None, more=0):
                pe.wait_ge(lo_split, more + (n + 1))
                wh, wl = slot4(w_hi, n, SPLIT), slot4(w_lo, n, SPLIT)
                for k in range(4):
                    kt = 4 * half + k
                    if tn is not None:
                        pe.wait_ge(lo_turned, KT * tn + kt + 1)
                    for tt in range(TT):
                        ins = mm3(acc(pair)[:, tt, :], x_hi[:, kt, tt * P:(tt + 1) * P], x_lo[:, kt, tt * P:(tt + 1) * P],
                                  wh[:, k, :], wl[:, k, :], kt == 0, kt == KT - 1)
                ins.then_inc(unit_used, 1)

            def narrow(which, bank):
                wh = s_hi[:, which, :].rearrange("p (k n) -> p k n", n=8)
                wl = s_lo[:, which, :].rearrange("p (k n) -> p k n", n=8)
                for tt in range(TT):
                    for kt in range(KT):
                        ins = mm3(ps[:, bank, tt * 8:(tt + 1) * 8], x_hi[:, kt, tt * P:(tt + 1) * P],
                                  x_lo[:, kt, tt * P:(tt + 1) * P], wh[:, kt, :], wl[:, kt, :], kt == 0, kt == KT - 1)
                return ins

            def sums(bank, x):
                pe.matmul(ps[:, bank, 0:8], tri[:, 0:P], x[:, 0], start=True, stop=True)
                pe.matmul(ps[:, bank, 8:16], tri[:, P:SEQ], x[:, 0], start=True, stop=False)
                return pe.matmul(ps[:, bank, 8:16], tri[:, 0:P], x[:, 1], start=False, stop=True)

            pe.wait_ge(ident_made, 1)
            pe.wait_ge(gains_landed, 16 * 4)
            pe.transpose(ps[:, 0, 0:64], gain_rows, ident[0:64, 0:64]).then_inc(gains_turned, 1)

            for l in range(LAYERS):
                n0 = l * L_UNITS
                a0 = 16 * l
                turn(6 * l)
                if l == 0:
                    pe.wait_ge(gains_kept, 1)
                pe.wait_ge(lo_turned, KT * (6 * l + 1))
                with pe.Fori(0, 2) as i:
                    for c in range(3):
                        for u in range(2):
                            unit(n0 + 2 * c + u, u, c, more=6 * i)
                if l == 0:
                    pe.wait_ge(small_split, 1)
                narrow(l, 7).then_inc(fl_done, 1)
                pe.wait_ge(fl_neg, l + 1)
                turn(6 * l + 1)
                pe.wait_ge(acc_free, a0 + 4)
                unit(n0 + 12, 0, 0, tn=6 * l + 1)
                unit(n0 + 13, 1, 0, tn=6 * l + 1)

                def turn_qk(g):
                    if g >= 2:
                        pe.wait_ge(qk_kept, 8 * l + g - 1)
                    for b in range(2):
                        blk = 2 * g + b if g < 4 else C_QF // P + 2 * (g - 4) + b
                        for tt in range(TT):
                            ins = pe.transpose(ps[:, 6 + g % 2, b * SEQ + tt * P:b * SEQ + (tt + 1) * P],
                                               proj[:, tt, blk * P:(blk + 1) * P], ident[:, :])
                    ins.then_inc(qk_turned, 1)

                pe.wait_ge(roped, l + 1)
                for g in range(4):
                    turn_qk(g)
                pe.wait_ge(acc_free, a0 + 7)
                unit(n0 + 14, 0, 0)
                for g in range(4, 8):
                    turn_qk(g)
                pe.wait_ge(logf_ready, l + 1)
                pe.wait_ge(pool_made, 5)
                pe.wait_ge(acc_free, a0 + 6)
                sums(4, fl[:, 1]).then_inc(cq_done, 1)
                for f in range(N_FOX):
                    if f >= 2:
                        pe.wait_ge(ck_used, N_FOX * l + f - 1)
                    o = ps[:, 2 + f % 2, 0:SEQ]
                    f0, f1 = (fl[:, 1, tt, f:f + 1].to_broadcast([P, P]) for tt in range(TT))
                    pe.matmul(o, f0, tri[:, :], start=True, stop=False)
                    pe.matmul(o[:, P:SEQ], f1, tri[:, 0:P], start=False, stop=True).then_inc(ck_done, 1)
                unit(n0 + 15, 1, 0)

                def scores(i):
                    for m in item_maps(i):
                        if m >= 2:
                            pe.wait_ge(masked, MAPS * l + m - 1)
                        elif m == 0:
                            pe.wait_ge(ck_used, N_FOX * (l + 1))
                        bq, bk, p0 = map_blocks(m)
                        q, k = qkt[p0:p0 + HD, bq, :], qkt[p0:p0 + HD, bk, :]
                        pe.matmul(ps[:, 4 + m % 2, 0:P], q[:, 0:P], k[:, 0:P], start=True, stop=True)
                        pe.matmul(ps[:, 4 + m % 2, P:SPAN], q[:, P:SEQ], k, start=True, stop=True).then_inc(scored, 1)

                def turn_p(i):
                    if i < N_DIFF:
                        pe.wait_ge(weighed, N_DIFF * l + i + 1)
                    else:
                        pe.wait_ge(expd, MAPS * l + item_maps(i)[0] + 1)
                    if i >= 2:
                        pe.wait_ge(p_kept, ITEMS * l + i - 1)
                    for b in range(3):
                        ins = pe.transpose(ps[:, 6 + i % 2, b * P:(b + 1) * P],
                                           probs(item_maps(i)[0])[:, b * P:(b + 1) * P], ident[:, :])
                    ins.then_inc(p_turned, 1)

                def pv(i):
                    pe.wait_ge(p_kept, ITEMS * l + i + 1)
                    if i >= 2:
                        pe.wait_ge(pv_taken, ITEMS * l + i - 1)
                    wide = P if i < N_DIFF else HD
                    c = C_VD + i * P if i < N_DIFF else C_VF + (i - N_DIFF) * HD
                    o, p = ps[:, 2 + i % 2, :], probs_t(i)
                    pe.matmul(o[:, 0:wide], p[:, 0:P], proj[:, 0, c:c + wide], start=True, stop=True)
                    pe.matmul(o[:, wide:2 * wide], p[:, P:2 * P], proj[:, 0, c:c + wide], start=True, stop=False)
                    pe.matmul(o[:, wide:2 * wide], p[:, 2 * P:SPAN], proj[:, 1, c:c + wide], start=False,
                              stop=True).then_inc(pv_done, 1)

                pe.wait_ge(qk_kept, 8 * (l + 1))
                nxt = n0 + 16
                for s in range(ITEMS + 2):
                    if s < ITEMS:
                        scores(s)
                    if s < 4:
                        if nxt % 2 == n0 % 2:
                            pe.wait_ge(acc_free, a0 + (nxt - n0) // 2)
                        unit(nxt, (nxt - n0) % 2, 0)
                        nxt += 1
                    if 1 <= s <= ITEMS:
                        turn_p(s - 1)
                    if s >= 2:
                        pv(s - 2)

                def half_turns(tn, b, after=True):
                    unit(b, 0, 0, tn=tn - 1)
                    unit(b + 1, 1, 0, tn=tn - 1)
                    unit(b + 2, 0, 1)
                    turn(tn, (0, 1))
                    unit(b + 3, 1, 1)
                    if after:
                        unit(b + 4, 0, 0, tn=tn)
                    turn(tn, (2, 3))
                    if after:
                        unit(b + 5, 1, 0, tn=tn)

                turn(6 * l + 2)
                pe.wait_ge(acc_free, a0 + 10)
                half_turns(6 * l + 3, n0 + U_OUT)
                unit(n0 + U_MQ + 2, 0, 1)
                unit(n0 + U_MQ + 3, 1, 1)

                for g in range(8):
                    if g >= 2:
                        pe.wait_ge(mqk_kept, 8 * l + g - 1)
                    if g == 4:
                        pe.wait_ge(acc_free, a0 + 14)
                    src = kv if g < 4 else mem_q
                    for b in range(2):
                        blk = 2 * (g % 4) + b
                        for tt in range(TT):
                            ins = pe.transpose(ps[:, 6 + g % 2, b * SEQ + tt * P:b * SEQ + (tt + 1) * P],
                                               src[:, tt, blk * P:(blk + 1) * P], ident[:, :])
                    ins.then_inc(mqk_turned, 1)
                pe.wait_ge(mqk_kept, 8 * (l + 1))
                for s in range(MEM_HEADS + 2):
                    if s < MEM_HEADS:
                        if s >= 2:
                            pe.wait_ge(mexpd, MEM_HEADS * l + s - 1)
                        for tt in range(TT):
                            for b in range(2):
                                ins = pe.matmul(ps[:, 4 + s % 2, tt * SEQ:(tt + 1) * SEQ],
                                                qkt[:, 8 + 2 * s + b, tt * P:(tt + 1) * P], qkt[:, 2 * s + b, :],
                                                start=b == 0, stop=b == 1)
                        ins.then_inc(mscored, 1)
                    if 1 <= s <= MEM_HEADS:
                        i = s - 1
                        pe.wait_ge(mexpd, MEM_HEADS * l + i + 1)
                        if i >= 2:
                            pe.wait_ge(mp_kept, MEM_HEADS * l + i - 1)
                        for tt in range(TT):
                            for b in range(2):
                                c = (2 * tt + b) * P
                                ins = pe.transpose(ps[:, 6 + i % 2, c:c + P], mem_p(i)[:, tt, b * P:(b + 1) * P], ident[:, :])
                        ins.then_inc(mp_turned, 1)
                    if s >= 2:
                        i = s - 2
                        pe.wait_ge(mp_kept, MEM_HEADS * l + i + 1)
                        if i >= 2:
                            pe.wait_ge(mpv_taken, (MEM_HEADS - 1) * l + i - 1)
                        for tt in range(TT):
                            for b in range(2):
                                c = (2 * tt + b) * P
                                ins = pe.matmul(ps[:, 2 + i % 2, tt * SEQ:(tt + 1) * SEQ], mem_pt(i)[:, c:c + P],
                                                kv[:, b, D + i * MEM_HD:D + (i + 1) * MEM_HD], start=b == 0, stop=b == 1)
                        ins.then_inc(mpv_done, 1)
                turn(6 * l + 4)
                half_turns(6 * l + 5, n0 + U_MO, after=l == 0)
                if l == 0:
                    f0 = n0 + U_FFN

                    def turn_g(pair, want, blocks=4):
                        pe.wait_ge(gated, want)
                        for b in range(blocks):
                            for tt in range(TT):
                                o = acc(pair)[:, b // 2, (b % 2) * SEQ + tt * P:(b % 2) * SEQ + (tt + 1) * P]
                                ins = pe.transpose(o, gate[:, tt, b * P:(b + 1) * P], ident[:, :])
                        ins.then_inc(g_turned, 1)

                    def down(n, half, buf, more=0):
                        pe.wait_ge(lo_split, more + (n + 1))
                        wh, wl = slot2(w_hi, n, SPLIT), slot2(w_lo, n, SPLIT)
                        for k in range(2):
                            for tt in range(TT):
                                for c in range(2):
                                    b = 2 * half + k
                                    ins = mm3(ps[:, 4 + 2 * tt + c, :], g_hi[:, buf, b, tt * P:(tt + 1) * P],
                                              g_lo[:, buf, b, tt * P:(tt + 1) * P], wh[:, k, c * COLS:(c + 1) * COLS],
                                              wl[:, k, c * COLS:(c + 1) * COLS], False, False, skip_group_check=True)
                        ins.then_inc(unit_used, 1)

                    unit(f0 + 2, 0, 1)
                    unit(f0 + 3, 1, 1)
                    turn_g(0, 1)
                    pe.wait_ge(out_zeroed, 1)
                    with pe.Fori(0, (FF_FULL - 1) // 2) as i:
                        for r in range(2):
                            b = f0 + 4 + 6 * r
                            for k in range(2):
                                unit(b + k, k % 2, (r + 1) % 2, more=12 * i)
                            pe.wait_ge(glo_kept, 2 * i + (r + 1))
                            for k in range(2, 4):
                                unit(b + k, k % 2, r % 2, more=12 * i)
                            for k in range(2):
                                down(b + 4 + k, k, r % 2, more=12 * i)
                            turn_g((r + 1) % 2, 2 * i + (r + 2))
                    f1 = f0 + 4 + 6 * (FF_FULL - 1)
                    for k in range(2):
                        if k == 1:
                            pe.wait_ge(glo_kept, FF_FULL)
                        pe.wait_ge(lo_split, f1 + k + 1)
                        wh, wl = slot8(w_hi, f1 + k, SPLIT), slot8(w_lo, f1 + k, SPLIT)
                        for kt in range(KT):
                            for tt in range(TT):
                                ins = mm3(acc(1 - k)[:, tt, 0:SEQ], x_hi[:, kt, tt * P:(tt + 1) * P],
                                          x_lo[:, kt, tt * P:(tt + 1) * P], wh[:, kt, :], wl[:, kt, :], kt == 0, kt == KT - 1)
                        ins.then_inc(unit_used, 1)
                    down(f1 + 2, 0, 0)
                    down(f1 + 3, 1, 0)
                    turn_g(1, FF_FULL + 1, 2)
                    pe.wait_ge(glo_kept, FF_FULL + 1)
                    down(f1 + 4, 0, 1)

            pe.wait_ge(lo_turned, KT * 12)
            pe.wait_ge(acc_free, 32)
            narrow(2, 3).then_inc(logits_done, 1)
            pe.wait_ge(picked_sum, 1)
            sums(2, route[:, :, 9, 0:8])
            for tt in range(TT):
                ins = pe.matmul(ps[:, 2, 16:24], tri[:, P:SEQ], route[:, tt, 9, 0:8], start=tt == 0, stop=tt == 1)
            ins.then_inc(counted, 1)

            def gather(q):
                pe.wait_ge(pick_made, q + 1)
                for g in range(2):
                    for k in range(4):
                        for tt in range(TT):
                            c = (4 * g + k) * P
                            ins = pe.matmul(ps[:, 5 + g, k * P:(k + 1) * P], hn[:, tt, c:c + P], pick[:, tt, :],
                                            start=tt == 0, stop=tt == 1)
                    ins.then_inc(gathered, 1)

            def scatter(q):
                pe.wait_ge(ye_kept, q + 1)
                for n, bank in enumerate((5, 6, 7, 2)):
                    tt, c = n // 2, n % 2
                    ins = pe.matmul(ps[:, bank, :], pick_t[:, tt, :], ye[:, c * COLS:(c + 1) * COLS], start=True, stop=True)
                ins.then_inc(scattered, 1)

            def up(n, half, bank, more):
                pe.wait_ge(lo_split, more + (n + 1))
                wh, wl = slot4(w_hi, n, SPLIT), slot4(w_lo, n, SPLIT)
                for k in range(4):
                    kt = 4 * half + k
                    ins = mm3(ps[:, bank, :], xe_hi[:, kt, :], xe_lo[:, kt, :], wh[:, k, :], wl[:, k, :], kt == 0, kt == KT - 1)
                ins.then_inc(unit_used, 1)

            def down1(n, half, more):
                pe.wait_ge(lo_split, more + (n + 1))
                wh, wl = slot2(w_hi, n, SPLIT), slot2(w_lo, n, SPLIT)
                for k in range(2):
                    for c in range(2):
                        b = 2 * half + k
                        ins = mm3(ps[:, 2 + c, :], g_hi[:, 0, b, 0:P], g_lo[:, 0, b, 0:P], wh[:, k, c * COLS:(c + 1) * COLS],
                                  wl[:, k, c * COLS:(c + 1) * COLS], False, False, skip_group_check=True)
                ins.then_inc(unit_used, 1)

            def turn_e(want):
                pe.wait_ge(e_gated, want)
                for b in range(4):
                    ins = pe.transpose(ps[:, 4, b * P:(b + 1) * P], gate[:, 0, b * P:(b + 1) * P], ident[:, :])
                ins.then_inc(e_turned, 1)

            def experts(q0):
                b0 = q0 // N_EXP
                pe.wait_ge(comb_ready, 2 + 2 * b0)
                pe.wait_ge(hn_ready, 1)
                gather(q0 + b0)
                pe.transpose(ps[:, 7, 0:P], ident[:, :], ident[:, :]).then_inc(ye_done, 1)
                with pe.Fori(0, N_EXP) as e:
                    q = e + q0
                    more = E_UNITS * q
                    pe.wait_ge(xe_lo_kept, 2 * (q + b0) + 2)
                    for k in range(4):
                        up(M0 + k, k % 2, k // 2, more)
                    scatter(q + b0)
                    for tt in range(TT):
                        ins = pe.transpose(ps[:, 3, tt * P:(tt + 1) * P], pick[:, tt, :], ident[:, :])
                    ins.then_inc(pick_turned, 1)
                    turn_e(EXP_CH * q + 1)
                    with pe.Fori(0, EXP_CH - 1) as j:
                        for k in range(4):
                            up(M0 + 4 + k, k % 2, k // 2, more + 6 * j)
                        pe.wait_ge(e_lo, EXP_CH * q + j + 1)
                        pe.wait_ge(e_zeroed, q + 1)
                        for k in range(2):
                            down1(M0 + 8 + k, k, more + 6 * j)
                        turn_e(EXP_CH * q + j + 2)
                    gather(q + b0 + 1)
                    pe.wait_ge(e_lo, EXP_CH * q + EXP_CH)
                    down1(M0 + 6 * EXP_CH - 2, 0, more)
                    down1(M0 + 6 * EXP_CH - 1, 1, more)
                    pe.transpose(ps[:, 7, 0:P], ident[:, :], ident[:, :]).then_inc(ye_done, 1)
                pe.wait_ge(xe_lo_kept, 2 * (q0 + N_EXP + b0) + 2)
                scatter(q0 + N_EXP + b0)

            experts(0)
            pe.wait_ge(over_ready, 1)
            over = pe.value_load(n_over[0:1, 0:1], min_val=0, max_val=SEQ)
            with pe.If(over > 0):
                experts(N_EXP)


def lam_init(l):
    return 0.8 - 0.6 * math.exp(-0.3 * l)


NAMES = ["x", "mem", "positions", "norm_mix_g", "w_in", "lam_q1", "lam_k1", "lam_q2", "lam_k2", "diff_subln_g",
         "fox_bias", "w_out", "norm_mem_g", "mem_norm_g", "w_mq", "w_mkv", "w_mo", "norm_ffn_g", "w_ff1", "w_ff3",
         "w_ff2", "w_router", "w_e1", "w_e3", "w_e2", "final_norm_g"]


def kernel(**inputs):
    import concourse.bacc as bacc
    from concourse.bass_utils import run_bass_kernel_spmd

    nc = bacc.Bacc("TRN2", target_bir_lowering=False, num_devices=1)
    arrays, aps = {}, {}
    for name in NAMES:
        a = np.ascontiguousarray(inputs[name])
        arrays[name] = a
        aps[name] = nc.dram_tensor(name, a.shape, mybir.dt.from_np(a.dtype), kind="ExternalInput").ap()
    out = nc.dram_tensor("out", (1, SEQ, D), F32, kind="ExternalOutput").ap()
    trunk(nc, aps, out)
    r = run_bass_kernel_spmd(nc, [arrays], core_ids=[0])
    return r.results[0]["out"]
```

```python
from contextlib import ExitStack
import math

import numpy as np

import concourse.bass as bass
from concourse import mybir
from concourse.alu_op_type import AluOpType as ALU

F32 = mybir.dt.float32
F32R = mybir.dt.float32r
BF16 = mybir.dt.bfloat16
I32 = mybir.dt.int32
U32 = mybir.dt.uint32
ACT = mybir.ActivationFunctionType
AX = mybir.AxisListType

P = 128
SEQ, D = 256, 1024
TT = SEQ // P
KT = D // P
LAYERS = 2
HD = 64
N_DIFF, N_FOX = 4, 8
D_MAPS = 4 * N_DIFF * HD
C_VD = D_MAPS
C_QF = C_VD + 2 * N_DIFF * HD
C_KF = C_QF + N_FOX * HD
C_VF = C_KF + N_FOX * HD
C_FL = C_VF + N_FOX * HD
D_IN = C_FL + N_FOX
ROPE_HALF = HD // 8
MEM_HEADS, MEM_HD = 4, 256
D_FF, D_EXP, N_EXP = 2816, 3584, 8
EPS, SUB_EPS = 1e-6, 1e-5
NEG = -1e30

COLS = 512
UNIT = 2048
RAW, SPLIT = 6, 3
U_IN, U_MKV, U_OUT, U_MQ, U_MO, U_FFN = 0, 12, 20, 24, 28, 32
FF_FULL = D_FF // COLS
U_DENSE = 6 * FF_FULL + 3
L_UNITS = U_FFN + U_DENSE
EXP_CH = D_EXP // COLS
E_UNITS = 6 * EXP_CH
M0 = L_UNITS + U_FFN
ITEMS = N_DIFF + N_FOX
MAPS = 2 * N_DIFF + N_FOX
KV_STEPS = (0, 1, 2, 3, 7)
SPLIT_STEPS = (0, 1, 2, 3)
N_FINAL, N_MEM = 3 * LAYERS, 3 * LAYERS + 1
SPAN = P + SEQ

TWO_PI = 2.0 * math.pi
PI_HI = 6.28125
PI_MID = float(np.float32(round((TWO_PI - PI_HI) * 2**20) / 2**20))
PI_LO = TWO_PI - PI_HI - PI_MID
ROUND = 1.5 * 2.0**23
SIN_MAX = 3.1415925


def item_maps(i):
    return [2 * i, 2 * i + 1] if i < N_DIFF else [N_DIFF + i]


def map_item(m):
    return m // 2 if m < 2 * N_DIFF else m - N_DIFF


def map_blocks(m):
    if m < 2 * N_DIFF:
        h, which = m // 2, m % 2
        return 2 * which + h // 2, 4 + 2 * which + h // 2, HD * (h % 2)
    h = m - 2 * N_DIFF
    return 8 + h // 2, 12 + h // 2, HD * (h % 2)


def trunk(nc, t, out):
    ctx = ExitStack()
    with ctx:
        def sb(name, shape, dt=F32, stack=ctx):
            return stack.enter_context(nc.sbuf_tensor(name, shape, dt))

        def sem(name):
            return ctx.enter_context(nc.semaphore(name))

        raw = sb("raw", [P, RAW, UNIT])
        w_hi = sb("w_hi", [P, SPLIT, UNIT], F32R)
        w_lo = sb("w_lo", [P, SPLIT, UNIT], F32R)
        h = sb("h", [P, TT, D])
        hn = sb("hn", [P, TT, D])
        x_hi = sb("x_hi", [P, KT, SEQ], F32R)
        x_lo = sb("x_lo", [P, KT, SEQ], F32R)
        junk = sb("junk", [P, D], BF16)
        gain = sb("gain", [P, 65])
        ident = sb("ident", [P, P])
        tri = sb("tri", [P, SEQ])
        mask = sb("mask", [P, SPAN])
        slots = sb("slots", [P, P])
        eight = sb("eight", [P, N_EXP])
        sub_g = sb("sub_g", [P, LAYERS, P])
        fox_b = sb("fox_b", [P, LAYERS * N_FOX])
        eps_c = sb("eps_c", [P, 2])
        pos_i = sb("pos_i", [P, TT], I32)
        cs = sb("cs", [P, 2, TT, ROPE_HALF])
        small = sb("small", [P, 3, KT * 8])
        s_hi = sb("s_hi", [P, 3, KT * 8], F32R)
        s_lo = sb("s_lo", [P, 3, KT * 8], F32R)
        stat = sb("stat", [P, 8, 8])
        sub = sb("sub", [P, 5, 8])
        newton = sb("newton", [P, 2])
        spare = sb("spare", [P, 1])
        lam = sb("lam", [P, 8])
        negmax = sb("negmax", [P, MAPS, TT])
        esum = sb("esum", [P, MAPS, TT])
        einv = sb("einv", [P, MAPS, TT])
        fl = sb("fl", [P, 4, TT, N_FOX])
        cq = sb("cq", [P, TT, N_FOX])
        route = sb("route", [P, TT, 12, N_EXP + 2])
        t_idx = sb("t_idx", [P, TT, 8], U32)
        n_over = sb("n_over", [P, 1], I32)
        attn = ExitStack()
        proj = sb("proj", [P, TT, D_IN - N_FOX], stack=attn)
        kv = sb("kv", [P, TT, 2 * D], stack=attn)
        qkt = sb("qkt", [P, 16, SEQ], stack=attn)
        decay = sb("decay", [P, N_FOX, SPAN], stack=attn)
        attn.close()
        ffn = ExitStack()
        gate = sb("gate", [P, TT, COLS], stack=ffn)
        g_hi = sb("g_hi", [P, 2, 4, SEQ], F32R, stack=ffn)
        g_lo = sb("g_lo", [P, 2, 4, SEQ], F32R, stack=ffn)
        xe_hi = sb("xe_hi", [P, KT, P], F32R, stack=ffn)
        xe_lo = sb("xe_lo", [P, KT, P], F32R, stack=ffn)
        ye = sb("ye", [P, D], stack=ffn)
        pick = sb("pick", [P, TT, P], stack=ffn)
        pick_t = sb("pick_t", [P, TT, P], stack=ffn)
        ffn_g = sb("ffn_g", [P, D], stack=ffn)
        fin_g = sb("fin_g", [P, D], stack=ffn)
        result = sb("result", [P, TT, D], stack=ffn)
        ffn.close()

        mixed = proj[:, :, 0:D]
        mem_q = proj[:, :, D:2 * D]
        rows = (qkt[0:8, 0, 0:SEQ], qkt[0:8, 0, 0:SEQ], ye[0:8, 0:SEQ])
        gain_rows = hn[0:64, 0, 0:P]
        ang = hn[:, 1, 0:256].rearrange("p (s k t i) -> p s k t i", s=8, k=2, t=TT)
        inv_f = hn[:, 1, 512:512 + ROPE_HALF]
        lam_v = kv[:, 0, D:D + 4 * LAYERS * HD].rearrange("p (v n) -> p v n", v=4)
        pos_f = hn[:, 1, 544:544 + TT]

        def probs(m):
            return proj[:, (m % 4) // 2, C_QF + (m % 2) * SPAN:C_QF + (m % 2 + 1) * SPAN]

        def probs_t(i):
            return hn[:, i % 2, 0:SPAN]

        def mem_p(i):
            return decay[:, 2 * (i % 2):2 * (i % 2) + 2, 0:SEQ]

        def mem_pt(i):
            return hn[:, i % 2, 0:2 * SEQ]

        ps = ctx.enter_context(nc.psum_tensor("ps", [P, 8, COLS], F32))

        def turn_bank(tn, g):
            if tn == 6:
                return (6, 4, 7, 5)[g]
            return (6, 7, 4, 5)[g] if tn % 6 in (1, 2, 4) else 6 + g % 2

        def acc(pair):
            return ps[:, 2 * pair:2 * pair + 2, :]

        raw_landed = [sem(f"raw_landed{i}") for i in range(RAW)]
        hi_split, lo_split, unit_used = sem("hi_split"), sem("lo_split"), sem("unit_used")
        x_landed, mem_landed, mem_again, out_landed = (
            sem("x_landed"), sem("mem_landed"), sem("mem_again"), sem("out_landed"))
        const_landed, late_landed = sem("const_landed"), sem("late_landed")
        pool_made, final_step = sem("pool_made"), sem("final_step")
        gains_turned, gains_kept = sem("gains_turned"), sem("gains_kept")
        ang_ready, sin_ready = sem("ang_ready"), sem("sin_ready")
        dots_ready, lam_exp, small_split = sem("dots_ready"), sem("lam_exp"), sem("small_split")
        rs_est, source_ready, ffn_added = sem("rs_est"), sem("source_ready"), sem("ffn_added")
        ident_made, gains_landed, pos_landed = sem("ident_made"), sem("gains_landed"), sem("pos_landed")
        rows_done, rows_kept, ffn_summed = sem("rows_done"), sem("rows_kept"), sem("ffn_summed")
        first_squared = sem("first_squared")
        squared = sem("squared")
        ffn_rooted, hn_ready, result_ready = sem("ffn_rooted"), sem("hn_ready"), sem("result_ready")
        mem_est = sem("mem_est")
        turned, hi_turned, lo_turned = sem("turned"), sem("hi_turned"), sem("lo_turned")
        acc_free = sem("acc_free")
        dve_step, act_step, pool_step = sem("dve_step"), sem("act_step"), sem("pool_step")
        fl_done, fl_neg, fl_ln, logf_ready = sem("fl_done"), sem("fl_neg"), sem("fl_ln"), sem("logf_ready")
        roped, qk_turned, qk_kept = sem("roped"), sem("qk_turned"), sem("qk_kept")
        cq_done, ck_done, ck_used = sem("cq_done"), sem("ck_done"), sem("ck_used")
        scored, masked, expd, weighed = sem("scored"), sem("masked"), sem("expd"), sem("weighed")
        p_turned, p_kept, pv_done, pv_taken = sem("p_turned"), sem("p_kept"), sem("pv_done"), sem("pv_taken")
        sub_est = sem("sub_est")
        mqk_turned, mqk_kept = sem("mqk_turned"), sem("mqk_kept")
        mscored, mmax, mexpd = sem("mscored"), sem("mmax"), sem("mexpd")
        mp_turned, mp_kept, mpv_done, mpv_taken = sem("mp_turned"), sem("mp_kept"), sem("mpv_done"), sem("mpv_taken")
        silu_done, gated, g_turned = sem("silu_done"), sem("gated"), sem("g_turned")
        ghi_kept, glo_kept, out_zeroed = sem("ghi_kept"), sem("glo_kept"), sem("out_zeroed")
        routed, route_exp, picked_sum, counted = sem("routed"), sem("route_exp"), sem("picked_sum"), sem("counted")
        logits_done, comb_ready, over_ready = sem("logits_done"), sem("comb_ready"), sem("over_ready")
        e_silu, e_gated, e_turned = sem("e_silu"), sem("e_gated"), sem("e_turned")
        e_hi, e_lo, e_zeroed = sem("e_hi"), sem("e_lo"), sem("e_zeroed")
        pick_made, gathered, xe_hi_kept, xe_lo_kept = sem("pick_made"), sem("gathered"), sem("xe_hi_kept"), sem("xe_lo_kept")
        ye_done, ye_kept, scattered, pick_turned, pick_kept = (
            sem("ye_done"), sem("ye_kept"), sem("scattered"), sem("pick_turned"), sem("pick_kept"))
        summed, h_added = sem("summed"), sem("h_added")

        def halves(w):
            return w.rearrange("(u k p) n -> u p k n", k=4, p=P)

        w_in = [halves(t["w_in"][l]) for l in range(LAYERS)]
        w_out = [halves(t["w_out"][l]) for l in range(LAYERS)]
        w_mq = [halves(t["w_mq"][l]) for l in range(LAYERS)]
        w_mkv = [halves(t["w_mkv"][l]) for l in range(LAYERS)]
        w_mo = [halves(t["w_mo"][l]) for l in range(LAYERS)]
        ff1, ff3 = halves(t["w_ff1"][0]), halves(t["w_ff3"][0])
        ff2 = t["w_ff2"][0].rearrange("(u k p) n -> u p k n", k=2, p=P)
        e1 = t["w_e1"].rearrange("a e (u k p) f -> (a e u) p k f", k=4, p=P)
        e3 = t["w_e3"].rearrange("a e (u k p) f -> (a e u) p k f", k=4, p=P)
        e2 = t["w_e2"].rearrange("a e (u k p) n -> (a e u) p k n", k=2, p=P)

        def slot4(buf, n, size):
            return buf[:, n % size, :].rearrange("p (k n) -> p k n", k=4)

        def slot2(buf, n, size):
            return buf[:, n % size, :].rearrange("p (k n) -> p k n", k=2)

        def slot8(buf, n, size):
            return buf[:, n % size, :].rearrange("p (k n) -> p k n", k=8)

        block = ctx.enter_context(nc.Block())

        @block.sync
        def _(sp):
            def load(n, src, view=slot4, more=0):
                if n >= RAW:
                    sp.wait_ge(lo_split, more + (n - RAW + 1))
                sp.dma_start(view(raw, n, RAW), src).then_inc(raw_landed[n % RAW], 16)

            def small_loads():
                for i, v in enumerate(("lam_q1", "lam_k1", "lam_q2", "lam_k2")):
                    sp.dma_start(lam_v[:, i, :], t[v].rearrange("l d -> (l d)").partition_broadcast(P)).then_inc(const_landed, 16)
                sp.dma_start(sub_g[:, :, :], t["diff_subln_g"].partition_broadcast(P)).then_inc(const_landed, 16)
                sp.dma_start(fox_b[:, :], t["fox_bias"].rearrange("l n -> (l n)").partition_broadcast(P)).then_inc(const_landed, 16)
                for l in range(LAYERS):
                    sp.dma_start(small[:, l, :].rearrange("p (k n) -> p k n", n=N_FOX),
                                 t["w_in"][l].rearrange("(k p) n -> p k n", p=P)[:, :, C_FL:D_IN]).then_inc(const_landed, 16)
                sp.dma_start(small[:, 2, :].rearrange("p (k n) -> p k n", n=N_EXP),
                             t["w_router"][0].rearrange("(k p) n -> p k n", p=P)).then_inc(const_landed, 16)

            gains = (t["norm_mix_g"], t["norm_mem_g"], t["mem_norm_g"], t["norm_ffn_g"])
            for i, g in enumerate(gains):
                sp.dma_start(gain_rows[16 * i:16 * i + 16, :],
                             g.rearrange("l (k p) -> (l k) p", p=P)).then_inc(gains_landed, 16)
            sp.dma_start(h[:, :, :], t["x"][0].rearrange("(t p) n -> p t n", p=P)).then_inc(x_landed, 16)
            for l in range(LAYERS):
                n0 = l * L_UNITS
                if l == 0:
                    for c in range(6):
                        for u in range(2):
                            load(n0 + 2 * c + u, w_in[l][u, :, :, c * COLS:(c + 1) * COLS])
                            if (c, u) == (0, 1):
                                small_loads()
                            if (c, u) == (1, 0):
                                sp.dma_start(kv[:, :, 0:D], t["mem"][0].rearrange("(t p) n -> p t n", p=P)).then_inc(mem_landed, 16)
                else:
                    with sp.Fori(0, 2) as i:
                        for c in range(3):
                            for u in range(2):
                                load(n0 + 2 * c + u, w_in[l][u, :, :, bass.ds((3 * i + c) * COLS, COLS)], more=6 * i)
                for at, w, chunks in ((U_MKV, w_mkv, 4), (U_OUT, w_out, 2)):
                    for c in range(chunks):
                        for u in range(2):
                            load(n0 + at + 2 * c + u, w[l][u, :, :, c * COLS:(c + 1) * COLS])
                for u in range(2):
                    for c in range(2):
                        load(n0 + U_MQ + 2 * u + c, w_mq[l][u, :, :, c * COLS:(c + 1) * COLS])
                for c in range(2):
                    for u in range(2):
                        load(n0 + U_MO + 2 * c + u, w_mo[l][u, :, :, c * COLS:(c + 1) * COLS])
                if l == 0:
                    f0 = n0 + U_FFN
                    for k in range(4):
                        load(f0 + k, (ff1, ff3)[k % 2][k // 2, :, :, 0:COLS])
                    with sp.Fori(0, FF_FULL - 1) as i:
                        for k in range(4):
                            load(f0 + 4 + k, (ff1, ff3)[k // 2][k % 2, :, :, bass.ds((i + 1) * COLS, COLS)], more=6 * i)
                        for u in range(2):
                            load(f0 + 8 + u, ff2[2 * i + u], slot2, more=6 * i)
                    f1 = f0 + 4 + 6 * (FF_FULL - 1)
                    for k, w in enumerate((t["w_ff1"][0], t["w_ff3"][0])):
                        load(f1 + k, w.rearrange("(k p) n -> p k n", p=P)[:, :, FF_FULL * COLS:D_FF], slot8)
                    for u in range(3):
                        load(f1 + 2 + u, ff2[2 * (FF_FULL - 1) + u], slot2)

            def experts(q0):
                with sp.Fori(0, N_EXP) as e:
                    q = E_UNITS * (e + q0)
                    for k in range(4):
                        load(M0 + k, (e1, e3)[k // 2][2 * e + k % 2, :, :, 0:COLS], more=q)
                    with sp.Fori(1, EXP_CH) as j:
                        for k in range(4):
                            load(M0 + 4 + k, (e1, e3)[k // 2][2 * e + k % 2, :, :, bass.ds(j * COLS, COLS)],
                                 more=q + 6 * (j - 1))
                        for u in range(2):
                            load(M0 + 8 + u, e2[2 * EXP_CH * e + 2 * (j - 1) + u], slot2, more=q + 6 * (j - 1))
                    for u in range(2):
                        load(M0 + 6 * EXP_CH - 2 + u, e2[2 * EXP_CH * e + 2 * (EXP_CH - 1) + u], slot2, more=q)

            experts(0)
            sp.wait_ge(over_ready, 1)
            over = sp.value_load(n_over[0:1, 0:1], min_val=0, max_val=SEQ)
            with sp.If(over > 0):
                experts(N_EXP)
            sp.wait_ge(out_landed, 16 * 2 * TT)

        @block.gpsimd
        def _(pool):
            pool.memset(ident[:, :], 0.0).then_inc(pool_step, 1)
            pool.wait_ge(pool_step, 1)
            pool.affine_select(out=ident[:, :], in_=ident[:, :], compare_op=ALU.not_equal, fill=1.0, base=0,
                               pattern=[[-1, P]], channel_multiplier=1).then_inc(ident_made, 1)
            pool.dma_start(pos_i[:, :], t["positions"].rearrange("b (t p) -> p (b t)", p=P),
                           allow_slow_non_contiguous=True).then_inc(pos_landed, 16)

            pool.memset(tri[:, :], 1.0).then_inc(pool_step, 1)
            pool.memset(mask[:, :], 0.0).then_inc(pool_step, 1)
            pool.wait_ge(pool_step, 3)
            pool.affine_select(out=tri[:, 0:P], in_=tri[:, 0:P], compare_op=ALU.is_ge, fill=0.0, base=0,
                               pattern=[[1, P]], channel_multiplier=-1).then_inc(pool_made, 1)
            for c in (0, SEQ):
                pool.affine_select(out=mask[:, c:c + P], in_=mask[:, c:c + P], compare_op=ALU.is_ge, fill=NEG, base=0,
                                   pattern=[[-1, P]], channel_multiplier=1).then_inc(pool_made, 1)
            pool.iota(slots[:, :], pattern=[[1, P]], base=1, channel_multiplier=0,
                      allow_small_or_imprecise_dtypes=True).then_inc(pool_made, 1)
            pool.iota(eight[:, :], pattern=[[1, N_EXP]], base=0, channel_multiplier=0,
                      allow_small_or_imprecise_dtypes=True).then_inc(pool_made, 1)
            pool.wait_ge(ffn_added, 2)
            pool.dma_start(kv[:, :, 0:D], t["mem"][0].rearrange("(t p) n -> p t n", p=P)).then_inc(mem_again, 16)
            pool.wait_ge(acc_free, 32)
            pool.dma_start(ffn_g[:, :], t["norm_ffn_g"][1].partition_broadcast(P)).then_inc(late_landed, 16)
            pool.dma_start(fin_g[:, :], t["final_norm_g"].partition_broadcast(P)).then_inc(late_landed, 16)

        @block.scalar
        def _(act):
            steps = [0]

            def link(ins):
                steps[0] += 1
                ins.then_inc(act_step, 1)
                act.wait_ge(act_step, steps[0])

            def split(n, more=0, turns=0):
                act.wait_ge(raw_landed[n % RAW], 16 * turns + 16 * (n // RAW + 1))
                if n >= SPLIT:
                    act.wait_ge(unit_used, more + (n - SPLIT + 1))
                act.activation(w_hi[:, n % SPLIT, :], raw[:, n % RAW, :], ACT.Copy).then_inc(hi_split, 1)

            def splits(a, b):
                for n in range(a, b):
                    split(n)

            def turn_hi(tn, columns, groups=range(4)):
                for g in groups:
                    act.wait_ge(turned, 4 * tn + g + 1)
                    for k in (2 * g, 2 * g + 1):
                        c = columns(k)
                        act.activation(x_hi[:, k, :], ps[:, turn_bank(tn, g), (k % 2) * SEQ:(k % 2 + 1) * SEQ], ACT.Copy,
                                       scale=gain[:, c:c + 1]).then_inc(hi_turned, 1)

            def keep_rows(which, bank):
                act.wait_ge(rows_done, which + 1)
                act.activation(rows[which], ps[0:8, bank, 0:SEQ], ACT.Copy).then_inc(rows_kept, 1)

            def norm_stats(src, at, inc):
                for tt in range(TT):
                    link(act.activation(junk[:, :], src[:, tt, 0:D], ACT.Square, accum_out=stat[:, at, tt:tt + 1]))
                act.activation(stat[:, at, 4:6], stat[:, at, 0:2], ACT.Sqrt, scale=1.0 / D, bias=eps_c[:, 0:1]).then_inc(inc, 1)

            def half_turns(tn, columns, b, more):
                splits(b + 3, b + 5)
                turn_hi(tn, columns, (0, 1))
                splits(b + 5, b + 6 + more)
                turn_hi(tn, columns, (2, 3))
                splits(b + 6 + more, b + 7 + more)

            for l in range(LAYERS):
                n0 = l * L_UNITS
                if l == 0:
                    act.wait_ge(ang_ready, 1)
                    act.activation(cs[:, :, :, :], ang[:, 4, :, :, :], ACT.Sin).then_inc(sin_ready, 1)
                    act.wait_ge(gains_kept, 1)
                    turn_hi(0, lambda k: k, (0, 1))
                    splits(0, 1)
                    turn_hi(0, lambda k: k, (2, 3))
                    splits(1, 2)
                else:
                    turn_hi(6 * l, lambda k: 8 * l + k)
                    splits(n0 + 2, n0 + 3)
                norm_stats(h, 3 * l, rs_est)
                if l == 0:
                    splits(2, 3)
                    act.wait_ge(mem_landed, 16)
                    norm_stats(kv, N_MEM, mem_est)
                    act.wait_ge(dots_ready, 1)
                    act.activation(lam[:, 4:8], lam[:, 0:4], ACT.Exp).then_inc(lam_exp, 1)
                with act.Fori(0, 2) as i:
                    for k in range(6):
                        split(n0 + 3 + k, 6 * i, i)
                keep_rows(l, 7)
                turn_hi(6 * l + 1, lambda k: 32 + 8 * l + k)

                act.wait_ge(fl_neg, l + 1)
                link(act.activation(fl[:, 2, :, :], fl[:, 1, :, :], ACT.Exp))
                act.activation(fl[:, 3, :, :], fl[:, 2, :, :], ACT.Ln, bias=1.0).then_inc(fl_ln, 1)
                splits(n0 + 15, n0 + 16)

                def evict(c):
                    act.wait_ge(unit_used, n0 + 2 * c + 2)
                    act.activation(kv[:, :, (c - 6) * COLS:(c - 5) * COLS], acc(0), ACT.Copy).then_inc(acc_free, 1)

                def keep_qk(g):
                    act.wait_ge(qk_turned, 8 * l + g + 1)
                    queries = g in (0, 1, 4, 5)
                    act.activation(qkt[:, 2 * g:2 * g + 2, :],
                                   ps[:, 6 + g % 2, :].rearrange("p (b n) -> p b n", b=2), ACT.Copy,
                                   scale=1.0 / math.sqrt(HD) if queries else 1.0).then_inc(qk_kept, 1)

                def exps(i):
                    for m in item_maps(i):
                        act.wait_ge(masked, MAPS * l + m + 1)
                        for tt, a, b in ((0, 0, P), (1, P, SPAN)):
                            ins = act.activation(probs(m)[:, a:b], probs(m)[:, a:b], ACT.Exp,
                                                 bias=negmax[:, m, tt:tt + 1], accum_out=esum[:, m, tt:tt + 1])
                        ins.then_inc(expd, 1)

                def keep_pt(i):
                    act.wait_ge(p_turned, ITEMS * l + i + 1)
                    if i >= 2:
                        act.wait_ge(pv_done, ITEMS * l + i - 1)
                    act.activation(probs_t(i), ps[:, 6 + i % 2, 0:SPAN], ACT.Copy).then_inc(p_kept, 1)

                for g in range(4):
                    keep_qk(g)
                splits(n0 + 16, n0 + 17)
                for g in range(4, 8):
                    keep_qk(g)
                for s in range(ITEMS + 1):
                    if s in (1, 3, 9):
                        evict(7 + (1, 3, 9).index(s))
                    if s in SPLIT_STEPS:
                        split(n0 + 17 + SPLIT_STEPS.index(s))
                    if s < ITEMS:
                        exps(s)
                    if s >= 1 and s not in KV_STEPS:
                        keep_pt(s - 1)
                    if 3 <= s < 3 + N_DIFF:
                        i = s - 3
                        act.wait_ge(pv_taken, ITEMS * l + i + 1)
                        for tt in range(TT):
                            c = 2 * i + tt
                            ins = act.activation(junk[:, c * P:(c + 1) * P], mixed[:, tt, i * P:(i + 1) * P], ACT.Square,
                                                 accum_out=sub[:, 0, c:c + 1])
                    if s == 2 + N_DIFF:
                        link(ins)
                        act.activation(sub[:, 2, :], sub[:, 0, :], ACT.Sqrt, scale=1.0 / P, bias=eps_c[:, 1:2]).then_inc(sub_est, 1)
                        link(act.activation(spare[:, :], eps_c[:, 0:1], ACT.Exp))
                    if s >= 1 and s in KV_STEPS:
                        keep_pt(s - 1)
                turn_hi(6 * l + 2, lambda k: 64)
                splits(n0 + 21, n0 + 23)
                half_turns(6 * l + 3, lambda k: 16 + 8 * l + k, n0 + U_OUT, 1)
                norm_stats(h, 3 * l + 1, rs_est)
                splits(n0 + 28, n0 + 30)

                def keep_mqk(g):
                    act.wait_ge(mqk_turned, 8 * l + g + 1)
                    act.activation(qkt[:, 2 * g:2 * g + 2, :],
                                   ps[:, 6 + g % 2, :].rearrange("p (b n) -> p b n", b=2), ACT.Copy,
                                   scale=1.0 / math.sqrt(MEM_HD) if g >= 4 else 1.0).then_inc(mqk_kept, 1)

                for g in range(8):
                    keep_mqk(g)
                for s in range(MEM_HEADS + 1):
                    if s < MEM_HEADS:
                        act.wait_ge(mmax, MEM_HEADS * l + s + 1)
                        for tt in range(TT):
                            ins = act.activation(mem_p(s)[:, tt, :], ps[:, 4 + s % 2, tt * SEQ:(tt + 1) * SEQ], ACT.Exp,
                                                 bias=negmax[:, s, tt:tt + 1], accum_out=esum[:, s, tt:tt + 1])
                        ins.then_inc(mexpd, 1)
                    if s >= 1:
                        act.wait_ge(mp_turned, MEM_HEADS * l + s)
                        if s >= 3:
                            act.wait_ge(mpv_done, MEM_HEADS * l + s - 2)
                        act.activation(mem_pt(s - 1), ps[:, 6 + (s - 1) % 2, :], ACT.Copy).then_inc(mp_kept, 1)
                turn_hi(6 * l + 4, lambda k: 64)
                splits(n0 + 30, n0 + 31)
                half_turns(6 * l + 5, lambda k: 48 + 8 * l + k, n0 + U_MO, 1 - l)
                norm_stats(h, 3 * l + 2, rs_est)

                if l == 0:
                    f0 = n0 + U_FFN

                    def silu(pair, used, wide=COLS):
                        act.wait_ge(unit_used, used)
                        for tt in range(TT):
                            ins = act.activation(gate[:, tt, 0:wide], acc(pair)[:, tt, 0:wide], ACT.Silu,
                                                 scale=stat[:, 2, 6 + tt:7 + tt])
                        ins.then_inc(silu_done, 1)

                    def keep_hi(pair, buf, want, blocks=4):
                        act.wait_ge(g_turned, want)
                        act.activation(g_hi[:, buf, 0:blocks, :], acc(pair).rearrange("p c (b n) -> p (c b) n", n=SEQ)[:, 0:blocks, :],
                                       ACT.Copy).then_inc(ghi_kept, 1)

                    act.wait_ge(ffn_rooted, 1)
                    splits(f0 + 4, f0 + 5)
                    silu(0, f0 + 3)
                    splits(f0 + 5, f0 + 6)
                    keep_hi(0, 0, 1)
                    with act.Fori(0, (FF_FULL - 1) // 2) as i:
                        for r in range(2):
                            b = f0 + 4 + 6 * r
                            for k in (2, 3):
                                split(b + k, 12 * i, 2 * i)
                            silu((r + 1) % 2, 12 * i + (b + 2))
                            for k in range(4, 8):
                                split(b + k, 12 * i, 2 * i)
                            keep_hi((r + 1) % 2, (r + 1) % 2, 2 * i + (r + 2))
                    f1 = f0 + 4 + 6 * (FF_FULL - 1)
                    splits(f1 + 2, f1 + 3)
                    silu(1, f1 + 1, SEQ)
                    splits(f1 + 3, f1 + 5)
                    keep_hi(1, 1, FF_FULL + 1, 2)
                    splits(L_UNITS, L_UNITS + 2)

            keep_rows(2, 4)
            act.wait_ge(routed, 1)
            act.activation(route[:, :, 4, 0:1], route[:, :, 3, 0:1], ACT.Exp).then_inc(route_exp, 1)

            def keep_xe(q):
                for g in range(2):
                    act.wait_ge(gathered, q * 2 + (g + 1))
                    act.activation(xe_hi[:, 4 * g:4 * g + 4, :], ps[:, 5 + g, :].rearrange("p (k n) -> p k n", k=4),
                                   ACT.Copy).then_inc(xe_hi_kept, 1)

            def keep_ye(q, b0):
                for c in range(2):
                    if c == 0:
                        act.wait_ge(ye_done, q + 1)
                    else:
                        act.wait_ge(unit_used, E_UNITS * (q - b0) + M0)
                    act.activation(ye[:, c * COLS:(c + 1) * COLS], ps[:, 2 + c, :], ACT.Copy).then_inc(ye_kept, 1)

            def expert(q, b0, ahead=0, last=False):
                more = E_UNITS * q

                def s(k, j=0):
                    split(M0 + k, more + 6 * j, EXP_CH * q + j)

                for k in range(ahead, 2):
                    s(k)
                keep_ye(q + b0, b0)
                for k in range(max(ahead, 2), 4):
                    s(k)
                act.wait_ge(unit_used, more + (M0 + 2))
                act.activation(gate[:, 0, :], ps[:, 0, :], ACT.Silu).then_inc(e_silu, 1)
                s(4), s(5)
                act.wait_ge(pick_turned, q + 1)
                act.activation(pick_t[:, :, :], ps[:, 3, 0:SEQ].rearrange("p (t n) -> p t n", t=TT), ACT.Copy).then_inc(pick_kept, 1)
                act.wait_ge(e_turned, EXP_CH * q + 1)
                act.activation(g_hi[:, 0, :, 0:P], ps[:, 4, :].rearrange("p (b n) -> p b n", b=4), ACT.Copy).then_inc(e_hi, 1)
                with act.Fori(0, EXP_CH - 1) as j:
                    s(6, j), s(7, j)
                    act.wait_ge(unit_used, more + 6 * j + (M0 + 6))
                    act.activation(gate[:, 0, :], ps[:, 0, :], ACT.Silu).then_inc(e_silu, 1)
                    for k in range(8, 12):
                        s(k, j)
                    act.wait_ge(e_turned, EXP_CH * q + j + 2)
                    act.activation(g_hi[:, 0, :, 0:P], ps[:, 4, :].rearrange("p (b n) -> p b n", b=4), ACT.Copy).then_inc(e_hi, 1)
                if not last:
                    keep_xe(q + 1)

            keep_xe(0)
            expert(0, 0, ahead=3)
            with act.Fori(1, N_EXP - 1) as e:
                expert(e, 0)
            expert(N_EXP - 1, 0, last=True)
            keep_ye(N_EXP, 0)
            act.wait_ge(over_ready, 1)
            over = act.value_load(n_over[0:1, 0:1], min_val=0, max_val=SEQ)
            with act.If(over > 0):
                keep_xe(N_EXP)
                with act.Fori(0, N_EXP - 1) as e:
                    expert(e + N_EXP, 1)
                expert(2 * N_EXP - 1, 1, last=True)
                keep_ye(2 * N_EXP + 1, 1)
            last = stat[:, N_FINAL, :]
            act.activation(spare[:, :], eps_c[:, 0:1], ACT.Sqrt)
            act.wait_ge(summed, 1)
            act.activation(junk[:, :], h[:, 0, :], ACT.Square, accum_out=last[:, 0:1]).then_inc(first_squared, 1)
            act.wait_ge(first_squared, 1)
            act.wait_ge(squared, 1)
            act.activation(last[:, 4:6], last[:, 0:2], ACT.Sqrt, scale=1.0 / D, bias=eps_c[:, 0:1]).then_inc(rs_est, 1)
            for n in range(2 * TT):
                tt, c = n // 2, n % 2
                act.wait_ge(result_ready, n + 1)
                act.dma_start(out[0, tt * P:(tt + 1) * P, c * COLS:(c + 1) * COLS],
                              result[:, tt, c * COLS:(c + 1) * COLS]).then_inc(out_landed, 16)

        @block.vector
        def _(dve):
            steps = [0]

            def link(ins):
                steps[0] += 1
                ins.then_inc(dve_step, 1)
                dve.wait_ge(dve_step, steps[0])

            def split(n, more=0):
                dve.wait_ge(hi_split, more + (n + 1))
                dve.tensor_tensor(w_lo[:, n % SPLIT, :], raw[:, n % RAW, :], w_hi[:, n % SPLIT, :].bitcast(F32),
                                  ALU.subtract).then_inc(lo_split, 1)

            def splits(a, b):
                for n in range(a, b):
                    split(n)

            def turn_lo(tn, columns, tiles=range(KT)):
                for k in tiles:
                    dve.wait_ge(hi_turned, KT * tn + k // 2 * 2 + 2)
                    c = columns(k)
                    dve.scalar_tensor_tensor(out=x_lo[:, k, :], in0=ps[:, turn_bank(tn, k // 2), (k % 2) * SEQ:(k % 2 + 1) * SEQ],
                                             scalar=gain[:, c:c + 1], in1=x_hi[:, k, :].bitcast(F32),
                                             op0=ALU.mult, op1=ALU.subtract).then_inc(lo_turned, 1)

            def refine(y, v, y0, tmp):
                link(dve.tensor_tensor(tmp, y0, y0, ALU.mult))
                link(dve.tensor_tensor(tmp, tmp, v, ALU.mult))
                link(dve.tensor_scalar(tmp, tmp, -0.5, 1.5, ALU.mult, ALU.add))
                link(dve.tensor_tensor(y, y0, tmp, ALU.mult))

            def rstd(at):
                dve.tensor_scalar(stat[:, at, 2:4], stat[:, at, 0:2], 1.0 / D, EPS, ALU.mult, ALU.add)
                link(dve.reciprocal(stat[:, at, 4:6], stat[:, at, 4:6]))
                refine(stat[:, at, 6:8], stat[:, at, 2:4], stat[:, at, 4:6], newton[:, :])

            def norm(number):
                dve.wait_ge(rs_est, number + 1)
                rstd(number)

            def root(number, tt):
                return stat[:, number, 6 + tt:7 + tt]

            for i in range(ROPE_HALF):
                f = float(np.float32(500000.0) ** np.float32(-2.0 * i / (2 * ROPE_HALF)))
                ins = dve.memset(inv_f[:, i:i + 1], f)
            dve.memset(eps_c[:, 0:1], EPS)
            dve.memset(eps_c[:, 1:2], SUB_EPS)
            dve.memset(gain[:, 64:65], 1.0)
            link(ins)
            dve.wait_ge(pos_landed, 16)
            link(dve.tensor_copy(pos_f, pos_i[:, :]))
            for tt in range(TT):
                ins = dve.tensor_scalar(ang[:, 0, 1, tt, :], inv_f, pos_f[:, tt:tt + 1], None, ALU.mult)
            link(ins)
            link(dve.tensor_copy(ang[:, 0, 0, :, :], ang[:, 0, 1, :, :]))
            dve.tensor_scalar(ang[:, 1, 0, :, :], ang[:, 0, 0, :, :], 1.0 / TWO_PI, 0.25, ALU.mult, ALU.add)
            link(dve.tensor_scalar(ang[:, 1, 1, :, :], ang[:, 0, 1, :, :], 1.0 / TWO_PI, None, ALU.mult))
            link(dve.tensor_scalar(ang[:, 2, :, :, :], ang[:, 1, :, :, :], ROUND, None, ALU.add))
            link(dve.tensor_scalar(ang[:, 3, :, :, :], ang[:, 2, :, :, :], -ROUND, None, ALU.add))
            for part in (PI_HI, PI_MID, PI_LO):
                link(dve.scalar_tensor_tensor(out=ang[:, 0, :, :, :], in0=ang[:, 3, :, :, :], scalar=-part,
                                              in1=ang[:, 0, :, :, :], op0=ALU.mult, op1=ALU.add))
            link(dve.tensor_scalar(ang[:, 0, 0, :, :], ang[:, 0, 0, :, :], math.pi / 2, None, ALU.add))
            dve.tensor_scalar(ang[:, 4, :, :, :], ang[:, 0, :, :, :], SIN_MAX, -SIN_MAX, ALU.min, ALU.max).then_inc(ang_ready, 1)
            link(dve.memset(route[:, :, :, :], 0.0))
            dve.wait_ge(gains_turned, 1)
            dve.tensor_copy(gain[:, 0:64], ps[:, 0, 0:64]).then_inc(gains_kept, 1)
            dve.wait_ge(gains_kept, 1)
            turn_lo(0, lambda k: k, range(4))
            splits(0, 1)
            turn_lo(0, lambda k: k, range(4, 8))
            splits(1, 2)
            norm(0)
            splits(2, 3)
            dve.wait_ge(const_landed, 16 * 9)
            for i in range(2):
                for l in range(LAYERS):
                    a, b = lam_v[:, 2 * i, l * HD:(l + 1) * HD], lam_v[:, 2 * i + 1, l * HD:(l + 1) * HD]
                    ins = dve.tensor_tensor_reduce(decay[:, 2 * i + l, 0:HD],
                                                   a, b, 1.0, 0.0, ALU.mult, ALU.add, lam[:, 2 * i + l:2 * i + l + 1])
            ins.then_inc(dots_ready, 1)
            for l in range(LAYERS):
                ins = dve.tensor_scalar(sub_g[:, l, :], sub_g[:, l, :], 1.0 - lam_init(l), None, ALU.mult)
            dve.wait_ge(lam_exp, 1)
            for l in range(LAYERS):
                ins = dve.scalar_tensor_tensor(out=lam[:, l:l + 1], in0=lam[:, 4 + l:5 + l], scalar=lam_init(l),
                                               in1=lam[:, 6 + l:7 + l], op0=ALU.add, op1=ALU.subtract)
            link(ins)
            link(dve.tensor_scalar(lam[:, 2:4], lam[:, 0:2], -1.0, None, ALU.mult))
            link(dve.tensor_copy(s_hi[:, :, :], small[:, :, :]))
            dve.tensor_tensor(s_lo[:, :, :], small[:, :, :], s_hi[:, :, :].bitcast(F32), ALU.subtract).then_inc(small_split, 1)
            dve.wait_ge(sin_ready, 1)

            for l in range(LAYERS):
                n0 = l * L_UNITS
                a0 = 16 * l
                if l:
                    turn_lo(6 * l, lambda k: 8 * l + k)
                    splits(n0 + 2, n0 + 3)
                if l == 0:
                    dve.wait_ge(mem_est, 1)
                    rstd(N_MEM)
                else:
                    norm(3 * l)
                dve.wait_ge((mem_landed, mem_again)[l], 16)
                for tt in range(TT):
                    ins = dve.tensor_scalar(hn[:, tt, :], kv[:, tt, 0:D], root(N_MEM, tt), None, ALU.mult)
                ins.then_inc(source_ready, 1)
                with dve.Fori(0, 2) as i:
                    for c in range(3):
                        split(n0 + 3 + 2 * c, 6 * i)
                        dve.wait_ge(unit_used, 6 * i + (n0 + 2 * c + 2))
                        for tt in range(TT):
                            ins = dve.tensor_scalar(proj[:, tt, bass.ds((3 * i + c) * COLS, COLS)], acc(c)[:, tt, :],
                                                    root(3 * l, tt), None, ALU.mult)
                        ins.then_inc(acc_free, 1)
                        split(n0 + 4 + 2 * c, 6 * i)
                dve.wait_ge(fl_done, l + 1)
                for tt in range(TT):
                    ins = dve.scalar_tensor_tensor(out=fl[:, 0, tt, :], in0=ps[:, 7, tt * N_FOX:(tt + 1) * N_FOX],
                                                   scalar=root(3 * l, tt), in1=fox_b[:, l * N_FOX:(l + 1) * N_FOX],
                                                   op0=ALU.mult, op1=ALU.add)
                link(ins)
                dve.scalar_tensor_tensor(out=fl[:, 1, :, :], in0=fl[:, 0, :, :], scalar=-1.0, in1=fl[:, 0, :, :],
                                         op0=ALU.mult, op1=ALU.min).then_inc(fl_neg, 1)
                turn_lo(6 * l + 1, lambda k: 32 + 8 * l + k)
                heads = proj[:, :, 0:D_MAPS].rearrange("p t (h d) -> p t h d", d=HD)
                rot = decay[:, :, :].rearrange("p a b -> p (a b)")[:, 0:1024].rearrange(
                    "p (s t h i) -> p s t h i", s=4, t=TT, h=16)
                for tt in range(TT):
                    t1, t2 = heads[:, tt, :, 0:ROPE_HALF], heads[:, tt, :, ROPE_HALF:2 * ROPE_HALF]
                    cos = cs[:, 0, tt, :].unsqueeze(1).to_broadcast([P, 16, ROPE_HALF])
                    sin = cs[:, 1, tt, :].unsqueeze(1).to_broadcast([P, 16, ROPE_HALF])
                    for s, (x, f) in enumerate(((t1, cos), (t2, sin), (t2, cos), (t1, sin))):
                        ins = dve.tensor_tensor(rot[:, s, tt], x, f, ALU.mult)
                link(ins)
                for tt in range(TT):
                    dve.tensor_tensor(heads[:, tt, :, 0:ROPE_HALF], rot[:, 0, tt], rot[:, 1, tt], ALU.subtract)
                    ins = dve.tensor_tensor(heads[:, tt, :, ROPE_HALF:2 * ROPE_HALF], rot[:, 2, tt], rot[:, 3, tt], ALU.add)
                ins.then_inc(roped, 1)
                dve.wait_ge(fl_ln, l + 1)
                dve.scalar_tensor_tensor(out=fl[:, 1, :, :], in0=fl[:, 0, :, :], scalar=0.0, in1=fl[:, 3, :, :],
                                         op0=ALU.min, op1=ALU.subtract).then_inc(logf_ready, 1)

                splits(n0 + 15, n0 + 16)
                dve.wait_ge(unit_used, n0 + 14)
                dve.tensor_copy(kv[:, :, 0:COLS], acc(0)).then_inc(acc_free, 1)
                splits(n0 + 16, n0 + 17)

                def mask_map(m):
                    dve.wait_ge(scored, MAPS * l + m + 1)
                    if m >= 4:
                        dve.wait_ge(p_turned, ITEMS * l + map_item(m - 4) + 1)
                    elif l:
                        dve.wait_ge(p_turned, ITEMS * l)
                    for tt, a, b in ((0, 0, P), (1, P, SPAN)):
                        add = mask[:, a:b] if m < 2 * N_DIFF else decay[:, m - 2 * N_DIFF, a:b]
                        ins = dve.tensor_tensor_reduce(probs(m)[:, a:b], ps[:, 4 + m % 2, a:b], add, 1.0, 3 * NEG,
                                                       ALU.add, ALU.max, negmax[:, m, tt:tt + 1])
                    link(ins)
                    dve.tensor_scalar(negmax[:, m, :], negmax[:, m, :], -1.0, None, ALU.mult).then_inc(masked, 1)

                def weigh(i):
                    for m in item_maps(i):
                        dve.wait_ge(expd, MAPS * l + m + 1)
                        ins = dve.reciprocal(einv[:, m, :], esum[:, m, :])
                    link(ins)
                    if i < N_DIFF:
                        a, b = item_maps(i)
                        link(dve.scalar_tensor_tensor(out=einv[:, b, :], in0=einv[:, b, :], scalar=lam[:, 2 + l:3 + l],
                                                      in1=esum[:, a, :], op0=ALU.mult, op1=ALU.mult))
                        for tt, x, y in ((0, 0, P), (1, P, SPAN)):
                            ins = dve.scalar_tensor_tensor(out=probs(a)[:, x:y], in0=probs(b)[:, x:y],
                                                           scalar=einv[:, b, tt:tt + 1], in1=probs(a)[:, x:y],
                                                           op0=ALU.mult, op1=ALU.add)
                        ins.then_inc(weighed, 1)

                def take_pv(i):
                    dve.wait_ge(pv_done, ITEMS * l + i + 1)
                    wide = P if i < N_DIFF else HD
                    c, m = (i * P if i < N_DIFF else N_DIFF * P + (i - N_DIFF) * HD), item_maps(i)[0]
                    for tt in range(TT):
                        ins = dve.tensor_scalar(mixed[:, tt, c:c + wide], ps[:, 2 + i % 2, tt * wide:(tt + 1) * wide],
                                                einv[:, m, tt:tt + 1], None, ALU.mult)
                    ins.then_inc(pv_taken, 1)

                def norm_heads():
                    dve.wait_ge(sub_est, l + 1)
                    dve.tensor_scalar(sub[:, 1, :], sub[:, 0, :], 1.0 / P, SUB_EPS, ALU.mult, ALU.add)
                    link(dve.reciprocal(sub[:, 2, :], sub[:, 2, :]))
                    refine(sub[:, 4, :], sub[:, 1, :], sub[:, 2, :], sub[:, 3, :])
                    for i in range(N_DIFF):
                        for tt in range(TT):
                            o = mixed[:, tt, i * P:(i + 1) * P]
                            ins = dve.scalar_tensor_tensor(out=o, in0=o, scalar=sub[:, 4, 2 * i + tt:2 * i + tt + 1],
                                                           in1=sub_g[:, l, :], op0=ALU.mult, op1=ALU.mult)
                    ins.then_inc(source_ready, 1)

                dve.wait_ge(pool_made, 5)
                dve.wait_ge(cq_done, l + 1)
                link(dve.tensor_copy(cq[:, :, :], ps[:, 4, 0:TT * N_FOX].rearrange("p (t n) -> p t n", t=TT)))
                for f in range(N_FOX):
                    dve.wait_ge(ck_done, N_FOX * l + f + 1)
                    c = ps[:, 2 + f % 2, 0:SEQ]
                    dve.scalar_tensor_tensor(out=decay[:, f, 0:P], in0=mask[:, 0:P], scalar=cq[:, 0, f:f + 1],
                                             in1=c[:, 0:P], op0=ALU.add, op1=ALU.subtract)
                    dve.scalar_tensor_tensor(out=decay[:, f, P:SPAN], in0=mask[:, P:SPAN], scalar=cq[:, 1, f:f + 1],
                                             in1=c, op0=ALU.add, op1=ALU.subtract).then_inc(ck_used, 1)
                for s in range(ITEMS + 2):
                    if 1 <= s <= N_DIFF:
                        weigh(s - 1)
                    if s < ITEMS:
                        for m in item_maps(s):
                            mask_map(m)
                    if s in SPLIT_STEPS:
                        split(n0 + 17 + SPLIT_STEPS.index(s))
                    if N_DIFF < s <= ITEMS:
                        weigh(s - 1)
                    if s == N_DIFF + 3:
                        norm_heads()
                    if s >= 2:
                        take_pv(s - 2)
                turn_lo(6 * l + 2, lambda k: 64)
                splits(n0 + 21, n0 + 23)

                def add_chunk(c, unit):
                    dve.wait_ge(unit_used, unit + 1)
                    r = h[:, :, c * COLS:(c + 1) * COLS]
                    dve.tensor_tensor(r, r, acc(c % 2), ALU.add).then_inc(acc_free, 1)

                def half_turns(tn, columns, b, more):
                    splits(b + 3, b + 4)
                    add_chunk(0, b + 1)
                    splits(b + 4, b + 5)
                    turn_lo(tn, columns, range(4))
                    splits(b + 5, b + 6)
                    add_chunk(1, b + 3)
                    splits(b + 6, b + 6 + more)
                    turn_lo(tn, columns, range(4, 8))
                    splits(b + 6 + more, b + 7 + more)

                half_turns(6 * l + 3, lambda k: 16 + 8 * l + k, n0 + U_OUT, 1)
                norm(3 * l + 1)

                def evict_q(c):
                    dve.wait_ge(unit_used, n0 + U_MQ + 3 + c)
                    for tt in range(TT):
                        ins = dve.tensor_scalar(mem_q[:, tt, c * COLS:(c + 1) * COLS], acc(c)[:, tt, :],
                                                root(3 * l + 1, tt), None, ALU.mult)
                    ins.then_inc(acc_free, 1)

                evict_q(0)
                splits(n0 + 28, n0 + 30)
                evict_q(1)
                for s in range(MEM_HEADS + 2):
                    if s < MEM_HEADS:
                        dve.wait_ge(mscored, MEM_HEADS * l + s + 1)
                        link(dve.tensor_reduce(negmax[:, s, :], ps[:, 4 + s % 2, :].rearrange("p (t n) -> p t n", t=TT),
                                               AX.X, ALU.max))
                        dve.tensor_scalar(negmax[:, s, :], negmax[:, s, :], -1.0, None, ALU.mult).then_inc(mmax, 1)
                    if s >= 2:
                        i = s - 2
                        link(dve.reciprocal(einv[:, i, :], esum[:, i, :]))
                        dve.wait_ge(mpv_done, MEM_HEADS * l + i + 1)
                        for tt in range(TT):
                            ins = dve.tensor_scalar(mixed[:, tt, i * MEM_HD:(i + 1) * MEM_HD],
                                                    ps[:, 2 + i % 2, tt * SEQ:(tt + 1) * SEQ], einv[:, i, tt:tt + 1],
                                                    None, ALU.mult)
                        ins.then_inc(source_ready if i == MEM_HEADS - 1 else mpv_taken, 1)
                turn_lo(6 * l + 4, lambda k: 64)
                splits(n0 + 30, n0 + 31)
                half_turns(6 * l + 5, lambda k: 48 + 8 * l + k, n0 + U_MO, 1 - l)
                if l:
                    dve.wait_ge(acc_free, 32)
                    dve.memset(ps[:, 2:4, :], 0.0).then_inc(comb_ready, 1)
                    dve.memset(pick_t[:, :, :], 0.0).then_inc(comb_ready, 1)
                norm(3 * l + 2)
                if l == 0:
                    dve.sem_inc(ffn_rooted, 1)
                    f0 = n0 + U_FFN

                    def gated_chunk(pair, used, want, wide=COLS):
                        dve.wait_ge(silu_done, want)
                        dve.wait_ge(unit_used, used)
                        for tt in range(TT):
                            ins = dve.scalar_tensor_tensor(out=gate[:, tt, 0:wide], in0=acc(pair)[:, tt, 0:wide],
                                                           scalar=root(2, tt), in1=gate[:, tt, 0:wide],
                                                           op0=ALU.mult, op1=ALU.mult)
                        ins.then_inc(gated, 1)

                    def keep_lo(pair, buf, want, blocks=4):
                        dve.wait_ge(ghi_kept, want)
                        dve.tensor_tensor(g_lo[:, buf, 0:blocks, :],
                                          acc(pair).rearrange("p c (b n) -> p (c b) n", n=SEQ)[:, 0:blocks, :],
                                          g_hi[:, buf, 0:blocks, :].bitcast(F32), ALU.subtract).then_inc(glo_kept, 1)

                    dve.wait_ge(lo_turned, KT * (6 * l + 6))
                    dve.memset(ps[:, 4:8, :], 0.0).then_inc(out_zeroed, 1)
                    splits(f0 + 4, f0 + 5)
                    gated_chunk(1, f0 + 4, 1)
                    splits(f0 + 5, f0 + 6)
                    keep_lo(0, 0, 1)
                    with dve.Fori(0, (FF_FULL - 1) // 2) as i:
                        for r in range(2):
                            b = f0 + 4 + 6 * r
                            for k in range(2, 6):
                                split(b + k, 12 * i)
                            gated_chunk(r % 2, 12 * i + (b + 4), 2 * i + (r + 2))
                            for k in range(6, 8):
                                split(b + k, 12 * i)
                            keep_lo((r + 1) % 2, (r + 1) % 2, 2 * i + (r + 2))
                    f1 = f0 + 4 + 6 * (FF_FULL - 1)
                    splits(f1 + 2, f1 + 4)
                    gated_chunk(0, f1 + 2, FF_FULL + 1, SEQ)
                    splits(f1 + 4, f1 + 5)
                    keep_lo(1, 1, FF_FULL + 1, 2)
                    splits(L_UNITS, L_UNITS + 1)
                    for c in range(2):
                        if c == 0:
                            dve.wait_ge(ffn_summed, 1)
                        else:
                            splits(L_UNITS + 1, L_UNITS + 2)
                            dve.wait_ge(unit_used, L_UNITS)
                        for tt in range(TT):
                            r = h[:, tt, c * COLS:(c + 1) * COLS]
                            ins = dve.tensor_tensor(r, r, ps[:, 4 + 2 * tt + c, :], ALU.add)
                        ins.then_inc(ffn_added, 1)

            dve.wait_ge(logits_done, 1)
            def make_pick(e):
                for tt in range(TT):
                    ins = dve.tensor_scalar(pick[:, tt, :], slots[:, :], posm[:, tt, bass.ds(e, 1)], None, ALU.is_equal)
                ins.then_inc(pick_made, 1)

            lg, top, place, gap, ex = (route[:, :, i, :] for i in range(5))
            sel1, sel2, comb, posm, picks = (route[:, :, i, :] for i in range(5, 10))
            for tt in range(TT):
                ins = dve.tensor_scalar(lg[:, tt, 0:8], ps[:, 4, tt * N_EXP:(tt + 1) * N_EXP], root(5, tt), None, ALU.mult)
            link(ins)
            for tt in range(TT):
                ins = dve.max(top[:, tt, 0:8], lg[:, tt, 0:8])
            link(ins)
            for tt in range(TT):
                ins = dve.max_index(t_idx[:, tt, :], top[:, tt, 0:8], lg[:, tt, 0:8])
            link(ins)
            dve.tensor_tensor(gap[:, :, 0:1], top[:, :, 1:2], top[:, :, 0:1], ALU.subtract).then_inc(routed, 1)
            link(dve.tensor_copy(place[:, :, 0:8], t_idx[:, :, :]))
            for tt in range(TT):
                dve.tensor_scalar(sel1[:, tt, 0:8], eight[:, :], place[:, tt, 0:1], None, ALU.is_equal)
                ins = dve.tensor_scalar(sel2[:, tt, 0:8], eight[:, :], place[:, tt, 1:2], None, ALU.is_equal)
            link(ins)
            dve.tensor_tensor(picks[:, :, 0:8], sel1[:, :, 0:8], sel2[:, :, 0:8], ALU.add).then_inc(picked_sum, 1)
            dve.wait_ge(late_landed, 32)
            for tt in range(TT):
                ins = dve.scalar_tensor_tensor(out=hn[:, tt, :], in0=h[:, tt, :], scalar=root(5, tt),
                                               in1=ffn_g[:, :], op0=ALU.mult, op1=ALU.mult)
            ins.then_inc(hn_ready, 1)
            dve.wait_ge(counted, 1)
            link(dve.tensor_tensor(posm[:, :, 0:8], ps[:, 4, 0:TT * N_EXP].rearrange("p (t n) -> p t n", t=TT),
                                   picks[:, :, 0:8], ALU.mult))
            make_pick(0)
            dve.wait_ge(route_exp, 1)
            link(dve.tensor_scalar(gap[:, :, 1:2], ex[:, :, 0:1], 1.0, None, ALU.add))
            link(dve.reciprocal(gap[:, :, 2:3], gap[:, :, 1:2]))
            link(dve.tensor_tensor(gap[:, :, 3:4], gap[:, :, 2:3], ex[:, :, 0:1], ALU.mult))
            for tt in range(TT):
                ins = dve.tensor_scalar(sel2[:, tt, 0:8], sel2[:, tt, 0:8], gap[:, tt, 3:4], None, ALU.mult)
            link(ins)
            for tt in range(TT):
                ins = dve.scalar_tensor_tensor(out=comb[:, tt, 1:9], in0=sel1[:, tt, 0:8], scalar=gap[:, tt, 2:3],
                                               in1=sel2[:, tt, 0:8], op0=ALU.mult, op1=ALU.add)
            link(ins)
            link(dve.tensor_reduce(gap[:, 0, 4:5], ps[:, 4, TT * N_EXP:(TT + 1) * N_EXP], AX.X, ALU.max))
            link(dve.tensor_scalar(gap[:, 0, 5:6], gap[:, 0, 4:5], -float(P), 0.0, ALU.add, ALU.max))
            dve.tensor_copy(n_over[:, :], gap[:, 0, 5:6]).then_inc(over_ready, 1)
            def keep_xe(q):
                for g in range(2):
                    dve.wait_ge(xe_hi_kept, q * 2 + (g + 1))
                    dve.tensor_tensor(xe_lo[:, 4 * g:4 * g + 4, :], ps[:, 5 + g, :].rearrange("p (k n) -> p k n", k=4),
                                      xe_hi[:, 4 * g:4 * g + 4, :].bitcast(F32), ALU.subtract).then_inc(xe_lo_kept, 1)

            def accumulate(q, column):
                for n, bank in enumerate((5, 6, 7, 2)):
                    c, tt = n // 2, n % 2
                    dve.wait_ge(scattered, 4 * q + (n + 1))
                    r = h[:, tt, c * COLS:(c + 1) * COLS]
                    ins = dve.scalar_tensor_tensor(out=r, in0=ps[:, bank, :], scalar=comb[:, tt, bass.ds(column, 1)],
                                                   in1=r, op0=ALU.mult, op1=ALU.add)
                return ins

            def expert(e, q0, b0, ahead=0, last=False):
                q = e + q0
                more = E_UNITS * q
                for k in range(ahead, 6):
                    split(M0 + k, more)
                dve.wait_ge(e_silu, EXP_CH * q + 1)
                dve.wait_ge(unit_used, more + (M0 + 4))
                dve.tensor_tensor(gate[:, 0, :], ps[:, 1, :], gate[:, 0, :], ALU.mult).then_inc(e_gated, 1)
                accumulate(q + b0, e).then_inc(h_added, 1)
                if not last:
                    dve.wait_ge(pick_turned, q + 1)
                    make_pick(e + 1)
                dve.wait_ge(pick_kept, q + 1)
                dve.wait_ge(h_added, q + 1)
                dve.memset(ps[:, 2:4, :], 0.0).then_inc(e_zeroed, 1)
                dve.wait_ge(e_hi, EXP_CH * q + 1)
                dve.tensor_tensor(g_lo[:, 0, :, 0:P], ps[:, 4, :].rearrange("p (b n) -> p b n", b=4),
                                  g_hi[:, 0, :, 0:P].bitcast(F32), ALU.subtract).then_inc(e_lo, 1)
                with dve.Fori(0, EXP_CH - 1) as j:
                    for k in range(6, 10):
                        split(M0 + k, more + 6 * j)
                    dve.wait_ge(e_silu, EXP_CH * q + j + 2)
                    dve.wait_ge(unit_used, more + 6 * j + (M0 + 8))
                    dve.tensor_tensor(gate[:, 0, :], ps[:, 1, :], gate[:, 0, :], ALU.mult).then_inc(e_gated, 1)
                    for k in range(10, 12):
                        split(M0 + k, more + 6 * j)
                    dve.wait_ge(e_hi, EXP_CH * q + j + 2)
                    dve.tensor_tensor(g_lo[:, 0, :, 0:P], ps[:, 4, :].rearrange("p (b n) -> p b n", b=4),
                                      g_hi[:, 0, :, 0:P].bitcast(F32), ALU.subtract).then_inc(e_lo, 1)
                if not last:
                    keep_xe(q + 1)

            keep_xe(0)
            expert(0, 0, 0, ahead=3)
            with dve.Fori(1, N_EXP - 1) as e:
                expert(e, 0, 0)
            expert(N_EXP - 1, 0, 0, last=True)
            link(accumulate(N_EXP, N_EXP))
            over = dve.value_load(n_over[0:1, 0:1], min_val=0, max_val=SEQ)
            with dve.If(over > 0):
                before = steps[0]
                link(dve.tensor_scalar(posm[:, :, 0:8], posm[:, :, 0:8], -float(P), None, ALU.add))
                dve.memset(pick_t[:, :, :], 0.0).then_inc(comb_ready, 1)
                dve.memset(ps[:, 2:4, :], 0.0).then_inc(comb_ready, 1)
                dve.wait_ge(pick_turned, N_EXP)
                make_pick(0)
                keep_xe(N_EXP)
                with dve.Fori(0, N_EXP - 1) as e:
                    expert(e, N_EXP, 1)
                expert(N_EXP - 1, N_EXP, 1, last=True)
                link(accumulate(2 * N_EXP + 1, N_EXP))
                steps[0] = before
            dve.sem_inc(summed, 1)

            last = stat[:, N_FINAL, :]
            dve.tensor_tensor_reduce(result[:, 1, :], h[:, 1, :], h[:, 1, :], 1.0, 0.0, ALU.mult, ALU.add,
                                     last[:, 1:2]).then_inc(squared, 1)
            dve.wait_ge(squared, 1)
            dve.wait_ge(rs_est, 7)
            final = [0]

            def flink(ins):
                final[0] += 1
                ins.then_inc(final_step, 1)
                dve.wait_ge(final_step, final[0])

            dve.tensor_scalar(last[:, 2:4], last[:, 0:2], 1.0 / D, EPS, ALU.mult, ALU.add)
            flink(dve.reciprocal(last[:, 4:6], last[:, 4:6]))
            flink(dve.tensor_tensor(newton[:, :], last[:, 4:6], last[:, 4:6], ALU.mult))
            flink(dve.tensor_tensor(newton[:, :], newton[:, :], last[:, 2:4], ALU.mult))
            flink(dve.tensor_scalar(newton[:, :], newton[:, :], -0.5, 1.5, ALU.mult, ALU.add))
            flink(dve.tensor_tensor(last[:, 6:8], last[:, 4:6], newton[:, :], ALU.mult))
            for n in range(2 * TT):
                tt, part = n // 2, slice(n % 2 * COLS, (n % 2 + 1) * COLS)
                dve.scalar_tensor_tensor(out=result[:, tt, part], in0=h[:, tt, part], scalar=root(N_FINAL, tt),
                                         in1=fin_g[:, part], op0=ALU.mult, op1=ALU.mult).then_inc(result_ready, 1)

        @block.tensor
        def _(pe):
            def mm3(o, xh, xl, wh, wl, first, last, **kw):
                pe.matmul(o, xh, wh, start=first, stop=False, **kw)
                pe.matmul(o, xh, wl, start=False, stop=False, **kw)
                return pe.matmul(o, xl, wh, start=False, stop=last, **kw)

            def turn(tn, groups=range(4)):
                l, which = tn // 6, tn % 6
                src = (h, hn, mixed, h, mixed, h)[which]
                if which in (1, 2):
                    pe.wait_ge(source_ready, 3 * l + which)
                elif tn == 0:
                    pe.wait_ge(x_landed, 16)
                for g in groups:
                    if tn == 6 and g % 2 == 0:
                        pe.wait_ge(ffn_added, g // 2 + 1)
                    if which in (3, 5) and g % 2 == 0:
                        pe.wait_ge(acc_free, 16 * l + (11 if which == 3 else 15) + g // 2)
                    if which == 2 and g >= 2:
                        pe.wait_ge(pv_taken, ITEMS * l + N_DIFF + 4 * (g - 1))
                    if which == 4 and g < 3:
                        pe.wait_ge(mpv_taken, (MEM_HEADS - 1) * l + g + 1)
                    if which == 4 and g == 3:
                        pe.wait_ge(source_ready, 3 * l + 3)
                    if g >= 2 and (which in (3, 5) or tn == 0):
                        pe.wait_ge(lo_turned, KT * tn + 2 * (g - 2) + 2)
                    if g == 2 and which == 1:
                        pe.wait_ge(acc_free, 16 * l + 6)
                    for k in (2 * g, 2 * g + 1):
                        for tt in range(TT):
                            c = (k % 2) * SEQ + tt * P
                            ins = pe.transpose(ps[:, turn_bank(tn, g), c:c + P], src[:, tt, k * P:(k + 1) * P], ident[:, :])
                    ins.then_inc(turned, 1)

            def unit(n, half, pair, tn=None, more=0):
                pe.wait_ge(lo_split, more + (n + 1))
                wh, wl = slot4(w_hi, n, SPLIT), slot4(w_lo, n, SPLIT)
                for k in range(4):
                    kt = 4 * half + k
                    if tn is not None:
                        pe.wait_ge(lo_turned, KT * tn + kt + 1)
                    for tt in range(TT):
                        ins = mm3(acc(pair)[:, tt, :], x_hi[:, kt, tt * P:(tt + 1) * P], x_lo[:, kt, tt * P:(tt + 1) * P],
                                  wh[:, k, :], wl[:, k, :], kt == 0, kt == KT - 1)
                ins.then_inc(unit_used, 1)

            def narrow(which, bank):
                wh = s_hi[:, which, :].rearrange("p (k n) -> p k n", n=8)
                wl = s_lo[:, which, :].rearrange("p (k n) -> p k n", n=8)
                for kt in range(KT):
                    ins = mm3(ps[0:8, bank, 0:SEQ], wh[:, kt, :], wl[:, kt, :], x_hi[:, kt, :], x_lo[:, kt, :],
                              kt == 0, kt == KT - 1)
                ins.then_inc(rows_done, 1)
                pe.wait_ge(rows_kept, which + 1)
                for tt in range(TT):
                    ins = pe.transpose(ps[:, bank, tt * 8:(tt + 1) * 8], rows[which][:, tt * P:(tt + 1) * P], ident[0:8, 0:8])
                return ins

            def sums(bank, x):
                pe.matmul(ps[:, bank, 0:8], tri[:, 0:P], x[:, 0], start=True, stop=True)
                pe.matmul(ps[:, bank, 8:16], tri[:, P:SEQ], x[:, 0], start=True, stop=False)
                return pe.matmul(ps[:, bank, 8:16], tri[:, 0:P], x[:, 1], start=False, stop=True)

            pe.wait_ge(ident_made, 1)
            pe.wait_ge(gains_landed, 16 * 4)
            pe.transpose(ps[:, 0, 0:64], gain_rows, ident[0:64, 0:64]).then_inc(gains_turned, 1)

            for l in range(LAYERS):
                n0 = l * L_UNITS
                a0 = 16 * l
                turn(6 * l)
                if l == 0:
                    pe.wait_ge(gains_kept, 1)
                with pe.Fori(0, 2) as i:
                    for c in range(3):
                        for u in range(2):
                            unit(n0 + 2 * c + u, u, c, tn=6 * l if c == 0 else None, more=6 * i)
                if l == 0:
                    pe.wait_ge(small_split, 1)
                narrow(l, 7).then_inc(fl_done, 1)
                turn(6 * l + 1, (0,))
                pe.wait_ge(fl_neg, l + 1)
                turn(6 * l + 1, (1, 2, 3))
                pe.wait_ge(acc_free, a0 + 4)
                unit(n0 + 12, 0, 0, tn=6 * l + 1)
                unit(n0 + 13, 1, 0, tn=6 * l + 1)

                def turn_qk(g):
                    if g >= 2:
                        pe.wait_ge(qk_kept, 8 * l + g - 1)
                    for b in range(2):
                        blk = 2 * g + b if g < 4 else C_QF // P + 2 * (g - 4) + b
                        for tt in range(TT):
                            ins = pe.transpose(ps[:, 6 + g % 2, b * SEQ + tt * P:b * SEQ + (tt + 1) * P],
                                               proj[:, tt, blk * P:(blk + 1) * P], ident[:, :])
                    ins.then_inc(qk_turned, 1)

                pe.wait_ge(roped, l + 1)
                for g in range(4):
                    turn_qk(g)
                pe.wait_ge(acc_free, a0 + 7)
                unit(n0 + 14, 0, 0)
                for g in range(4, 8):
                    turn_qk(g)
                pe.wait_ge(logf_ready, l + 1)
                pe.wait_ge(pool_made, 5)
                pe.wait_ge(acc_free, a0 + 6)
                sums(4, fl[:, 1]).then_inc(cq_done, 1)
                for f in range(N_FOX):
                    if f >= 2:
                        pe.wait_ge(ck_used, N_FOX * l + f - 1)
                    o = ps[:, 2 + f % 2, 0:SEQ]
                    f0, f1 = (fl[:, 1, tt, f:f + 1].to_broadcast([P, P]) for tt in range(TT))
                    pe.matmul(o, f0, tri[:, :], start=True, stop=False)
                    pe.matmul(o[:, P:SEQ], f1, tri[:, 0:P], start=False, stop=True).then_inc(ck_done, 1)

                def scores(i):
                    for m in item_maps(i):
                        if m >= 2:
                            pe.wait_ge(masked, MAPS * l + m - 1)
                        elif m == 0:
                            pe.wait_ge(ck_used, N_FOX * l + 1)
                        bq, bk, p0 = map_blocks(m)
                        q, k = qkt[p0:p0 + HD, bq, :], qkt[p0:p0 + HD, bk, :]
                        pe.matmul(ps[:, 4 + m % 2, 0:P], q[:, 0:P], k[:, 0:P], start=True, stop=True)
                        pe.matmul(ps[:, 4 + m % 2, P:SPAN], q[:, P:SEQ], k, start=True, stop=True).then_inc(scored, 1)

                def turn_p(i):
                    if i < N_DIFF:
                        pe.wait_ge(weighed, N_DIFF * l + i + 1)
                    else:
                        pe.wait_ge(expd, MAPS * l + item_maps(i)[0] + 1)
                    if i >= 2:
                        pe.wait_ge(p_kept, ITEMS * l + i - 1)
                    for b in range(3):
                        ins = pe.transpose(ps[:, 6 + i % 2, b * P:(b + 1) * P],
                                           probs(item_maps(i)[0])[:, b * P:(b + 1) * P], ident[:, :])
                    ins.then_inc(p_turned, 1)

                def pv(i):
                    pe.wait_ge(p_kept, ITEMS * l + i + 1)
                    if i >= 2:
                        pe.wait_ge(pv_taken, ITEMS * l + i - 1)
                    wide = P if i < N_DIFF else HD
                    c = C_VD + i * P if i < N_DIFF else C_VF + (i - N_DIFF) * HD
                    o, p = ps[:, 2 + i % 2, :], probs_t(i)
                    pe.matmul(o[:, 0:wide], p[:, 0:P], proj[:, 0, c:c + wide], start=True, stop=True)
                    pe.matmul(o[:, wide:2 * wide], p[:, P:2 * P], proj[:, 0, c:c + wide], start=True, stop=False)
                    pe.matmul(o[:, wide:2 * wide], p[:, 2 * P:SPAN], proj[:, 1, c:c + wide], start=False,
                              stop=True).then_inc(pv_done, 1)

                pe.wait_ge(qk_kept, 8 * (l + 1))
                for s in range(ITEMS + 2):
                    if s < ITEMS:
                        scores(s)
                    if s in KV_STEPS:
                        u = 15 + KV_STEPS.index(s)
                        if u % 2 == 0:
                            pe.wait_ge(acc_free, a0 + u // 2)
                        unit(n0 + u, u % 2, 0)
                    if 1 <= s <= ITEMS:
                        turn_p(s - 1)
                    if s >= 2:
                        pv(s - 2)

                def half_turns(tn, b, after=True):
                    unit(b, 0, 0, tn=tn - 1)
                    unit(b + 1, 1, 0, tn=tn - 1)
                    unit(b + 2, 0, 1)
                    turn(tn, (0, 1))
                    unit(b + 3, 1, 1)
                    if after:
                        unit(b + 4, 0, 0, tn=tn)
                    turn(tn, (2, 3))
                    if after:
                        unit(b + 5, 0, 1)
                        unit(b + 6, 1, 0, tn=tn)
                        unit(b + 7, 1, 1)

                turn(6 * l + 2)
                pe.wait_ge(acc_free, a0 + 10)
                half_turns(6 * l + 3, n0 + U_OUT)

                for g in range(8):
                    if g >= 2:
                        pe.wait_ge(mqk_kept, 8 * l + g - 1)
                    if g == 4:
                        pe.wait_ge(acc_free, a0 + 14)
                    src = kv if g < 4 else mem_q
                    for b in range(2):
                        blk = 2 * (g % 4) + b
                        for tt in range(TT):
                            ins = pe.transpose(ps[:, 6 + g % 2, b * SEQ + tt * P:b * SEQ + (tt + 1) * P],
                                               src[:, tt, blk * P:(blk + 1) * P], ident[:, :])
                    ins.then_inc(mqk_turned, 1)
                pe.wait_ge(mqk_kept, 8 * (l + 1))
                for s in range(MEM_HEADS + 2):
                    if s < MEM_HEADS:
                        if s >= 2:
                            pe.wait_ge(mexpd, MEM_HEADS * l + s - 1)
                        for tt in range(TT):
                            for b in range(2):
                                ins = pe.matmul(ps[:, 4 + s % 2, tt * SEQ:(tt + 1) * SEQ],
                                                qkt[:, 8 + 2 * s + b, tt * P:(tt + 1) * P], qkt[:, 2 * s + b, :],
                                                start=b == 0, stop=b == 1)
                        ins.then_inc(mscored, 1)
                    if 1 <= s <= MEM_HEADS:
                        i = s - 1
                        pe.wait_ge(mexpd, MEM_HEADS * l + i + 1)
                        if i >= 2:
                            pe.wait_ge(mp_kept, MEM_HEADS * l + i - 1)
                        for tt in range(TT):
                            for b in range(2):
                                c = (2 * tt + b) * P
                                ins = pe.transpose(ps[:, 6 + i % 2, c:c + P], mem_p(i)[:, tt, b * P:(b + 1) * P], ident[:, :])
                        ins.then_inc(mp_turned, 1)
                    if s >= 2:
                        i = s - 2
                        pe.wait_ge(mp_kept, MEM_HEADS * l + i + 1)
                        if i >= 2:
                            pe.wait_ge(mpv_taken, (MEM_HEADS - 1) * l + i - 1)
                        for tt in range(TT):
                            for b in range(2):
                                c = (2 * tt + b) * P
                                ins = pe.matmul(ps[:, 2 + i % 2, tt * SEQ:(tt + 1) * SEQ], mem_pt(i)[:, c:c + P],
                                                kv[:, b, D + i * MEM_HD:D + (i + 1) * MEM_HD], start=b == 0, stop=b == 1)
                        ins.then_inc(mpv_done, 1)
                turn(6 * l + 4)
                half_turns(6 * l + 5, n0 + U_MO, after=l == 0)
                if l == 0:
                    f0 = n0 + U_FFN

                    def turn_g(pair, want, blocks=4):
                        pe.wait_ge(gated, want)
                        for b in range(blocks):
                            for tt in range(TT):
                                o = acc(pair)[:, b // 2, (b % 2) * SEQ + tt * P:(b % 2) * SEQ + (tt + 1) * P]
                                ins = pe.transpose(o, gate[:, tt, b * P:(b + 1) * P], ident[:, :])
                        ins.then_inc(g_turned, 1)

                    def down(n, half, buf, more=0):
                        pe.wait_ge(lo_split, more + (n + 1))
                        wh, wl = slot2(w_hi, n, SPLIT), slot2(w_lo, n, SPLIT)
                        for k in range(2):
                            for tt in range(TT):
                                for c in range(2):
                                    b = 2 * half + k
                                    ins = mm3(ps[:, 4 + 2 * tt + c, :], g_hi[:, buf, b, tt * P:(tt + 1) * P],
                                              g_lo[:, buf, b, tt * P:(tt + 1) * P], wh[:, k, c * COLS:(c + 1) * COLS],
                                              wl[:, k, c * COLS:(c + 1) * COLS], False, False, skip_group_check=True)
                        ins.then_inc(unit_used, 1)

                    turn_g(0, 1)
                    pe.wait_ge(out_zeroed, 1)
                    with pe.Fori(0, (FF_FULL - 1) // 2) as i:
                        for r in range(2):
                            b = f0 + 4 + 6 * r
                            for k in range(2):
                                unit(b + k, k % 2, (r + 1) % 2, more=12 * i)
                            pe.wait_ge(glo_kept, 2 * i + (r + 1))
                            for k in range(2, 4):
                                unit(b + k, k % 2, r % 2, more=12 * i)
                            for k in range(2):
                                down(b + 4 + k, k, r % 2, more=12 * i)
                            turn_g((r + 1) % 2, 2 * i + (r + 2))
                    f1 = f0 + 4 + 6 * (FF_FULL - 1)
                    for k in range(2):
                        if k == 1:
                            pe.wait_ge(glo_kept, FF_FULL)
                        pe.wait_ge(lo_split, f1 + k + 1)
                        wh, wl = slot8(w_hi, f1 + k, SPLIT), slot8(w_lo, f1 + k, SPLIT)
                        for kt in range(KT):
                            for tt in range(TT):
                                ins = mm3(acc(1 - k)[:, tt, 0:SEQ], x_hi[:, kt, tt * P:(tt + 1) * P],
                                          x_lo[:, kt, tt * P:(tt + 1) * P], wh[:, kt, :], wl[:, kt, :], kt == 0, kt == KT - 1)
                        ins.then_inc(unit_used, 1)
                    down(f1 + 2, 0, 0)
                    down(f1 + 3, 1, 0)
                    turn_g(1, FF_FULL + 1, 2)
                    pe.wait_ge(glo_kept, FF_FULL + 1)
                    pe.wait_ge(lo_split, L_UNITS)
                    wh, wl = slot2(w_hi, f1 + 4, SPLIT), slot2(w_lo, f1 + 4, SPLIT)
                    for c in range(2):
                        for k in range(2):
                            for tt in range(TT):
                                ins = mm3(ps[:, 4 + 2 * tt + c, :], g_hi[:, 1, k, tt * P:(tt + 1) * P],
                                          g_lo[:, 1, k, tt * P:(tt + 1) * P], wh[:, k, c * COLS:(c + 1) * COLS],
                                          wl[:, k, c * COLS:(c + 1) * COLS], False, False, skip_group_check=True)
                        ins.then_inc((ffn_summed, unit_used)[c], 1)

            pe.wait_ge(lo_turned, KT * 12)
            pe.wait_ge(acc_free, 32)
            narrow(2, 4).then_inc(logits_done, 1)
            pe.wait_ge(picked_sum, 1)
            sums(4, route[:, :, 9, 0:8])
            for tt in range(TT):
                ins = pe.matmul(ps[:, 4, 16:24], tri[:, P:SEQ], route[:, tt, 9, 0:8], start=tt == 0, stop=tt == 1)
            ins.then_inc(counted, 1)

            def gather(q):
                pe.wait_ge(pick_made, q + 1)
                for g in range(2):
                    for k in range(4):
                        for tt in range(TT):
                            c = (4 * g + k) * P
                            ins = pe.matmul(ps[:, 5 + g, k * P:(k + 1) * P], hn[:, tt, c:c + P], pick[:, tt, :],
                                            start=tt == 0, stop=tt == 1)
                    ins.then_inc(gathered, 1)

            def scatter(q):
                for n, bank in enumerate((5, 6, 7, 2)):
                    c, tt = n // 2, n % 2
                    pe.wait_ge(ye_kept, 2 * q + (c + 1))
                    pe.matmul(ps[:, bank, :], pick_t[:, tt, :], ye[:, c * COLS:(c + 1) * COLS], start=True,
                              stop=True).then_inc(scattered, 1)

            def up(n, half, bank, more):
                pe.wait_ge(lo_split, more + (n + 1))
                wh, wl = slot4(w_hi, n, SPLIT), slot4(w_lo, n, SPLIT)
                for k in range(4):
                    kt = 4 * half + k
                    ins = mm3(ps[:, bank, :], xe_hi[:, kt, :], xe_lo[:, kt, :], wh[:, k, :], wl[:, k, :], kt == 0, kt == KT - 1)
                ins.then_inc(unit_used, 1)

            def down1(n, half, more):
                pe.wait_ge(lo_split, more + (n + 1))
                wh, wl = slot2(w_hi, n, SPLIT), slot2(w_lo, n, SPLIT)
                for k in range(2):
                    for c in range(2):
                        b = 2 * half + k
                        ins = mm3(ps[:, 2 + c, :], g_hi[:, 0, b, 0:P], g_lo[:, 0, b, 0:P], wh[:, k, c * COLS:(c + 1) * COLS],
                                  wl[:, k, c * COLS:(c + 1) * COLS], False, False, skip_group_check=True)
                ins.then_inc(unit_used, 1)

            def turn_e(want):
                pe.wait_ge(e_gated, want)
                for b in range(4):
                    ins = pe.transpose(ps[:, 4, b * P:(b + 1) * P], gate[:, 0, b * P:(b + 1) * P], ident[:, :])
                ins.then_inc(e_turned, 1)

            def expert(q, b0, last=False):
                more = E_UNITS * q
                pe.wait_ge(xe_lo_kept, 2 * q + 2)
                for k in range(4):
                    up(M0 + k, k % 2, k // 2, more)
                scatter(q + b0)
                for tt in range(TT):
                    ins = pe.transpose(ps[:, 3, tt * P:(tt + 1) * P], pick[:, tt, :], ident[:, :])
                ins.then_inc(pick_turned, 1)
                turn_e(EXP_CH * q + 1)
                with pe.Fori(0, EXP_CH - 1) as j:
                    for k in range(4):
                        up(M0 + 4 + k, k % 2, k // 2, more + 6 * j)
                    pe.wait_ge(e_lo, EXP_CH * q + j + 1)
                    pe.wait_ge(e_zeroed, q + 1)
                    for k in range(2):
                        down1(M0 + 8 + k, k, more + 6 * j)
                    turn_e(EXP_CH * q + j + 2)
                if not last:
                    gather(q + 1)
                pe.wait_ge(e_lo, EXP_CH * q + EXP_CH)
                down1(M0 + 6 * EXP_CH - 2, 0, more)
                n = M0 + 6 * EXP_CH - 1
                pe.wait_ge(lo_split, more + (n + 1))
                wh, wl = slot2(w_hi, n, SPLIT), slot2(w_lo, n, SPLIT)
                for c in range(2):
                    for k in range(2):
                        ins = mm3(ps[:, 2 + c, :], g_hi[:, 0, 2 + k, 0:P], g_lo[:, 0, 2 + k, 0:P],
                                  wh[:, k, c * COLS:(c + 1) * COLS], wl[:, k, c * COLS:(c + 1) * COLS],
                                  False, False, skip_group_check=True)
                    ins.then_inc((ye_done, unit_used)[c], 1)

            def experts(q0):
                b0 = q0 // N_EXP
                pe.wait_ge(comb_ready, 2 + 2 * b0)
                pe.wait_ge(hn_ready, 1)
                gather(q0)
                pe.transpose(ps[:, 7, 0:P], ident[:, :], ident[:, :]).then_inc(ye_done, 1)
                with pe.Fori(0, N_EXP - 1) as e:
                    expert(e + q0, b0)
                expert(q0 + N_EXP - 1, b0, last=True)
                scatter(q0 + N_EXP + b0)

            experts(0)
            pe.wait_ge(over_ready, 1)
            over = pe.value_load(n_over[0:1, 0:1], min_val=0, max_val=SEQ)
            with pe.If(over > 0):
                experts(N_EXP)


def lam_init(l):
    return 0.8 - 0.6 * math.exp(-0.3 * l)


NAMES = ["x", "mem", "positions", "norm_mix_g", "w_in", "lam_q1", "lam_k1", "lam_q2", "lam_k2", "diff_subln_g",
         "fox_bias", "w_out", "norm_mem_g", "mem_norm_g", "w_mq", "w_mkv", "w_mo", "norm_ffn_g", "w_ff1", "w_ff3",
         "w_ff2", "w_router", "w_e1", "w_e3", "w_e2", "final_norm_g"]


def kernel(**inputs):
    import concourse.bacc as bacc
    from concourse.bass_utils import run_bass_kernel_spmd

    nc = bacc.Bacc("TRN2", target_bir_lowering=False, num_devices=1)
    arrays, aps = {}, {}
    for name in NAMES:
        a = np.ascontiguousarray(inputs[name])
        arrays[name] = a
        aps[name] = nc.dram_tensor(name, a.shape, mybir.dt.from_np(a.dtype), kind="ExternalInput").ap()
    out = nc.dram_tensor("out", (1, SEQ, D), F32, kind="ExternalOutput").ap()
    trunk(nc, aps, out)
    r = run_bass_kernel_spmd(nc, [arrays], core_ids=[0])
    return r.results[0]["out"]
```
